# Optimizing a Trainium2 kernel written in Bass

```python
import math
import jax, jax.numpy as jnp
from jax import lax
import numpy as np

D_MODEL = 1024
BATCH = 1
SEQ = 1024
DEPTH = 1
DEC_BATCH = 8
DEC_SEQ = 4
PAST_LEN = 256
PAGE_SIZE = 128

H_M = 4
DH_M = 128
W_M = H_M * DH_M
CHUNK = 64
F_BIAS_LO = 3.0
F_BIAS_HI = 6.0
H_D = 4
DQK_D = 64
DV_D = 2 * DQK_D
W_D = H_D * DV_D
Q_BLOCK = 128
D_FF = 2816
CONV_W = 3
EPS = 1e-6
IN_SIZES = (W_M, W_M, W_M, W_M, 2 * H_M, H_D * 2 * DQK_D, H_D * 2 * DQK_D, W_D, D_MODEL, D_MODEL)
D_IN = 4 * W_M + 2 * H_M + 2 * H_D * 2 * DQK_D + W_D + 2 * D_MODEL

kernel_name = 'hybrid_mlstm_diffattn_convffn_step'

def rms_norm(x, g):
    xf = x.astype(jnp.float32)
    y = xf * lax.rsqrt(jnp.mean(xf * xf, axis=-1, keepdims=True) + EPS)
    return (y * g.astype(jnp.float32)).astype(x.dtype)

def adaln_terms(c, w_ada, b_ada):
    ada = jnp.einsum('bd,de->be', c, w_ada) + b_ada
    return jnp.split(ada[:, None, :], 6, axis=-1)

def split_columns(z):
    offsets = np.cumsum(np.array(IN_SIZES))[:-1].tolist()
    return jnp.split(z, offsets, axis=-1)

def chunk_len(t):
    return CHUNK if t % CHUNK == 0 else t

def mlstm_scan(q, k, v, i_raw, logf, C0, n0, m0):
    B, T, H, Dh = q.shape
    L = chunk_len(T)
    nc = T // L

    def to_chunks(a):
        return jnp.moveaxis(a.reshape((B, nc, L) + a.shape[2:]), 1, 0)

    causal = jnp.tril(jnp.ones((L, L), dtype=bool))[None, :, :, None]

    def step(carry, blk):
        C, n, m = carry
        qb, kb, vb, ib, fb = blk
        F = jnp.cumsum(fb, axis=1)
        a = ib - F
        m_t = F + jnp.maximum(m[:, None, :], lax.cummax(a, axis=1))
        logD = jnp.where(causal, F[:, :, None, :] + a[:, None, :, :] - m_t[:, :, None, :], -jnp.inf)
        s = jnp.einsum('bthd,bshd->btsh', qb, kb) * jnp.exp(logD)
        inter = jnp.exp(F + m[:, None, :] - m_t)
        num = jnp.einsum('btsh,bshv->bthv', s, vb) + inter[..., None] * jnp.einsum('bhvd,bthd->bthv', C, qb)
        den = jnp.sum(s, axis=2) + inter * jnp.einsum('bhd,bthd->bth', n, qb)
        h = num / jnp.maximum(jnp.abs(den), jnp.exp(-m_t))[..., None]
        m_end = m_t[:, -1]
        F_end = F[:, -1]
        w_end = jnp.exp(F_end[:, None, :] + a - m_end[:, None, :])
        decay = jnp.exp(F_end + m - m_end)
        C_new = decay[..., None, None] * C + jnp.einsum('bsh,bshv,bshd->bhvd', w_end, vb, kb)
        n_new = decay[..., None] * n + jnp.einsum('bsh,bshd->bhd', w_end, kb)
        return (C_new, n_new, m_end), h

    blocks = (to_chunks(q), to_chunks(k), to_chunks(v), to_chunks(i_raw), to_chunks(logf))
    (C, n, m), hs = lax.scan(step, (C0, n0, m0), blocks)
    return jnp.moveaxis(hs, 0, 1).reshape(B, T, H, Dh), C, n, m

def mlstm_branch(mq, mk, mv, mo, mif, b_if, g_norm, C0, n0, m0):
    B, T, _ = mq.shape
    f32 = jnp.float32
    q = mq.astype(f32).reshape(B, T, H_M, DH_M)
    k = mk.astype(f32).reshape(B, T, H_M, DH_M) * (DH_M ** -0.5)
    v = mv.astype(f32).reshape(B, T, H_M, DH_M)
    gates = mif.astype(f32) + b_if.astype(f32)
    i_raw = gates[..., :H_M]
    logf = jax.nn.log_sigmoid(gates[..., H_M:])
    h, C, n, m = mlstm_scan(q, k, v, i_raw, logf, C0.astype(f32), n0.astype(f32), m0.astype(f32))
    h = rms_norm(h, g_norm.reshape(H_M, DH_M)).astype(mq.dtype)
    out = jax.nn.sigmoid(mo) * h.reshape(B, T, W_M)
    return out, C, n, m

def diff_attend(q1, q2, k1, k2, v, mask, lam):
    scale = DQK_D ** -0.5
    s1 = jnp.einsum('bqhd,bkhd->bhqk', q1, k1).astype(jnp.float32) * scale
    s2 = jnp.einsum('bqhd,bkhd->bhqk', q2, k2).astype(jnp.float32) * scale
    s1 = jnp.where(mask, s1, -jnp.inf)
    s2 = jnp.where(mask, s2, -jnp.inf)
    a = jax.nn.softmax(s1, axis=-1) - lam * jax.nn.softmax(s2, axis=-1)
    return jnp.einsum('bhqk,bkhv->bqhv', a.astype(v.dtype), v)

def diff_branch(dq, dk, dv, lq1, lk1, lq2, lk2, g_norm, lam_init, past_k, past_v):
    B, T, _ = dq.shape
    f32 = jnp.float32
    q = dq.reshape(B, T, H_D, 2 * DQK_D)
    k_rows = dk.reshape(B, T, H_D, 2 * DQK_D)
    v_rows = dv.reshape(B, T, H_D, DV_D)
    lam = (jnp.exp(jnp.sum(lq1.astype(f32) * lk1.astype(f32)))
           - jnp.exp(jnp.sum(lq2.astype(f32) * lk2.astype(f32))) + lam_init)
    q1, q2 = q[..., :DQK_D], q[..., DQK_D:]
    if past_k is None:
        k1, k2 = k_rows[..., :DQK_D], k_rows[..., DQK_D:]
        nb = T // Q_BLOCK
        key_pos = jnp.arange(T)

        def block(args):
            bi, qb1, qb2 = args
            q_pos = bi * Q_BLOCK + jnp.arange(Q_BLOCK)
            return diff_attend(qb1, qb2, k1, k2, v_rows, key_pos[None, :] <= q_pos[:, None], lam)

        def to_blocks(a):
            return jnp.moveaxis(a.reshape(B, nb, Q_BLOCK, H_D, DQK_D), 1, 0)

        o = lax.map(block, (jnp.arange(nb), to_blocks(q1), to_blocks(q2)))
        o = jnp.moveaxis(o, 0, 1).reshape(B, T, H_D, DV_D)
    else:
        past_len = past_k.shape[1]
        k_all = jnp.concatenate([past_k.astype(k_rows.dtype), k_rows], axis=1)
        v_all = jnp.concatenate([past_v.astype(v_rows.dtype), v_rows], axis=1)
        mask = jnp.arange(past_len + T)[None, :] <= past_len + jnp.arange(T)[:, None]
        o = diff_attend(q1, q2, k_all[..., :DQK_D], k_all[..., DQK_D:], v_all, mask, lam)
    o = rms_norm(o, g_norm.reshape(H_D, DV_D)) * (1.0 - lam_init)
    return o.reshape(B, T, W_D), k_rows, v_rows

def conv_ffn(h, w_up, conv_w, conv_b, w_down, conv_state):
    T = h.shape[1]
    u = jnp.einsum('btd,df->btf', h, w_up)
    a, b = u[..., :D_FF], u[..., D_FF:]
    a_ext = jnp.concatenate([conv_state.astype(a.dtype), a], axis=1)
    conv = conv_b
    for j in range(CONV_W):
        conv = conv + conv_w[j] * a_ext[:, j:j + T]
    out = jnp.einsum('btf,fd->btd', jax.nn.gelu(conv, approximate=True) * b, w_down)
    return out, a_ext[:, -(CONV_W - 1):]

def layer_forward(x, c, p, lam_init, past_k, past_v, C0, n0, m0, conv0):
    shift1, scale1, gate1, shift2, scale2, gate2 = adaln_terms(c, p['w_ada'], p['b_ada'])
    h = rms_norm(x, p['g_pre_mix']) * (1.0 + scale1) + shift1
    z = jnp.einsum('btd,de->bte', h, p['w_in'])
    mq, mk, mv, mo, mif, dq, dk, dv, gm, gd = split_columns(z)
    hm, C, n, m = mlstm_branch(mq, mk, mv, mo, mif, p['b_if'], p['g_mlstm'], C0, n0, m0)
    hd, k_rows, v_rows = diff_branch(dq, dk, dv, p['lq1'], p['lk1'], p['lq2'], p['lk2'],
                                     p['g_diff'], lam_init, past_k, past_v)
    merged = (jax.nn.sigmoid(gm) * jnp.einsum('btw,wd->btd', hm, p['w_proj_m'])
              + jax.nn.sigmoid(gd) * jnp.einsum('btw,wd->btd', hd, p['w_proj_d']))
    y = jnp.einsum('btd,de->bte', merged, p['w_out'])
    x = x + gate1 * rms_norm(y, p['g_post_mix'])
    h2 = rms_norm(x, p['g_pre_ffn']) * (1.0 + scale2) + shift2
    f, conv_new = conv_ffn(h2, p['w_up'], p['conv_w'], p['conv_b'], p['w_down'], conv0)
    x = x + gate2 * rms_norm(f, p['g_post_ffn'])
    return x, k_rows, v_rows, C, n, m, conv_new

def setup_inputs(seed: int = 0) -> dict:
    key = jax.random.key(seed)
    ks = jax.random.split(key, 40)
    n_pages = PAST_LEN // PAGE_SIZE
    n_used = DEC_BATCH * n_pages
    n_pool = (n_used * 5) // 4

    def nrm(k, shape, scale=1.0):
        return scale * jax.random.normal(k, shape, jnp.float32)

    def gain(k, shape):
        return 1.0 + 0.05 * jax.random.normal(k, shape, jnp.float32)

    page_table = jax.random.permutation(ks[6], n_pool)[:n_used].reshape(DEC_BATCH, n_pages).astype(jnp.int32)
    f_bias = jnp.broadcast_to(jnp.linspace(F_BIAS_LO, F_BIAS_HI, H_M, dtype=jnp.float32), (DEPTH, H_M))
    b_if = jnp.concatenate([nrm(ks[16], (DEPTH, H_M), 0.1), f_bias + nrm(ks[17], (DEPTH, H_M), 0.1)], axis=-1)
    return {
        'x_prompt': nrm(ks[0], (BATCH, SEQ, D_MODEL)),
        'x_sample': nrm(ks[1], (DEC_BATCH, DEC_SEQ, D_MODEL)),
        'c_prompt': nrm(ks[2], (BATCH, D_MODEL)),
        'c_sample': nrm(ks[3], (DEC_BATCH, D_MODEL)),
        'cache_k': nrm(ks[4], (DEPTH, n_pool, PAGE_SIZE, H_D, 2 * DQK_D)),
        'cache_v': nrm(ks[5], (DEPTH, n_pool, PAGE_SIZE, H_D, DV_D)),
        'page_table': page_table,
        'state_C': nrm(ks[7], (DEPTH, DEC_BATCH, H_M, DH_M, DH_M), 0.1),
        'state_n': nrm(ks[8], (DEPTH, DEC_BATCH, H_M, DH_M), 0.1),
        'state_m': jax.random.uniform(ks[9], (DEPTH, DEC_BATCH, H_M), jnp.float32, 0.0, 4.0),
        'state_conv': nrm(ks[10], (DEPTH, DEC_BATCH, CONV_W - 1, D_FF)),
        'w_ada': nrm(ks[11], (DEPTH, D_MODEL, 6 * D_MODEL), 0.5 * D_MODEL ** -0.5),
        'b_ada': nrm(ks[12], (DEPTH, 6 * D_MODEL), 0.01),
        'g_pre_mix': gain(ks[13], (DEPTH, D_MODEL)),
        'g_post_mix': gain(ks[14], (DEPTH, D_MODEL)),
        'w_in': nrm(ks[15], (DEPTH, D_MODEL, D_IN), D_MODEL ** -0.5),
        'b_if': b_if,
        'g_mlstm': gain(ks[18], (DEPTH, W_M)),
        'lambda_q1': nrm(ks[19], (DEPTH, DQK_D), 0.1),
        'lambda_k1': nrm(ks[20], (DEPTH, DQK_D), 0.1),
        'lambda_q2': nrm(ks[21], (DEPTH, DQK_D), 0.1),
        'lambda_k2': nrm(ks[22], (DEPTH, DQK_D), 0.1),
        'g_diff': gain(ks[23], (DEPTH, W_D)),
        'w_proj_m': nrm(ks[24], (DEPTH, W_M, D_MODEL), W_M ** -0.5),
        'w_proj_d': nrm(ks[25], (DEPTH, W_D, D_MODEL), W_D ** -0.5),
        'w_out': nrm(ks[26], (DEPTH, D_MODEL, D_MODEL), D_MODEL ** -0.5),
        'g_pre_ffn': gain(ks[27], (DEPTH, D_MODEL)),
        'g_post_ffn': gain(ks[28], (DEPTH, D_MODEL)),
        'w_up': nrm(ks[29], (DEPTH, D_MODEL, 2 * D_FF), D_MODEL ** -0.5),
        'conv_w': nrm(ks[30], (DEPTH, CONV_W, D_FF), CONV_W ** -0.5),
        'conv_b': nrm(ks[31], (DEPTH, D_FF), 0.01),
        'w_down': nrm(ks[32], (DEPTH, D_FF, D_MODEL), D_FF ** -0.5),
    }

def reference(x_prompt, x_sample, c_prompt, c_sample, cache_k, cache_v, page_table,
              state_C, state_n, state_m, state_conv, w_ada, b_ada, g_pre_mix, g_post_mix,
              w_in, b_if, g_mlstm, lambda_q1, lambda_k1, lambda_q2, lambda_k2, g_diff,
              w_proj_m, w_proj_d, w_out, g_pre_ffn, g_post_ffn, w_up, conv_w, conv_b, w_down):
    f32 = jnp.float32
    B = x_prompt.shape[0]
    n_seq, n_pages = page_table.shape
    page = cache_k.shape[2]
    xp, xs = x_prompt, x_sample
    kp_l, vp_l, Cp_l, np_l, mp_l, cvp_l = [], [], [], [], [], []
    ks_l, vs_l, Cs_l, ns_l, ms_l, cvs_l = [], [], [], [], [], []
    for l in range(DEPTH):
        p = {'w_ada': w_ada[l], 'b_ada': b_ada[l], 'g_pre_mix': g_pre_mix[l], 'g_post_mix': g_post_mix[l],
             'w_in': w_in[l], 'b_if': b_if[l], 'g_mlstm': g_mlstm[l],
             'lq1': lambda_q1[l], 'lk1': lambda_k1[l], 'lq2': lambda_q2[l], 'lk2': lambda_k2[l],
             'g_diff': g_diff[l], 'w_proj_m': w_proj_m[l], 'w_proj_d': w_proj_d[l], 'w_out': w_out[l],
             'g_pre_ffn': g_pre_ffn[l], 'g_post_ffn': g_post_ffn[l], 'w_up': w_up[l],
             'conv_w': conv_w[l], 'conv_b': conv_b[l], 'w_down': w_down[l]}
        lam_init = 0.8 - 0.6 * math.exp(-0.3 * l)
        xp, kp, vp, Cp, n_p, mp, cvp = layer_forward(
            xp, c_prompt, p, lam_init, None, None,
            jnp.zeros((B, H_M, DH_M, DH_M), f32), jnp.zeros((B, H_M, DH_M), f32),
            jnp.zeros((B, H_M), f32), jnp.zeros((B, CONV_W - 1, D_FF), xp.dtype))
        past_k = cache_k[l][page_table].reshape(n_seq, n_pages * page, H_D, 2 * DQK_D)
        past_v = cache_v[l][page_table].reshape(n_seq, n_pages * page, H_D, DV_D)
        xs, ksm, vsm, Cs, n_s, ms, cvs = layer_forward(
            xs, c_sample, p, lam_init, past_k, past_v,
            state_C[l], state_n[l], state_m[l], state_conv[l])
        kp_l.append(kp); vp_l.append(vp)
        Cp_l.append(Cp.astype(state_C.dtype)); np_l.append(n_p.astype(state_n.dtype))
        mp_l.append(mp.astype(state_m.dtype)); cvp_l.append(cvp.astype(state_conv.dtype))
        ks_l.append(ksm); vs_l.append(vsm)
        Cs_l.append(Cs.astype(state_C.dtype)); ns_l.append(n_s.astype(state_n.dtype))
        ms_l.append(ms.astype(state_m.dtype)); cvs_l.append(cvs.astype(state_conv.dtype))
    return (xp, xs,
            jnp.stack(kp_l), jnp.stack(vp_l), jnp.stack(Cp_l), jnp.stack(np_l), jnp.stack(mp_l), jnp.stack(cvp_l),
            jnp.stack(ks_l), jnp.stack(vs_l), jnp.stack(Cs_l), jnp.stack(ns_l), jnp.stack(ms_l), jnp.stack(cvs_l))


_drawn_inputs = setup_inputs


def setup_inputs(seed=0):
    import zlib

    import numpy as np

    out = dict(_drawn_inputs(seed))
    spreads = {}
    factors = {'g_mlstm': 4.524,
     'lambda_q1': 5.559,
     'lambda_k1': 8.0,
     'lambda_q2': 4.509,
     'lambda_k2': 7.562,
     'g_diff': 3.076,
     'conv_b': 8.0}
    for name, (base, spread) in spreads.items():
        noise = np.random.default_rng([zlib.crc32(name.encode()), seed]).standard_normal(out[name].shape)
        drawn = base * np.exp(spread * noise) if base else spread * noise
        out[name] = __import__('jax').numpy.asarray(drawn.astype(out[name].dtype))
    for name, factor in factors.items():
        out[name] = (out[name] * factor).astype(out[name].dtype)
    return out
```

```python
import math
from contextlib import ExitStack

import concourse.bass as bass
from concourse import mybir
from concourse.alu_op_type import AluOpType as ALU

ACT = mybir.ActivationFunctionType
F32 = mybir.dt.float32
F32R = mybir.dt.float32r
I32 = mybir.dt.int32
AX_X = mybir.AxisListType.X

P = 128
D_MODEL, SEQ, DEC_B, DEC_T, PAST, PAGE = 1024, 1024, 8, 4, 256, 128
H, DH, DQK, D_FF, CONV_W = 4, 128, 64, 2816, 3
W_MIX = H * DH
D_IN = 4 * W_MIX + 2 * H + 3 * W_MIX + 2 * D_MODEL
EPS = 1e-6
LAM_INIT = 0.8 - 0.6 * math.exp(0.0)
NEG = -1e30
TS = DEC_B * DEC_T
T = SEQ + TS
NTB, TB = 3, T // 3
KT = D_MODEL // P
NCH = SEQ // P
NTT = NCH + 1
FT = D_FF // P
NPG = PAST // PAGE
CW = 2048
NC_ = 256
ADA_CHUNKS = 6 * D_MODEL // NC_
TOK_C = TS + 1
Z_MQ, Z_MK, Z_MV, Z_DQ, Z_DK, Z_DV, Z_MO, Z_GM, Z_GD = 0, 4, 8, 12, 16, 20, 24, 28, 36
Z_TILES = 44
IN_SEGMENTS = [(6, 0, Z_MQ, False), (6, 4 * W_MIX + 2 * H, Z_DQ, False),
               (2, 3 * W_MIX, Z_MO, True)]
GATE_CHUNKS, GATE_COL = 8, 7 * W_MIX + 2 * H
IF_COL = 4 * W_MIX
Q_A, Q_G, Q_INTER, Q_EMT, Q_WEND = range(5)


def build(nc, ins, outs):
    I, O = ins, outs
    base = ExitStack()
    cur = [base]
    base.enter_context(nc.allow_non_contiguous_dma(reason="a few columns of 32 to 1024 elements"))

    def sb(name, shape, dt=F32):
        return cur[0].enter_context(nc.sbuf_tensor(name, shape, dt))

    def sem(name):
        return base.enter_context(nc.semaphore(name))

    def scratch(name, shape):
        return nc.dram_tensor(name, shape, F32).ap()

    ZT = scratch("z_scratch", (Z_TILES, P, T))
    GATES = scratch("gate_scratch", (2, TOK_C, D_MODEL))
    GIFP = scratch("if_scratch", (2, H, SEQ))
    GIFD = scratch("ifd_scratch", (2, H, TS))
    ROWS = scratch("rows_scratch", (5, H, SEQ))
    ROWD = scratch("rowd_scratch", (5, H, TS))
    ENDS = scratch("ends_scratch", (4, H * NCH))
    DECD = scratch("decd_scratch", (1, H * DEC_B))
    X1 = scratch("x1_scratch", (T, D_MODEL))

    ps = base.enter_context(nc.psum_tensor("ps", [P, 8, 512], F32))
    w_raw = sb("w_raw", [P, 2, CW])
    w_hi = sb("w_hi", [P, 2, CW], F32R)
    w_lo = sb("w_lo", [P, 2, CW], F32R)
    ident = sb("ident", [P, P])
    mask_q = sb("mask_q", [P, P])
    mask_s = sb("mask_s", [P, P])
    mask_n = sb("mask_n", [TS, TS])
    ones = sb("ones", [P, P])
    ada_t = sb("ada_t", [P, 4, KT, TOK_C])
    vec_t = sb("vec_t", [P, KT, 3])
    ff_t = sb("ff_t", [P, FT, 20])
    neg_lam = sb("neg_lam", [P, 1])
    minus_half = sb("minus_half", [P, NTT])
    same_seq = sb("same_seq", [TS, DEC_B])
    rows_t = sb("rows_t", [P, 5, H * NCH])
    decay_p = sb("decay_p", [P, H * NCH])
    branch_s = sb("branch_s", [P, KT, TS])
    acts_hi = sb("acts_hi", [P, KT, T], F32R)
    acts_lo_at = nc.sbuf_base
    acts_lo = sb("acts_lo", [P, KT, T], F32R)

    w_loaded = [sem("w_loaded0"), sem("w_loaded1")]
    w_hi_ready = sem("w_hi_ready")
    w_lo_ready = sem("w_lo_ready")
    tile_done = sem("tile_done")

    def load_chunk(sp, slot, src, kt, split_before=None):
        if split_before is not None:
            sp.wait_ge(w_lo_ready, split_before)
        sp.dma_start(w_raw[:, slot, :].rearrange("p (k n) -> p k n", k=kt), src).then_inc(w_loaded[slot], 16)

    def split_hi(act, slot, loads, tiles_before=None):
        act.wait_ge(w_loaded[slot], loads)
        if tiles_before is not None:
            act.wait_ge(tile_done, tiles_before)
        act.activation(w_hi[:, slot, :], w_raw[:, slot, :], ACT.Copy).then_inc(w_hi_ready, 1)

    def split_lo(dve, slot, chunks):
        dve.wait_ge(w_hi_ready, chunks)
        dve.tensor_tensor(w_lo[:, slot, :], w_raw[:, slot, :], w_hi[:, slot, :].bitcast(F32),
                          ALU.subtract).then_inc(w_lo_ready, 1)

    def products(kt):
        return [(k, w, a) for k in range(kt) for w, a in ((0, 0), (0, 1), (1, 0))]

    def gemm_tile(pe, slot, kt, cols, j, a_hi, a_lo, bank, rows_ready=None):
        w = [x[:, slot, :].rearrange("p (k n) -> p k n", k=kt) for x in (w_hi, w_lo)]
        order = products(kt)
        for n, (k, wi, ai) in enumerate(order):
            if rows_ready is not None and n % 3 == 0:
                pe.wait_ge(rows_ready, k + 1)
            for b in range(NTB):
                mm = pe.matmul(ps[:, bank + b, 0:TB], w[wi][:, k, j * P:(j + 1) * P],
                               (a_hi, a_lo)[ai][:, k, b * TB:(b + 1) * TB],
                               start=(n == 0), stop=(n == len(order) - 1))
        mm.then_inc(tile_done, 1)

    def loads_of(n):
        return 16 * (n // 2 + 1)

    def w_cols(w, col0):
        return w.rearrange("(k p) n -> p k n", p=P)[:, :, bass.ds(col0, NC_)]

    s_const = sem("s_const")
    s_small = sem("s_small")
    s_crow = sem("s_crow")
    s_bada = [sem("s_bada0"), sem("s_bada1")]
    s_ct = sem("s_ct")
    s_cthi = sem("s_cthi")
    s_ctlo = sem("s_ctlo")
    s_vecp = sem("s_vecp")
    s_vect = sem("s_vect")
    s_lam = sem("s_lam")
    s_lame = sem("s_lame")
    s_adarow = sem("s_adarow")
    s_adatp = sem("s_adatp")
    s_adat = sem("s_adat")
    s_gpost = sem("s_gpost")
    s_gst = [sem("s_gst0"), sem("s_gst1")]
    s_xl = [sem("s_xl0"), sem("s_xl1")]
    s_xss = sem("s_xss")
    s_xv = sem("s_xv")
    s_xr = sem("s_xr")
    s_xs = sem("s_xs")
    s_xtp = sem("s_xtp")
    s_xt = sem("s_xt")
    s_aff = sem("s_aff")
    s_ahi = sem("s_ahi")
    s_alo = sem("s_alo")

    def tile_rows(t):
        return P if t < NCH else TS

    def affine_rows(dve, x_t, which, sem_aff):
        A, B = ada_t[:, 2 * which], ada_t[:, 2 * which + 1]
        for k in range(KT):
            dve.tensor_scalar(x_t[:, k, 0:SEQ], x_t[:, k, 0:SEQ], A[:, k, TS:TS + 1], B[:, k, TS:TS + 1],
                              ALU.mult, ALU.add).then_inc(sem_aff, 1)
        dve.tensor_tensor(x_t[:, :, SEQ:T], x_t[:, :, SEQ:T], A[:, :, 0:TS], ALU.mult).then_inc(sem_aff, 1)
        dve.wait_ge(sem_aff, KT + 1)
        dve.tensor_tensor(x_t[:, :, SEQ:T], x_t[:, :, SEQ:T], B[:, :, 0:TS], ALU.add).then_inc(sem_aff, 1)

    def split_rows_hi(act, x_t, sem_aff, sem_hi):
        for k in range(KT):
            act.wait_ge(sem_aff, k + 1)
            act.activation(acts_hi[:, k, 0:SEQ], x_t[:, k, 0:SEQ], ACT.Copy).then_inc(sem_hi, 1)
        act.wait_ge(sem_aff, KT + 2)
        act.activation(acts_hi[:, :, SEQ:T], x_t[:, :, SEQ:T], ACT.Copy).then_inc(sem_hi, 1)

    def split_rows_lo(dve, x_t, sem_hi, sem_lo):
        for k in range(KT):
            dve.wait_ge(sem_hi, k + 1)
            dve.tensor_tensor(acts_lo[:, k, 0:SEQ], x_t[:, k, 0:SEQ], acts_hi[:, k, 0:SEQ].bitcast(F32),
                              ALU.subtract).then_inc(sem_lo, 1)
        dve.wait_ge(sem_hi, KT + 1)
        dve.tensor_tensor(acts_lo[:, :, SEQ:T], x_t[:, :, SEQ:T], acts_hi[:, :, SEQ:T].bitcast(F32),
                          ALU.subtract).then_inc(sem_lo, 1)

    with ExitStack() as scope:
        cur[0] = scope
        c_rows = sb("c_rows", [P, D_MODEL])
        ct_hi = sb("ct_hi", [P, KT, P], F32R)
        ct_lo = sb("ct_lo", [P, KT, P], F32R)
        b_ada = sb("b_ada_rows", [TOK_C, 2, D_MODEL])
        g_post = sb("g_post", [TOK_C, D_MODEL])
        row_vecs = sb("row_vecs", [35, D_FF])
        ffrows, vrows = row_vecs[0:20, :], row_vecs[32:35, 0:D_MODEL]
        lams = sb("lams", [1, 4, DQK])
        lam_e = sb("lam_e", [1, 4])
        lam_p = sb("lam_p", [1, DQK])
        ada_row = sb("ada_row", [TOK_C, 2, NC_])
        x_in = sb("x_in", [P, 2, D_MODEL])
        sq = sb("sq", [P, D_MODEL], mybir.dt.bfloat16)
        st = sb("st", [P, NTT, 3])
        x_t = sb("x_t", [P, KT, T])
        bank_small, bank_x = 3, 4
        bank_ada, bank_adat = 0, 2

        with nc.Block() as block:
            def transposed(n):
                return sum(1 for m in range(n + 1) if m // 4 % 3 != 2)

            def row_count(n):
                return sum(2 if m // 4 % 3 == 2 else 1 for m in range(n + 1))

            def gate_stores(n):
                return sum(1 for m in range(n + 1) if m // 4 % 3 == 2 and m % 2 == n % 2)

            @block.gpsimd
            def _(pool):
                pool.memset(ident[:], 0.0).then_inc(s_const, 1)
                pool.memset(mask_q[:], 0.0).then_inc(s_const, 1)
                pool.memset(mask_s[:], 0.0).then_inc(s_const, 1)
                pool.memset(mask_n[:], 0.0).then_inc(s_const, 1)
                pool.memset(ones[:], 1.0).then_inc(s_const, 1)
                pool.memset(minus_half[:], -0.5).then_inc(s_const, 1)
                pool.memset(same_seq[:], 1.0).then_inc(s_const, 1)
                pool.wait_ge(s_const, 7)
                pool.affine_select(out=ident[:], in_=ident[:], compare_op=ALU.not_equal, fill=1.0, base=0,
                                   pattern=[[-1, P]], channel_multiplier=1).then_inc(s_const, 1)
                pool.affine_select(out=mask_q[:], in_=mask_q[:], compare_op=ALU.is_ge, fill=NEG, base=0,
                                   pattern=[[-1, P]], channel_multiplier=1).then_inc(s_const, 1)
                pool.affine_select(out=mask_s[:], in_=mask_s[:], compare_op=ALU.is_ge, fill=NEG, base=0,
                                   pattern=[[1, P]], channel_multiplier=-1).then_inc(s_const, 1)
                m = mask_n[:].rearrange("p (b t) -> p b t", b=DEC_B)
                pool.affine_select(out=m, in_=m, compare_op=ALU.is_ge, fill=NEG, base=0,
                                   pattern=[[-DEC_T, DEC_B], [0, DEC_T]], channel_multiplier=1).then_inc(s_const, 1)
                pool.affine_select(out=same_seq[:], in_=same_seq[:], compare_op=ALU.is_ge, fill=0.0, base=0,
                                   pattern=[[-DEC_T, DEC_B]], channel_multiplier=1).then_inc(s_const, 1)
                pool.wait_ge(s_const, 12)
                pool.affine_select(out=same_seq[:], in_=same_seq[:], compare_op=ALU.is_ge, fill=0.0, base=DEC_T - 1,
                                   pattern=[[DEC_T, DEC_B]], channel_multiplier=-1).then_inc(s_const, 1)
                pool.affine_select(out=m, in_=m, compare_op=ALU.is_ge, fill=NEG, base=0,
                                   pattern=[[DEC_T, DEC_B], [1, DEC_T]], channel_multiplier=-1).then_inc(s_const, 1)

            @block.sync
            def _(sp):
                sp.dma_start(c_rows[0:TS, :], I["c_sample"].unsqueeze(1).broadcast_to((DEC_B, DEC_T, D_MODEL)))\
                    .then_inc(s_crow, 16)
                sp.dma_start(c_rows[TS:P, :], I["c_prompt"].broadcast_to((P - TS, D_MODEL))).then_inc(s_crow, 16)
                load_chunk(sp, 0, w_cols(I["w_ada"][0], 0), KT)
                load_chunk(sp, 1, w_cols(I["w_ada"][0], NC_), KT)
                for n in range(2, ADA_CHUNKS):
                    load_chunk(sp, n % 2, w_cols(I["w_ada"][0], n * NC_), KT, n - 1)
                for n in range(2):
                    load_chunk(sp, n, w_cols(I["w_in"][0], n * NC_), KT, ADA_CHUNKS - 1 + n)

            @block.scalar
            def _(act):
                for i, nm in enumerate(("lambda_q1", "lambda_k1", "lambda_q2", "lambda_k2")):
                    act.dma_start(lams[:, i, :], I[nm]).then_inc(s_small, 16)
                act.dma_start(vrows[0:1, :], I["g_pre_mix"]).then_inc(s_small, 16)
                act.dma_start(vrows[1:2, :], I["g_pre_ffn"]).then_inc(s_small, 16)
                act.dma_start(vrows[2:3, 0:W_MIX], I["g_mlstm"]).then_inc(s_small, 16)
                act.dma_start(vrows[2:3, W_MIX:2 * W_MIX], I["g_diff"]).then_inc(s_small, 16)
                act.dma_start(ffrows[0:16, :], I["state_conv"][0].rearrange("b w f -> (b w) f")).then_inc(s_small, 16)
                act.dma_start(ffrows[16:19, :], I["conv_w"][0]).then_inc(s_small, 16)
                act.dma_start(ffrows[19:20, :], I["conv_b"]).then_inc(s_small, 16)

                def load_x(t):
                    r = tile_rows(t)
                    src = I["x_prompt"][0, t * P:(t + 1) * P, :] if t < NCH else \
                        I["x_sample"].rearrange("b t d -> (b t) d")
                    act.dma_start(x_in[0:r, t % 2, :], src).then_inc(s_xl[t % 2], 16)

                load_x(0)
                load_x(1)
                for hf in range(2):
                    act.wait_ge(s_ct, hf + 1)
                    act.activation(ct_hi[:, 4 * hf:4 * hf + 4, :], ps[:, bank_x + hf, :].rearrange("p (k n) -> p k n", k=4),
                                   ACT.Copy).then_inc(s_cthi, 1)
                split_hi(act, 0, 16)
                split_hi(act, 1, 16)

                def x_norm(t):
                    r = tile_rows(t)
                    act.wait_ge(s_xl[t % 2], 16 * (t // 2 + 1))
                    if t:
                        act.wait_ge(s_xss, t)
                    act.activation(sq[0:r, :], x_in[0:r, t % 2, :], ACT.Square, accum_out=st[0:r, t, 0:1])\
                        .then_inc(s_xss, 1)

                def x_out(t):
                    r = tile_rows(t)
                    for hf in range(2):
                        act.wait_ge(s_xtp, 2 * t + hf + 1)
                        act.activation(x_t[:, 4 * hf:4 * hf + 4, t * P:t * P + r],
                                       ps[:, bank_x + 2 * (t % 2) + hf, :].rearrange("p (k n) -> p k n", k=4)[:, :, 0:r],
                                       ACT.Copy).then_inc(s_xt, 1)

                for n in range(2, ADA_CHUNKS + 1):
                    split_hi(act, n % 2, 16 * (n // 2 + 1), n - 1)
                    if n == 3:
                        act.wait_ge(s_lam, 4)
                        act.activation(lam_e[:, 2:4], lam_e[:, 0:2], ACT.Exp).then_inc(s_lame, 1)
                    if 3 <= n < 3 + NTT:
                        t = n - 3
                        x_norm(t)
                    if 4 <= n < 4 + NTT:
                        t = n - 4 
                        x_out(t)
                        if t + 2 < NTT:
                            load_x(t + 2)
                split_rows_hi(act, x_t, s_aff, s_ahi)

            @block.vector
            def _(dve):
                for hf in range(2):
                    dve.wait_ge(s_cthi, hf + 1)
                    dve.tensor_tensor(ct_lo[:, 4 * hf:4 * hf + 4, :],
                                      ps[:, bank_x + hf, :].rearrange("p (k n) -> p k n", k=4),
                                      ct_hi[:, 4 * hf:4 * hf + 4, :].bitcast(F32), ALU.subtract).then_inc(s_ctlo, 1)
                split_lo(dve, 0, 1)
                split_lo(dve, 1, 2)
                dve.wait_ge(s_small, 16 * 11)
                for i in range(2):
                    dve.tensor_tensor(lam_p[:], lams[:, 2 * i, :], lams[:, 2 * i + 1, :], ALU.mult).then_inc(s_lam, 1)
                    dve.wait_ge(s_lam, 2 * i + 1)
                    dve.reduce_sum(lam_e[:, i:i + 1], lam_p[:], AX_X).then_inc(s_lam, 1)
                    dve.wait_ge(s_lam, 2 * i + 2)
                dve.wait_ge(s_vecp, 2)
                dve.tensor_copy(vec_t[:], ps[:, 7, 0:3 * KT].rearrange("p (k n) -> p k n", k=KT)).then_inc(s_vect, 1)
                dve.wait_ge(s_vect, 1)
                dve.tensor_scalar(vec_t[:, 4:8, 2], vec_t[:, 4:8, 2], 1.0 - LAM_INIT, None, ALU.mult).then_inc(s_vect, 1)
                dve.tensor_copy(ff_t[:], ps[:, bank_small, 32:32 + 20 * FT].rearrange("p (k n) -> p k n", k=FT)).then_inc(s_vect, 1)

                def ada_evac(n):
                    part, q = n // 4, n % 4
                    if n >= 2:
                        if (n - 2) // 4 % 3 == 2:
                            dve.wait_ge(s_gst[n % 2], 16 * gate_stores(n - 2))
                        else:
                            dve.wait_ge(s_adatp, transposed(n - 2))
                    dve.wait_ge(tile_done, n + 1)
                    dve.wait_ge(s_bada[part % 2], 16 * (part // 2 + 1))
                    ins_ = dve.tensor_tensor(ada_row[:, n % 2, :], ps[0:TOK_C, bank_ada + n % 2, 0:NC_],
                                             b_ada[:, part % 2, q * NC_:(q + 1) * NC_], ALU.add)
                    ins_.then_inc(s_adarow, 1)
                    if part % 3 == 2:
                        dve.wait_ge(s_adarow, row_count(n) - 1)
                        dve.wait_ge(s_gpost, 16 * (part // 3 + 1))
                        dve.tensor_tensor(ada_row[:, n % 2, :], ada_row[:, n % 2, :],
                                          g_post[:, q * NC_:(q + 1) * NC_], ALU.mult).then_inc(s_adarow, 1)

                def ada_cols(n):
                    part, q = n // 4, n % 4
                    if part % 3 == 2:
                        return
                    dve.wait_ge(s_adatp, transposed(n))
                    src = ps[:, bank_adat, 0:2 * TOK_C].rearrange("p (k n) -> p k n", k=2)
                    which = part // 3
                    if part % 3 == 0:
                        dve.tensor_copy(ada_t[:, 2 * which + 1, 2 * q:2 * q + 2, :], src).then_inc(s_adat, 1)
                    else:
                        for kk in range(2):
                            k = 2 * q + kk
                            ins_ = dve.tensor_scalar(ada_t[:, 2 * which, k, :], src[:, kk, :], 1.0,
                                                     vec_t[:, k, which:which + 1], ALU.add, ALU.mult)
                        ins_.then_inc(s_adat, 1)

                def x_scale(t):
                    r = tile_rows(t)
                    dve.wait_ge(s_xss, t + 1)
                    dve.tensor_scalar(st[0:r, t, 1:2], st[0:r, t, 0:1], 1.0 / D_MODEL, EPS, ALU.mult, ALU.add).then_inc(s_xv, 1)
                    dve.wait_ge(s_xr, t + 1)
                    dve.tensor_scalar(x_in[0:r, t % 2, :], x_in[0:r, t % 2, :], st[0:r, t, 2:3], None, ALU.mult)\
                        .then_inc(s_xs, 1)

                for n in range(2, ADA_CHUNKS + 1):
                    split_lo(dve, n % 2, n + 1)
                    ada_evac(n - 2)
                    if n >= 3:
                        ada_cols(n - 3)
                    if n == 4:
                        dve.wait_ge(s_lame, 1)
                        dve.tensor_tensor(lam_e[:, 0:1], lam_e[:, 3:4], lam_e[:, 2:3], ALU.subtract).then_inc(s_lam, 1)
                        dve.wait_ge(s_lam, 5)
                        dve.tensor_scalar(lam_e[:, 0:1], lam_e[:, 0:1], -LAM_INIT, None, ALU.add).then_inc(s_lam, 1)
                    if 3 <= n < 3 + NTT:
                        x_scale(n - 3)
                ada_evac(ADA_CHUNKS - 1)
                dve.wait_ge(s_vecp, 3)
                dve.tensor_copy(neg_lam[:], ps[:, bank_small, 500:501]).then_inc(s_vect, 1)
                dve.wait_ge(s_xt, 2 * NTT)
                dve.wait_ge(s_adat, 16)
                affine_rows(dve, x_t, 0, s_aff)
                split_rows_lo(dve, x_t, s_ahi, s_alo)

            @block.gpsimd
            def _(pool):
                def load_b_ada(pt):
                    pool.dma_start(b_ada[:, pt % 2, :], I["b_ada"][:, pt * D_MODEL:(pt + 1) * D_MODEL]
                                   .broadcast_to((TOK_C, D_MODEL))).then_inc(s_bada[pt % 2], 16)

                def load_g_post(i):
                    pool.dma_start(g_post[:], I[("g_post_mix", "g_post_ffn")[i]].broadcast_to((TOK_C, D_MODEL)))\
                        .then_inc(s_gpost, 16)

                load_b_ada(0)
                load_b_ada(1)
                load_g_post(0)
                for n in range(ADA_CHUNKS):
                    part, q = n // 4, n % 4
                    if q == 0 and 1 <= part < 5:
                        pool.wait_ge(s_adarow, row_count(4 * part - 1))
                        load_b_ada(part + 1)
                    if n == 16:
                        load_g_post(1)
                    if n < NTT:
                        r = tile_rows(n)
                        pool.wait_ge(s_xv, n + 1)
                        pool.tensor_tensor(st[0:r, n, 2:3], st[0:r, n, 1:2], minus_half[0:r, 0:1], ALU.pow).then_inc(s_xr, 1)
                    if part % 3 == 2:
                        pool.wait_ge(s_adarow, row_count(n))
                        pool.dma_start(GATES[part // 3, :, q * NC_:(q + 1) * NC_], ada_row[:, n % 2, :])\
                            .then_inc(s_gst[n % 2], 16)
                for i in range(2):
                    pool.wait_ge(s_gst[i], 16 * 4)

            @block.tensor
            def _(pe):
                pe.wait_ge(s_const, 14)
                pe.wait_ge(s_crow, 32)
                for hf in range(2):
                    for k in range(4):
                        tr = pe.transpose(ps[:, bank_x + hf, k * P:(k + 1) * P],
                                          c_rows[:, (4 * hf + k) * P:(4 * hf + k + 1) * P], ident[:])
                    tr.then_inc(s_ct, 1)
                pe.wait_ge(s_small, 16 * 11)
                for k in range(KT):
                    tr = pe.transpose(ps[:, 7, 3 * k:3 * k + 3], vrows[:, k * P:(k + 1) * P], ident[32:35, 32:35])
                tr.then_inc(s_vecp, 1)
                for k in range(FT):
                    tr = pe.transpose(ps[:, bank_small, 32 + 20 * k:52 + 20 * k], ffrows[:, k * P:(k + 1) * P], ident[0:20, 0:20])
                tr.then_inc(s_vecp, 1)
                pe.wait_ge(s_ctlo, 2)

                def ada_chunk(n):
                    pe.wait_ge(w_lo_ready, n + 1)
                    if n >= 2:
                        pe.wait_ge(s_adarow, row_count(n - 2))
                    w = [x[:, n % 2, :].rearrange("p (k n) -> p k n", k=KT) for x in (w_hi, w_lo)]
                    order = products(KT)
                    for m, (k, wi, ai) in enumerate(order):
                        mm = pe.matmul(ps[:, bank_ada + n % 2, 0:NC_], (ct_hi, ct_lo)[ai][:, k, :], w[wi][:, k, :],
                                       start=(m == 0), stop=(m == len(order) - 1))
                    mm.then_inc(tile_done, 1)

                def ada_tr(n):
                    if n // 4 % 3 == 2:
                        return
                    pe.wait_ge(s_adarow, row_count(n))
                    if transposed(n) > 1:
                        pe.wait_ge(s_adat, transposed(n) - 1)
                    for kk in range(2):
                        tr = pe.transpose(ps[:, bank_adat, kk * TOK_C:(kk + 1) * TOK_C],
                                          ada_row[:, n % 2, kk * P:(kk + 1) * P], ident[0:TOK_C, 0:TOK_C])
                    tr.then_inc(s_adatp, 1)

                def x_tr(t):
                    r = tile_rows(t)
                    pe.wait_ge(s_xs, t + 1)
                    if t >= 2:
                        pe.wait_ge(s_xt, 2 * (t - 1))
                    for hf in range(2):
                        for k in range(4):
                            kk = 4 * hf + k
                            tr = pe.transpose(ps[:, bank_x + 2 * (t % 2) + hf, k * P:k * P + r],
                                              x_in[0:r, t % 2, kk * P:(kk + 1) * P], ident[0:r, 0:r])
                        tr.then_inc(s_xtp, 1)

                for n in range(ADA_CHUNKS):
                    ada_chunk(n)
                    if n >= 1:
                        ada_tr(n - 1)
                    if 3 <= n < 3 + NTT:
                        x_tr(n - 3)
                    if n == 4:
                        pe.wait_ge(s_lam, 6)
                        pe.wait_ge(s_vect, 3)
                        pe.matmul(ps[:, bank_small, 500:501], ones[0:1, :], lam_e[:, 0:1], start=True, stop=True)\
                            .then_inc(s_vecp, 1)

    s_if = sem("s_if")
    s_ifz = sem("s_ifz")
    s_ifhi = sem("s_ifhi")
    s_iflo = sem("s_iflo")
    s_ifmm = sem("s_ifmm")
    s_ifst = sem("s_ifst")
    z_evac = [sem("z_evac_act"), sem("z_evac_dve")]
    s_rl = sem("s_rows_loaded")
    s_rv = sem("s_rows_dve")
    s_ra = sem("s_rows_act")
    s_ends = sem("s_ends_moved")
    s_mrun = sem("s_m_moved")
    s_rst = sem("s_rows_stored")
    z_stored = [[sem(f"z_stored{j}{s}") for s in range(2)] for j in range(2)]
    IN_CHUNKS = 14
    T0 = ADA_CHUNKS
    with ExitStack() as scope:
        cur[0] = scope
        if_raw = sb("if_raw", [P, KT, 2 * H])
        if_hi = sb("if_hi", [P, KT, P], F32R)
        if_lo = sb("if_lo", [P, KT, P], F32R)
        if_out = sb("if_out", [36, T])
        stage = sb("stage", [P, 2, 2, T])
        R = H * NCH
        assert NCH == DEC_B
        b_if = sb("b_if", [R, 2])
        WID = (P, DEC_T)
        raw_i = [sb(f"raw_i{g}", [R, w]) for g, w in enumerate(WID)]
        f_x = [sb(f"f_x{g}", [R, w]) for g, w in enumerate(WID)]
        f_abs = [sb(f"f_abs{g}", [R, w]) for g, w in enumerate(WID)]
        f_sum = [sb(f"f_sum{g}", [R, w]) for g, w in enumerate(WID)]
        a_max = [sb(f"a_max{g}", [R, w]) for g, w in enumerate(WID)]
        m_t = [sb(f"m_t{g}", [R, w]) for g, w in enumerate(WID)]
        rows = [sb(f"rows{g}", [R, 5, w]) for g, w in enumerate(WID)]
        m_in = [sb(f"m_in{g}", [R, 1]) for g in range(2)]
        neg_end = [sb(f"neg_end{g}", [R, 1]) for g in range(2)]
        ends = sb("ends", [H, 2, NCH])
        m_run = sb("m_run", [H, NCH + 1])

        def bank3(b):
            return ps[:, b:b + 3, 0:TB]

        A_END = 16

        with nc.Block() as block:
            @block.gpsimd
            def _(pool):
                pool.dma_start(b_if[:, 0:1], I["b_if"][0, 0:H].unsqueeze(1).broadcast_to((H, NCH)).unsqueeze(2))\
                    .then_inc(s_rl, 16)
                pool.dma_start(b_if[:, 1:2], I["b_if"][0, H:2 * H].unsqueeze(1).broadcast_to((H, NCH)).unsqueeze(2))\
                    .then_inc(s_rl, 16)
                pool.dma_start(m_in[1][:], I["state_m"][0].rearrange("b h -> h b").unsqueeze(2)).then_inc(s_rl, 16)
                for g in range(2):
                    pool.wait_ge(z_evac[g], 1)
                    pool.dma_start(GIFP[g], if_out[32 * g:32 * g + H, 0:SEQ]).then_inc(s_ifst, 16)
                    pool.dma_start(GIFD[g], if_out[32 * g:32 * g + H, SEQ:T]).then_inc(s_ifst, 16)
                pool.wait_ge(s_ifst, 64)
                for g, dst in enumerate((raw_i, f_x)):
                    pool.dma_start(dst[0][:], GIFP[g].rearrange("h (c t) -> (h c) t", c=NCH)).then_inc(s_rl, 16)
                    pool.dma_start(dst[1][:], GIFD[g].rearrange("h (b t) -> (h b) t", b=DEC_B)).then_inc(s_rl, 16)
                pool.wait_ge(s_rl, 16 * 7)
                pool.wait_ge(s_rv, A_END)
                pool.dma_start(ENDS[0].unsqueeze(1), f_sum[0][:, P - 1:P]).then_inc(s_ends, 16)
                pool.dma_start(ENDS[1].unsqueeze(1), a_max[0][:, P - 1:P]).then_inc(s_ends, 16)
                pool.wait_ge(s_ends, 32)
                for q in range(2):
                    pool.dma_start(ends[:, q, :], ENDS[q].rearrange("(h c) -> h c", c=NCH)).then_inc(s_ends, 16)
                pool.wait_ge(s_rv, A_END + 1)
                pool.dma_start(ENDS[2].rearrange("(h c) -> h c", c=NCH), m_run[:, 0:NCH]).then_inc(s_mrun, 16)
                pool.wait_ge(s_mrun, 16)
                pool.dma_start(m_in[0][:], ENDS[2].unsqueeze(1)).then_inc(s_mrun, 16)
                pool.dma_start(O["m_prompt"][0, 0].unsqueeze(1), m_run[:, NCH:NCH + 1]).then_inc(s_rst, 16)
                pool.wait_ge(s_ra, 10)
                pool.dma_start(ROWS.rearrange("q h (c t) -> (h c) q t", c=NCH), rows[0][:]).then_inc(s_rst, 16)
                pool.dma_start(ROWD.rearrange("q h (b t) -> (h b) q t", b=DEC_B), rows[1][:]).then_inc(s_rst, 16)
                pool.dma_start(ENDS[3].unsqueeze(1), rows[0][:, Q_INTER, P - 1:P]).then_inc(s_rst, 16)
                pool.dma_start(DECD[0].unsqueeze(1), rows[1][:, Q_INTER, DEC_T - 1:DEC_T]).then_inc(s_rst, 16)
                pool.dma_start(O["m_sample"][0].rearrange("b h -> h b").unsqueeze(2), m_t[1][:, DEC_T - 1:DEC_T]).then_inc(s_rst, 16)
                pool.wait_ge(s_rst, 96)

            def in_chunks():
                c = 0
                for n, col, zt, sig in IN_SEGMENTS:
                    yield c, n, col, zt, sig
                    c += n

            @block.sync
            def _(sp):
                sp.dma_start(if_raw[:], I["w_in"][0].rearrange("(k p) n -> p k n", p=P)[:, :, IF_COL:IF_COL + 2 * H])\
                    .then_inc(s_if, 16)

                def store(c, s, zt):
                    for j in range(2):
                        sp.wait_ge(z_evac[j], c + 2)
                        sp.dma_start(ZT[bass.ds(zt + j, 1), :, :].rearrange("a p t -> p (a t)"), stage[:, j, s, :])\
                            .then_inc(z_stored[j][s], 16)

                for c0, n, col, zt, sig in in_chunks():
                    nxt = c0 + n
                    if n > 2:
                        with sp.Fori(0, n - 3, 2) as i:
                            for s in range(2):
                                load_chunk(sp, s, w_cols(I["w_in"][0], col + (i + 2 + s) * NC_), KT,
                                           T0 + c0 + 1 + i + s)
                                store(c0 + i + s, s, zt + 2 * (i + s))
                    for s in range(2):
                        m = nxt + s
                        if m < IN_CHUNKS:
                            col2 = next(cc for a, b, cc, _, _ in in_chunks() if a == nxt)
                            load_chunk(sp, s, w_cols(I["w_in"][0], col2 + s * NC_), KT, T0 + m - 1)
                        else:
                            load_chunk(sp, s, w_cols(I["w_in"][0], GATE_COL + s * NC_), KT, T0 + m - 1)
                        store(nxt - 2 + s, s, zt + 2 * (n - 2 + s))
                for j in range(2):
                    for s in range(2):
                        sp.wait_ge(z_stored[j][s], 16 * IN_CHUNKS // 2)

            @block.scalar
            def _(act):
                act.wait_ge(s_if, 16)
                act.wait_ge(s_ifz, 2)
                for g in range(2):
                    act.activation(if_hi[:, :, 32 * g:32 * g + H], if_raw[:, :, g * H:(g + 1) * H], ACT.Copy).then_inc(s_ifhi, 1)

                act.wait_ge(s_ifmm, 1)
                act.activation(if_out[0:H, :].rearrange("p (b t) -> p b t", b=NTB), ps[0:H, 3:6, 0:TB], ACT.Copy)\
                    .then_inc(z_evac[0], 1)

                def chunk(c, s, sig, odd_loads, first):
                    split_hi(act, 1 - s, odd_loads + (16 if s else 0), T0 + 2 * c)
                    for j in range(2 if sig else 1):
                        act.wait_ge(tile_done, T0 + 2 * c + 1 + j)
                        if not first:
                            act.wait_ge(z_stored[j][s], 8 * (c - s))
                        act.activation(stage[:, j, s, :].rearrange("p (b t) -> p b t", b=NTB), bank3(3 * j),
                                       ACT.Sigmoid if sig else ACT.Copy).then_inc(z_evac[j], 1)

                def log_sigmoid():
                    for g in range(2):
                        act.wait_ge(s_rv, 2 + 3 * g)
                        act.activation(f_abs[g][:], f_abs[g][:], ACT.Exp, scale=-1.0).then_inc(s_ra, 1)
                    for g in range(2):
                        act.wait_ge(s_rv, 7 + g)
                        act.activation(f_abs[g][:], f_abs[g][:], ACT.Ln).then_inc(s_ra, 1)

                def row_exps():
                    for g in range(2):
                        act.wait_ge(s_rv, A_END + 1 + 3 * (g + 1))
                        act.activation(rows[g][:, Q_INTER, :], rows[g][:, Q_G, :], ACT.Exp, bias=m_in[g][:], scale=-1.0)\
                            .then_inc(s_ra, 1)
                        act.activation(rows[g][:, Q_EMT, :], m_t[g][:], ACT.Exp, scale=-1.0).then_inc(s_ra, 1)
                        act.activation(rows[g][:, Q_WEND, :], rows[g][:, Q_A, :], ACT.Exp, bias=neg_end[g][:])\
                            .then_inc(s_ra, 1)

                for c0, n, col, zt, sig in in_chunks():
                    if zt == Z_MO:
                        row_exps()
                    if c0 == 0:
                        for s in range(2):
                            chunk(s, s, sig, 8 * T0 + 16, True)
                        log_sigmoid()
                    with act.Fori(2 if c0 == 0 else 0, n - 1, 2) as i:
                        for s in range(2):
                            chunk(i + c0 + s, s, sig, 8 * i + 8 * (T0 + c0) + 16, False)

            @block.vector
            def _(dve):
                dve.memset(if_hi[:].bitcast(F32), 0.0).then_inc(s_ifz, 1)
                dve.memset(if_lo[:].bitcast(F32), 0.0).then_inc(s_ifz, 1)
                dve.wait_ge(s_ifhi, 2)
                dve.wait_ge(s_ifz, 2)
                for g in range(2):
                    dve.tensor_tensor(if_lo[:, :, 32 * g:32 * g + H], if_raw[:, :, g * H:(g + 1) * H],
                                      if_hi[:, :, 32 * g:32 * g + H].bitcast(F32), ALU.subtract).then_inc(s_iflo, 1)
                dve.wait_ge(s_ifmm, 1)
                dve.tensor_copy(if_out[32:32 + H, :].rearrange("p (b t) -> p b t", b=NTB), ps[32:32 + H, 3:6, 0:TB])\
                    .then_inc(z_evac[1], 1)

                def chunk(c, s, sig, first):
                    split_lo(dve, 1 - s, c + T0 + 2)
                    if sig:
                        return
                    dve.wait_ge(tile_done, T0 + 2 * c + 2)
                    if not first:
                        dve.wait_ge(z_stored[1][s], 8 * (c - s))
                    dve.tensor_copy(stage[:, 1, s, :].rearrange("p (b t) -> p b t", b=NTB), bank3(3))\
                        .then_inc(z_evac[1], 1)

                def log_sigmoid():
                    dve.wait_ge(s_rl, 16 * 7)
                    for g in range(2):
                        n0 = 3 * g
                        dve.tensor_scalar(f_x[g][:], f_x[g][:], b_if[:, 1:2], None, ALU.add).then_inc(s_rv, 1)
                        dve.wait_ge(s_rv, n0 + 1)
                        dve.scalar_tensor_tensor(out=f_abs[g][:], in0=f_x[g][:], scalar=-1.0, in1=f_x[g][:],
                                                 op0=ALU.mult, op1=ALU.max).then_inc(s_rv, 1)
                        dve.tensor_scalar(f_x[g][:], f_x[g][:], 0.0, None, ALU.min).then_inc(s_rv, 1)
                    for g in range(2):
                        dve.wait_ge(s_ra, g + 1)
                        dve.tensor_scalar(f_abs[g][:], f_abs[g][:], 1.0, None, ALU.add).then_inc(s_rv, 1)
                    for g in range(2):
                        n0 = 8 + 4 * g
                        dve.wait_ge(s_ra, 3 + g)
                        dve.tensor_tensor(f_x[g][:], f_x[g][:], f_abs[g][:], ALU.subtract).then_inc(s_rv, 1)
                        dve.wait_ge(s_rv, n0 + 1)
                        dve.tensor_tensor_scan(f_sum[g][:], ones[0:R, 0:WID[g]], f_x[g][:], 0.0, ALU.mult, ALU.add)\
                            .then_inc(s_rv, 1)
                        dve.wait_ge(s_rv, n0 + 2)
                        dve.scalar_tensor_tensor(out=rows[g][:, Q_A, :], in0=raw_i[g][:], scalar=b_if[:, 0:1],
                                                 in1=f_sum[g][:], op0=ALU.add, op1=ALU.subtract).then_inc(s_rv, 1)
                        dve.wait_ge(s_rv, n0 + 3)
                        dve.tensor_tensor_scan(a_max[g][:], rows[g][:, Q_A, :], rows[g][:, Q_A, :], NEG * 100,
                                               ALU.max, ALU.max).then_inc(s_rv, 1)

                def chunk_m():
                    dve.memset(m_run[:, 0:1], 0.0)
                    dve.wait_ge(s_ends, 64)
                    dve.tensor_tensor_scan(m_run[:, 1:NCH + 1], ends[:, 1, :], ends[:, 0, :], 0.0, ALU.max, ALU.add)\
                        .then_inc(s_rv, 1)

                def row_gates():
                    dve.wait_ge(s_mrun, 32)
                    for g in range(2):
                        dve.tensor_scalar(rows[g][:, Q_G, :], a_max[g][:], m_in[g][:], None, ALU.max).then_inc(s_rv, 1)
                        dve.wait_ge(s_rv, A_END + 2 + 3 * g)
                        dve.tensor_scalar(neg_end[g][:], rows[g][:, Q_G, WID[g] - 1:WID[g]], -1.0, None, ALU.mult)\
                            .then_inc(s_rv, 1)
                        dve.tensor_tensor(m_t[g][:], f_sum[g][:], rows[g][:, Q_G, :], ALU.add).then_inc(s_rv, 1)

                for c0, n, col, zt, sig in in_chunks():
                    if zt == Z_DQ:
                        chunk_m()
                    if zt == Z_MO:
                        row_gates()
                    if c0 == 0:
                        for s in range(2):
                            chunk(s, s, sig, True)
                        log_sigmoid()
                    with dve.Fori(2 if c0 == 0 else 0, n - 1, 2) as i:
                        for s in range(2):
                            chunk(i + c0 + s, s, sig, False)

            @block.tensor
            def _(pe):
                pe.wait_ge(s_iflo, 2)
                order = products(KT)
                for m, (k, wi, ai) in enumerate(order):
                    for b in range(NTB):
                        mm = pe.matmul(ps[:, 3 + b, 0:TB], (if_hi, if_lo)[wi][:, k, :],
                                       (acts_hi, acts_lo)[ai][:, k, b * TB:(b + 1) * TB],
                                       start=(m == 0), stop=(m == len(order) - 1))
                mm.then_inc(s_ifmm, 1)
                with pe.Fori(0, IN_CHUNKS - 1, 2) as i:
                    for s in range(2):
                        pe.wait_ge(w_lo_ready, T0 + i + s + 1)
                        for j in range(2):
                            pe.wait_ge(z_evac[j], i + s + 1)
                            gemm_tile(pe, s, KT, NC_, j, acts_hi, acts_lo, 3 * j)

    B8 = range(DEC_B)
    PE_STEPS = (["tok_d", "tok_m", "new0", "new1"] + [("kt", 0)] + [x for b in B8[1:] for x in (("sc", b - 1), ("kt", b))] + [("sc", DEC_B - 1)]
                + ["rows0", "rows1", "pt0", "pt1", "pv", "o_rows", "o_cols"]
                + ["s_m", "num1"] + [("ct", 0)] + [x for b in B8[1:] for x in (("cq", b - 1), ("ct", b))] + [("cq", DEC_B - 1)]
                + ["num2", "n_new", "h_cols"] + [("cu", b) for b in B8])
    ACT_STEPS = (["tok_k", "tok_v", "tok_q", "tok_mk", "tok_mv"] + [("kt", b) for b in B8]
                 + ["sd0", "sd1", "exp0", "exp1", "pt0", "ptn0", "pt1", "ptn1", "o_t", "sq"]
                 + [("d", h) for h in range(H)] + [("ct", b) for b in B8] + ["num2_t"]
                 + [("sq", h) for h in range(H)])
    DVE_STEPS = (["one", "new0", "new1"]
                 + [x + str(g) for g in range(2) for x in ("max", "nmax", "rsum", "norm")]
                 + ["at0", "at1"] + [("atn", h) for h in range(H)] + ["o_rows", "o_ms", "o_nrm"]
                 + [("hd", h) for h in range(H)] + ["negg", "wm", "w", "num1a", "num1b", "nq", "nqs", "nqi"]
                 + [("num", h) for h in range(H)] + ["den", "abs", "max", "rec", "h", "ms", "hn"]
                 + [("hm", h) for h in range(H)]
                 + [x for b in B8 for x in (("kw", b), ("cd", b), ("ca", b))] + ["nd", "nn"])
    POOL_STEPS = ["pow_o", "pow_h"]

    class Steps:

        def __init__(self, name, names):
            self.sem, self.at = sem(name), {n: i + 1 for i, n in enumerate(names)}
            self.next = 1
            assert len(self.at) == len(names)

        def done(self, ins_, name):
            assert self.at[name] == self.next, name
            self.next += 1
            ins_.then_inc(self.sem, 1)

        def wait(self, engine, name):
            engine.wait_ge(self.sem, self.at[name])

    d_small = sem("d_small")
    d_zs = sem("d_zs")
    d_tables = sem("d_tables")
    d_kl = [sem("d_kl0"), sem("d_kl1")]
    d_vl = sem("d_vl")
    d_c = sem("d_c")
    d_st = sem("d_stored")
    pes, acs, dvs, pos = (Steps("d_pe", PE_STEPS), Steps("d_act", ACT_STEPS), Steps("d_dve", DVE_STEPS),
                          Steps("d_pool", POOL_STEPS))
    SCALE_D = DQK ** -0.5
    SCALE_M = DH ** -0.5
    PV1 = DH + 1
    GATE0, TILEG = ADA_CHUNKS + IN_CHUNKS, ADA_CHUNKS + 2 * IN_CHUNKS
    PER_CHUNK = 2 * NTB
    GATE_TILES = GATE_CHUNKS * PER_CHUNK
    AT_TOK, AT_K, AT_ROWS, AT_PT, AT_PV = 5, 7, 16, 17, 18
    AT_O = AT_PV + DEC_B
    AT_M, AT_C = AT_O + 1, AT_O + 2
    AT_N2, AT_CU = AT_C + DEC_B + 1, AT_C + DEC_B + 4
    PROJ0, TILE4 = GATE0 + GATE_CHUNKS, TILEG + GATE_TILES
    BG = 6
    gate_evac = sem("gate_evac")
    gate_stored = [sem("gate_stored0"), sem("gate_stored1")]
    NEWC = NPG * PAGE
    NK = NEWC + TS
    with ExitStack() as scope:
        cur[0] = scope
        zs = sb("zs", [P, 28, TS])
        table = sb("table", [1, DEC_B * NPG], I32)
        big = sb("big", [P, DEC_B, H, P])
        big_v = big[:].rearrange("p b h k -> p (b h k)")
        HB = NPG * H * P
        k_pg = big_v[:, 0:2 * HB].rearrange("p (s g n) -> p s g n", s=2, g=NPG)
        kt = big_v[:, 2 * HB:4 * HB].rearrange("p (s g h k) -> p s g h k", s=2, g=NPG, h=H)
        C = big
        v_pg = sb("v_pg", [P, DEC_B, NPG, H * P])
        ks_tok = sb("ks_tok", [TS, H, P])
        vs_tok = sb("vs_tok", [TS, H, P])
        q_tok = sb("q_tok", [TS, H, P])
        mk_tok = sb("mk_tok", [TS, H, P])
        mv_tok = sb("mv_tok", [TS, H, PV1])
        new_t = sb("new_t", [TS, DEC_B, H, 2, DEC_T])
        s_sb = sb("s_sb", [P, NPG, DEC_B, H, 2, DEC_T])
        e_s = sb("e_s", [P, 2, NK])
        sm = sb("sm", [P, 2, 4])
        pt = sb("pt", [P, 2, NPG, P])
        ptn = sb("ptn", [TS, 2, P])
        at = sb("at", [P, 2 * NPG * 4 * H, DEC_T])
        atn = sb("atn", [TS, H, TS])
        o_t = sb("o_t", [P, P])
        o_r = sb("o_r", [P, P])
        o_s = sb("o_s", [P, 3])
        squashed = sb("squashed", [P, 2, TB])
        junk = sb("junk", [P, P], mybir.dt.bfloat16)
        colq = sb("colq", [TS, 5, H])
        g_bc = sb("g_bc", [TS, H, TS])
        dec_bc = sb("dec_bc", [P, H, DEC_B])
        dec8 = sb("dec8", [DEC_B, H])
        d_s = sb("d_s", [TS, H, TS])
        w_s = sb("w_s", [TS, H, TS])
        wm = sb("wm", [TS, DEC_B, H])
        ct = v_pg[:, 0, :, :].rearrange("p s (h k) -> p s h k", h=H)
        kw = v_pg[0:TS, 1, :, :].rearrange("p s (h k) -> p s h k", h=H)
        n_tok = sb("n_tok", [TS, H, P])
        n8 = sb("n8", [DEC_B, H, P])
        num1 = sb("num1", [TS, H, PV1])
        num2 = sb("num2", [P, H, TS])
        nq = sb("nq", [TS, 4, H])

        with nc.Block() as block:
            def counted(part):
                at_ = [0]

                def until(n):
                    for t in range(at_[0], n):
                        part(t)
                    at_[0] = max(at_[0], n)
                return until

            def behind(t):
                return GATE0 + (t - 1) // PER_CHUNK + 1 if (t - 1) % PER_CHUNK == 0 else None

            @block.sync
            def _(sp):
                def gates(t):
                    if t >= 1:
                        c, j, b = (t - 1) // PER_CHUNK, (t - 1) // NTB % 2, (t - 1) % NTB
                        sp.wait_ge(gate_evac, t)
                        sp.dma_start(ZT[Z_GM + 2 * c + j, :, b * TB:(b + 1) * TB], squashed[:, (t - 1) % 2, :])\
                            .then_inc(gate_stored[(t - 1) % 2], 16)
                        n = behind(t)
                        if n is not None and n + 2 < PROJ0 + 2:
                            if n + 2 < PROJ0:
                                load_chunk(sp, n % 2, w_cols(I["w_in"][0], GATE_COL + (n + 2 - GATE0) * NC_), KT, n + 1)
                            else:
                                src = (I["w_proj_m"][0], I["w_proj_d"][0])[n % 2].rearrange("(k p) n -> p k n", p=P)
                                load_chunk(sp, n % 2, src[:, :, 0:CW // 4], W_MIX // P, n + 1)

                until = counted(gates)
                sp.dma_start(table[:], I["page_table"].rearrange("b g -> (b g)").unsqueeze(0)).then_inc(d_tables, 16)
                sp.dma_start(zs[:], ZT[0:28, :, SEQ:T].rearrange("a p t -> p a t")).then_inc(d_zs, 16)
                sp.wait_ge(d_tables, 16)
                load_chunk(sp, 0, w_cols(I["w_in"][0], GATE_COL + 2 * NC_), KT, GATE0 + 1)
                n_pool = I["cache_k"].shape[1]
                for b in range(DEC_B):
                    until(b + 2 if b < 2 else AT_K + b - 2)
                    if b >= 2:
                        pes.wait(sp, ("kt", b - 2))
                    for g in range(NPG):
                        page = sp.value_load(table[0:1, NPG * b + g:NPG * b + g + 1], min_val=0, max_val=n_pool - 1)
                        for dst, src, s in ((k_pg[:, b % 2, g, :], I["cache_k"], d_kl[b % 2]), (v_pg[:, b, g, :], I["cache_v"], d_vl)):
                            sp.dma_start(dst, src[0].rearrange("a p h d -> a p (h d)")[bass.ds(page, 1), :, :]
                                         .rearrange("a p n -> p (a n)")).then_inc(s, 16)
                until(AT_K + DEC_B)
                acs.wait(sp, "tok_v")
                sp.dma_start(O["k_sample"][0].rearrange("b t h d -> (b t) h d"), ks_tok[:]).then_inc(d_st, 16)
                sp.dma_start(O["v_sample"][0].rearrange("b t h d -> (b t) h d"), vs_tok[:]).then_inc(d_st, 16)
                for b in range(DEC_B):
                    until(AT_CU + b + 1)
                    dvs.wait(sp, ("ca", b))
                    sp.dma_start(O["C_sample"][0, b].rearrange("h v d -> v h d"), C[:, b, :, :]).then_inc(d_st, 16)
                dvs.wait(sp, "nn")
                sp.dma_start(O["n_sample"][0], n8[:]).then_inc(d_st, 16)
                until(GATE_TILES + 1)
                sp.wait_ge(d_st, 16 * 11)
                for i in range(2):
                    sp.wait_ge(gate_stored[i], 8 * GATE_TILES)

            @block.gpsimd
            def _(pool):
                dvs.wait(pool, "o_ms")
                pos.done(pool.tensor_tensor(o_s[:, 2:3], o_s[:, 1:2], minus_half[:, 0:1], ALU.pow), "pow_o")
                dvs.wait(pool, "ms")
                pos.done(pool.tensor_tensor(nq[:, 3, :], nq[:, 2, :], minus_half[0:TS, 0:H], ALU.pow), "pow_h")

            @block.scalar
            def _(act):
                act.dma_start(colq[:], ROWD.rearrange("q h t -> t q h").unsqueeze(3)).then_inc(d_small, 16)
                act.dma_start(g_bc[:], ROWD[Q_G].unsqueeze(0).broadcast_to((TS, H, TS))).then_inc(d_small, 16)
                act.dma_start(dec_bc[:], DECD[0].rearrange("(h b) -> h b", h=H).unsqueeze(0).broadcast_to((P, H, DEC_B))).then_inc(d_small, 16)
                act.dma_start(dec8[:], DECD[0].rearrange("(h b) -> b h", h=H).unsqueeze(2)).then_inc(d_small, 16)
                act.dma_start(n_tok[:], I["state_n"][0].unsqueeze(1).broadcast_to((DEC_B, DEC_T, H, P))).then_inc(d_small, 16)
                act.dma_start(n8[:], I["state_n"][0]).then_inc(d_small, 16)

                def gates(t):
                    if t >= 1:
                        act.wait_ge(tile_done, TILEG + t)
                        if t > 2:
                            act.wait_ge(gate_stored[(t - 1) % 2], 16 * ((t - 1) // 2))
                        act.activation(squashed[:, (t - 1) % 2, :], ps[:, BG + (t - 1) % 2, 0:TB], ACT.Sigmoid).then_inc(gate_evac, 1)
                        n = behind(t)
                        if n is not None:
                            split_hi(act, n % 2, loads_of(n), TILEG + t - 1)

                until = counted(gates)

                def load_states():
                    pes.wait(act, ("sc", DEC_B - 1))
                    for b in range(0, DEC_B, 2):
                        act.dma_start(C[:, b:b + 2, :, :], I["state_C"][0, b:b + 2].rearrange("b h v d -> v (b h) d")).then_inc(d_c, 16)

                def bank(n, rows, cols_):
                    return ps[0:rows, n, 0:cols_]

                until(AT_TOK)
                pes.wait(act, "tok_d")
                acs.done(act.activation(ks_tok[:], bank(0, TS, 512).rearrange("p (h d) -> p h d", h=H), ACT.Copy), "tok_k")
                acs.done(act.activation(vs_tok[:], bank(1, TS, 512).rearrange("p (h d) -> p h d", h=H), ACT.Copy), "tok_v")
                pes.wait(act, "tok_m")
                acs.done(act.activation(q_tok[:], bank(2, TS, 512).rearrange("p (h d) -> p h d", h=H), ACT.Copy), "tok_q")
                acs.done(act.activation(mk_tok[:], bank(3, TS, 512).rearrange("p (h d) -> p h d", h=H), ACT.Copy,
                                        scale=SCALE_M), "tok_mk")
                acs.done(act.activation(mv_tok[:, :, 0:DH], bank(4, TS, 512).rearrange("p (h d) -> p h d", h=H), ACT.Copy), "tok_mv")
                for b in B8:
                    until(AT_K + b)
                    pes.wait(act, ("kt", b))
                    if b >= 2:
                        pes.wait(act, ("sc", b - 2))
                    k0 = 2 * (b % 2)
                    acs.done(act.activation(kt[:, b % 2, :, :, :], ps[:, k0:k0 + 2, :].rearrange("p g (h k) -> p g h k", h=H), ACT.Copy),
                             ("kt", b))
                until(AT_K + DEC_B)
                load_states()
                for m, bk in ((0, 4), (1, 5)):
                    acs.done(act.activation(s_sb[:, :, :, :, m, :].rearrange("p g b h t -> p (g b h) t"),
                                            ps[:, bk, 0:NPG * DEC_B * H * DEC_T].rearrange("p (a t) -> p a t", t=DEC_T), ACT.Copy), f"sd{m}")
                until(AT_ROWS)
                for g in range(2):
                    dvs.wait(act, f"nmax{g}")
                    acs.done(act.activation(e_s[:, g, :], ps[:, g, 0:NK], ACT.Exp, bias=sm[:, g, 1:2], scale=SCALE_D,
                                            accum_out=sm[:, g, 2:3]), f"exp{g}")
                until(AT_PT)
                for g in range(2):
                    pes.wait(act, f"pt{g}")
                    acs.done(act.activation(pt[:, g, :, :], ps[:, 2 + g, 0:NPG * P].rearrange("p (g k) -> p g k", g=NPG), ACT.Copy), f"pt{g}")
                    acs.done(act.activation(ptn[:, g, :], ps[0:TS, 2 + g, NPG * P:(NPG + 1) * P], ACT.Copy), f"ptn{g}")
                until(AT_O - 1)
                pes.wait(act, "pv")
                acs.done(act.activation(o_t[:], ps[:, 5, 0:P], ACT.Copy), "o_t")
                until(AT_O)
                dvs.wait(act, "o_rows")
                acs.done(act.activation(junk[:], o_r[:], ACT.Square, accum_out=o_s[:, 0:1]), "sq")
                until(AT_M)
                dvs.wait(act, "negg")
                for h in range(H):
                    acs.done(act.activation(d_s[:, h, :], g_bc[:, h, :], ACT.Exp, bias=colq[:, Q_A, h:h + 1]), ("d", h))
                for b in B8:
                    until(AT_C + b)
                    pes.wait(act, ("ct", b))
                    if b >= 2:
                        pes.wait(act, ("cq", b - 2))
                    acs.done(act.activation(ct[:, b % 2, :, :], ps[:, b % 2, :].rearrange("p (h k) -> p h k", h=H), ACT.Copy), ("ct", b))
                until(AT_C + DEC_B)
                pes.wait(act, ("cq", DEC_B - 1))
                acs.done(act.activation(num2[:], ps[:, 5, 0:H * TS].rearrange("p (h t) -> p h t", h=H), ACT.Copy), "num2_t")
                until(AT_N2)
                dvs.wait(act, "h")
                for h in range(H):
                    acs.wait(act, ("sq", h - 1) if h else "num2_t")
                    acs.done(act.activation(junk[0:TS, :], num1[:, h, 0:DH], ACT.Square, accum_out=nq[:, 1, h:h + 1]), ("sq", h))
                until(GATE_TILES + 1)

            @block.vector
            def _(dve):
                def gates(t):
                    if t >= 1 and behind(t) is not None:
                        split_lo(dve, behind(t) % 2, behind(t) + 1)

                until = counted(gates)
                dvs.done(dve.memset(mv_tok[:, :, DH:PV1], 1.0), "one")
                until(AT_TOK)
                for m in range(2):
                    until(AT_TOK + m)
                    pes.wait(dve, f"new{m}")
                    dvs.done(dve.tensor_tensor(new_t[:, :, :, m, :].rearrange("p b h t -> p h b t"),
                                               ps[0:TS, (5, 0)[m], 0:H * TS].rearrange("p (h b t) -> p h b t", h=H, b=DEC_B),
                                               mask_n[:].rearrange("p (b t) -> p b t", b=DEC_B).unsqueeze(1)
                                               .broadcast_to((TS, H, DEC_B, DEC_T)), ALU.add), f"new{m}")
                until(AT_ROWS)
                for g in range(2):
                    pes.wait(dve, f"rows{g}")
                    dvs.done(dve.tensor_reduce(sm[:, g, 0:1], ps[:, g, 0:NK], AX_X, ALU.max), f"max{g}")
                    dvs.wait(dve, f"max{g}")
                    dvs.done(dve.tensor_scalar(sm[:, g, 1:2], sm[:, g, 0:1], -SCALE_D, None, ALU.mult), f"nmax{g}")
                    acs.wait(dve, f"exp{g}")
                    dvs.done(dve.reciprocal(sm[:, g, 3:4], sm[:, g, 2:3]), f"rsum{g}")
                    dvs.wait(dve, f"rsum{g}")
                    dvs.done(dve.tensor_scalar(e_s[:, g, :], e_s[:, g, :], sm[:, g, 3:4], None, ALU.mult), f"norm{g}")
                until(AT_PT)
                for g in range(2):
                    acs.wait(dve, f"ptn{g}")
                    v = pt[:, g, :, :].rearrange("p g (a m t) -> p (g a) m t", m=2, t=DEC_T)
                    dvs.done(dve.scalar_tensor_tensor(out=at[:, 32 * g:32 * g + 32, :], in0=v[:, :, 1, :], scalar=neg_lam[:],
                                                      in1=v[:, :, 0, :], op0=ALU.mult, op1=ALU.add), f"at{g}")
                vn = ptn[:].rearrange("p g (b h m t) -> p (g b) h m t", b=4, h=H, m=2)
                for h in range(H):
                    dvs.done(dve.scalar_tensor_tensor(out=atn[:, h, :].rearrange("p (b t) -> p b t", t=DEC_T), in0=vn[:, :, h, 1, :],
                                                      scalar=neg_lam[0:TS], in1=vn[:, :, h, 0, :],
                                                      op0=ALU.mult, op1=ALU.add), ("atn", h))
                until(AT_O)
                pes.wait(dve, "o_rows")
                dvs.done(dve.tensor_copy(o_r[:], ps[:, 0, 0:P]), "o_rows")
                acs.wait(dve, "sq")
                dvs.done(dve.tensor_scalar(o_s[:, 1:2], o_s[:, 0:1], 1.0 / DH, EPS, ALU.mult, ALU.add), "o_ms")
                pos.wait(dve, "pow_o")
                dvs.done(dve.tensor_scalar(o_r[:], o_r[:], o_s[:, 2:3], None, ALU.mult), "o_nrm")
                until(AT_M)
                pes.wait(dve, "o_cols")
                for h in range(H):
                    dvs.done(dve.tensor_scalar(branch_s[:, H + h, :], ps[:, 1, h * TS:(h + 1) * TS], vec_t[:, 4 + h, 2:3], None, ALU.mult), ("hd", h))

                dve.wait_ge(d_small, 16 * 6)
                dvs.done(dve.tensor_tensor(g_bc[:], mask_n[:].unsqueeze(1).broadcast_to((TS, H, TS)), g_bc[:], ALU.subtract), "negg")
                dvs.done(dve.tensor_tensor(wm[:], same_seq[:].unsqueeze(2).broadcast_to((TS, DEC_B, H)),
                                           colq[:, Q_WEND, :].unsqueeze(1).broadcast_to((TS, DEC_B, H)), ALU.mult), "wm")
                pes.wait(dve, "s_m")
                acs.wait(dve, ("d", H - 1))
                dvs.done(dve.scalar_tensor_tensor(out=w_s[:].rearrange("p h t -> p (h t)"), in0=ps[0:TS, 4, 0:H * TS], scalar=SCALE_M,
                                                  in1=d_s[:].rearrange("p h t -> p (h t)"), op0=ALU.mult, op1=ALU.mult), "w")
                until(AT_C)
                pes.wait(dve, "num1")
                dvs.done(dve.tensor_copy(num1[:, 0:3, :], ps[0:TS, 2, 0:3 * PV1].rearrange("p (h v) -> p h v", h=3)), "num1a")
                dvs.done(dve.tensor_copy(num1[:, 3, :], ps[0:TS, 3, 0:PV1]), "num1b")
                acs.wait(dve, "tok_q")
                dvs.done(dve.tensor_tensor(q_tok[:], q_tok[:], n_tok[:], ALU.mult), "nq")
                dvs.wait(dve, "nq")
                dvs.done(dve.tensor_reduce(nq[:, 0, :], q_tok[:], AX_X, ALU.add), "nqs")
                dvs.wait(dve, "nqs")
                dvs.done(dve.tensor_tensor(nq[:, 0, :], nq[:, 0, :], colq[:, Q_INTER, :], ALU.mult), "nqi")
                until(AT_N2)
                pes.wait(dve, "num2")
                for h in range(H):
                    dvs.done(dve.scalar_tensor_tensor(out=num1[:, h, 0:DH], in0=ps[0:TS, 4, h * P:(h + 1) * P],
                                                      scalar=colq[:, Q_INTER, h:h + 1], in1=num1[:, h, 0:DH],
                                                      op0=ALU.mult, op1=ALU.add), ("num", h))
                dvs.wait(dve, ("num", H - 1))
                dvs.done(dve.tensor_tensor(nq[:, 0, :], nq[:, 0, :], num1[:, :, DH], ALU.add), "den")
                dvs.wait(dve, "den")
                dvs.done(dve.scalar_tensor_tensor(out=nq[:, 1, :], in0=nq[:, 0, :], scalar=-1.0, in1=nq[:, 0, :],
                                                  op0=ALU.mult, op1=ALU.max), "abs")
                dvs.wait(dve, "abs")
                dvs.done(dve.tensor_tensor(nq[:, 1, :], nq[:, 1, :], colq[:, Q_EMT, :], ALU.max), "max")
                dvs.wait(dve, "max")
                dvs.done(dve.reciprocal(nq[:, 2, :], nq[:, 1, :]), "rec")
                dvs.wait(dve, "rec")
                dvs.done(dve.tensor_tensor(num1[:, :, 0:DH], num1[:, :, 0:DH], nq[:, 2, :].unsqueeze(2).broadcast_to((TS, H, DH)),
                                           ALU.mult), "h")
                acs.wait(dve, ("sq", H - 1))
                dvs.done(dve.tensor_scalar(nq[:, 2, :], nq[:, 1, :], 1.0 / DH, EPS, ALU.mult, ALU.add), "ms")
                pos.wait(dve, "pow_h")
                dvs.done(dve.tensor_tensor(num1[:, :, 0:DH], num1[:, :, 0:DH], nq[:, 3, :].unsqueeze(2).broadcast_to((TS, H, DH)),
                                           ALU.mult), "hn")
                until(AT_N2 + 2)
                pes.wait(dve, "h_cols")
                for h in range(H):
                    dvs.done(dve.scalar_tensor_tensor(out=branch_s[:, h, :], in0=ps[:, 2, h * TS:(h + 1) * TS], scalar=vec_t[:, h, 2:3],
                                                      in1=zs[:, Z_MO + h, :], op0=ALU.mult, op1=ALU.mult), ("hm", h))
                dve.wait_ge(d_c, 64)
                for b in B8:
                    until(AT_CU + b - 1)
                    if b >= 2:
                        pes.wait(dve, ("cu", b - 2))
                    dvs.done(dve.tensor_tensor(kw[:, b % 2, :, :], mk_tok[:], wm[:, b, :].unsqueeze(2).broadcast_to((TS, H, P)), ALU.mult),
                             ("kw", b))
                    dvs.done(dve.tensor_tensor(C[:, b, :, :], C[:, b, :, :], dec_bc[:, :, b].unsqueeze(2).broadcast_to((P, H, P)), ALU.mult),
                             ("cd", b))
                    until(AT_CU + b)
                    pes.wait(dve, ("cu", b))
                    dvs.wait(dve, ("cd", b))
                    dvs.done(dve.tensor_tensor(C[:, b, :, :], C[:, b, :, :], ps[:, b % 2, :].rearrange("p (h k) -> p h k", h=H), ALU.add),
                             ("ca", b))
                dvs.done(dve.tensor_tensor(n8[:], n8[:], dec8[:].unsqueeze(2).broadcast_to((DEC_B, H, P)), ALU.mult), "nd")
                dvs.wait(dve, "nd")
                dvs.done(dve.tensor_tensor(n8[:], n8[:], ps[0:DEC_B, 3, :].rearrange("p (h k) -> p h k", h=H), ALU.add), "nn")
                until(GATE_TILES)

            @block.tensor
            def _(pe):
                def gates(t):
                    c, j, b = t // PER_CHUNK, t // NTB % 2, t % NTB
                    if t % PER_CHUNK == 0:
                        pe.wait_ge(w_lo_ready, GATE0 + c + 1)
                    if t >= 2:
                        pe.wait_ge(gate_evac, t - 1)
                    w = [x[:, c % 2, :].rearrange("p (k n) -> p k n", k=KT) for x in (w_hi, w_lo)]
                    order = products(KT)
                    for n, (k, wi, ai) in enumerate(order):
                        mm = pe.matmul(ps[:, BG + t % 2, 0:TB], w[wi][:, k, j * P:(j + 1) * P],
                                       (acts_hi, acts_lo)[ai][:, k, b * TB:(b + 1) * TB],
                                       start=(n == 0), stop=(n == len(order) - 1))
                    mm.then_inc(tile_done, 1)

                until = counted(gates)
                until(AT_TOK)
                pe.wait_ge(d_zs, 16)
                for bk, z in enumerate((Z_DK, Z_DV, Z_MQ, Z_MK, Z_MV)):
                    for h in range(H):
                        tr = pe.transpose(ps[0:TS, bk, h * P:(h + 1) * P], zs[:, z + h, :], ident[:])
                    if bk in (1, 4):
                        pes.done(tr, "tok_d" if bk == 1 else "tok_m")
                for m in range(2):
                    if m:
                        until(AT_TOK + 1)
                        acs.wait(pe, "tok_k")
                    for h in range(H):
                        mm = pe.matmul(ps[0:TS, (5, 0)[m], h * TS:(h + 1) * TS], zs[m * DQK:(m + 1) * DQK, Z_DK + h, :],
                                       zs[m * DQK:(m + 1) * DQK, Z_DQ + h, :], start=True, stop=True)
                    pes.done(mm, f"new{m}")
                acs.wait(pe, "tok_mv")
                dvs.wait(pe, "new1")

                def k_transposes(b):
                    pe.wait_ge(d_kl[b % 2], 16 * NPG * (b // 2 + 1))
                    if b >= 2:
                        acs.wait(pe, ("kt", b - 2))
                    for g in range(NPG):
                        for h in range(H):
                            tr = pe.transpose(ps[:, 2 * (b % 2) + g, h * P:(h + 1) * P], k_pg[:, b % 2, g, h * P:(h + 1) * P], ident[:])
                    pes.done(tr, ("kt", b))

                def scores(b):
                    acs.wait(pe, ("kt", b))
                    for m, bk in ((0, 4), (1, 5)):
                        for g in range(NPG):
                            for h in range(H):
                                c0 = ((g * DEC_B + b) * H + h) * DEC_T
                                mm = pe.matmul(ps[:, bk, c0:c0 + DEC_T], kt[m * DQK:(m + 1) * DQK, b % 2, g, h, :],
                                               zs[m * DQK:(m + 1) * DQK, Z_DQ + h, DEC_T * b:DEC_T * (b + 1)], start=True, stop=True)
                    pes.done(mm, ("sc", b))

                for b in B8:
                    until(AT_K + b)
                    if b:
                        scores(b - 1)
                    k_transposes(b)
                until(AT_K + DEC_B)
                scores(DEC_B - 1)
                until(AT_ROWS)
                acs.wait(pe, "sd1")
                for g in range(2):
                    for pg in range(NPG):
                        pe.transpose(ps[:, g, pg * P:(pg + 1) * P], s_sb[:, pg, 4 * g:4 * g + 4, :, :, :].rearrange("p b h m t -> p (b h m t)"),
                                     ident[:])
                    pes.done(pe.transpose(ps[:, g, NEWC:NK], new_t[:, 4 * g:4 * g + 4, :, :, :].rearrange("p b h m t -> p (b h m t)"),
                                          ident[0:TS, 0:TS]), f"rows{g}")
                until(AT_PT)
                for g in range(2):
                    dvs.wait(pe, f"norm{g}")
                    for pg in range(NPG):
                        pe.transpose(ps[:, 2 + g, pg * P:(pg + 1) * P], e_s[:, g, pg * P:(pg + 1) * P], ident[:])
                    pes.done(pe.transpose(ps[0:TS, 2 + g, NPG * P:(NPG + 1) * P], e_s[:, g, NEWC:NK], ident[:]), f"pt{g}")
                until(AT_PV)
                dvs.wait(pe, ("atn", H - 1))
                pe.wait_ge(d_vl, 16 * NPG * DEC_B)
                for h in range(H):
                    pe.matmul(ps[:, 5, h * TS:(h + 1) * TS], vs_tok[:, h, :], atn[:, h, :], start=(h == 0), stop=False, skip_group_check=True)
                for b in B8:
                    until(AT_PV + b)
                    for pg in range(NPG):
                        for h in range(H):
                            a = ((b // 4 * NPG + pg) * 4 + b % 4) * H + h
                            mm = pe.matmul(ps[:, 5, h * TS + DEC_T * b:h * TS + DEC_T * (b + 1)], v_pg[:, b, pg, h * P:(h + 1) * P],
                                           at[:, a, :], start=False, stop=(pg == NPG - 1), skip_group_check=True)
                pes.done(mm, "pv")
                until(AT_O)
                acs.wait(pe, "o_t")
                pes.done(pe.transpose(ps[:, 0, 0:P], o_t[:], ident[:]), "o_rows")
                until(AT_M)
                dvs.wait(pe, "o_nrm")
                pes.done(pe.transpose(ps[:, 1, 0:P], o_r[:], ident[:]), "o_cols")

                for h in range(H):
                    mm = pe.matmul(ps[0:TS, 4, h * TS:(h + 1) * TS], zs[:, Z_MK + h, :], zs[:, Z_MQ + h, :], start=True, stop=True)
                pes.done(mm, "s_m")
                until(AT_C)
                dvs.wait(pe, "w")
                for h in range(H):
                    mm = pe.matmul(ps[0:TS, 2 + h // 3, h % 3 * PV1:h % 3 * PV1 + PV1], w_s[:, h, :], mv_tok[:, h, :], start=True, stop=True)
                pes.done(mm, "num1")
                pe.wait_ge(d_c, 64)

                def state_q(b):
                    acs.wait(pe, ("ct", b))
                    for h in range(H):
                        mm = pe.matmul(ps[:, 5, h * TS + DEC_T * b:h * TS + DEC_T * (b + 1)], ct[:, b % 2, h, :],
                                       zs[:, Z_MQ + h, DEC_T * b:DEC_T * (b + 1)], start=True, stop=True)
                    pes.done(mm, ("cq", b))

                for b in B8:
                    until(AT_C + b)
                    if b:
                        state_q(b - 1)
                    if b == 1:
                        dvs.wait(pe, ("hd", H - 1))
                    if b >= 2:
                        acs.wait(pe, ("ct", b - 2))
                    for h in range(H):
                        tr = pe.transpose(ps[:, b % 2, h * P:(h + 1) * P], C[:, b, h, :], ident[:])
                    pes.done(tr, ("ct", b))
                until(AT_C + DEC_B)
                state_q(DEC_B - 1)
                until(AT_N2)
                acs.wait(pe, "num2_t")
                for h in range(H):
                    tr = pe.transpose(ps[0:TS, 4, h * P:(h + 1) * P], num2[:, h, :], ident[:])
                pes.done(tr, "num2")
                dvs.wait(pe, "num1b")
                for h in range(H):
                    mm = pe.matmul(ps[0:DEC_B, 3, h * P:(h + 1) * P], wm[:, :, h], mk_tok[:, h, :], start=True, stop=True)
                pes.done(mm, "n_new")
                until(AT_N2 + 2)
                dvs.wait(pe, "hn")
                for h in range(H):
                    tr = pe.transpose(ps[:, 2, h * TS:(h + 1) * TS], num1[:, h, 0:DH], ident[0:TS, 0:TS])
                pes.done(tr, "h_cols")
                for b in B8:
                    until(AT_CU + b)
                    dvs.wait(pe, ("kw", b))
                    if b >= 2:
                        dvs.wait(pe, ("ca", b - 2))
                    for h in range(H):
                        mm = pe.matmul(ps[:, b % 2, h * P:(h + 1) * P], mv_tok[:, h, 0:DH], kw[:, b % 2, h, :], start=True, stop=True)
                    pes.done(mm, ("cu", b))
                until(GATE_TILES)

    s_rowl = sem("s_rowl")
    s_rowp = sem("s_rowp")
    s_rowt = sem("s_rowt")
    d_loaded = sem("d_loaded")
    m_loaded = sem("m_loaded")
    tr_full = sem("tr_full")
    tr_free = sem("tr_free")
    kv_stored = sem("kv_stored")
    a_scores = sem("a_scores")
    a_max_ = sem("a_max")
    a_exp = sem("a_exp")
    a_coef = sem("a_coef")
    a_diff = sem("a_diff")
    m_sqs = sem("m_sqs")
    s_ones1 = sem("s_ones1")
    a_pv = sem("a_pv")
    a_out = sem("a_out")
    a_sq = sem("a_sq")
    o_rstd = sem("o_rstd")
    o_norm = sem("o_norm")
    o_tr = sem("o_tr")
    o_cols = sem("o_cols")
    o_hi = sem("o_hi")
    o_lo = sem("o_lo")
    m_prep = sem("m_prep")
    m_negg = sem("m_negg")
    m_s = sem("m_s")
    m_d = sem("m_d")
    m_p = sem("m_p")
    m_num = sem("m_num")
    m_cu = sem("m_cu")
    m_c = sem("m_c")
    m_tmp = sem("m_tmp")
    m_numv = sem("m_numv")
    m_den = sem("m_den")
    m_state = sem("m_state")
    FILLS_KV = 4
    FILLS_A = FILLS_KV + sum((i + 4) // 4 for i in range(NCH))
    FILLS_M = NCH + 1
    FILLS = FILLS_A + FILLS_M
    with ExitStack() as scope:
        cur[0] = scope
        row_in = sb("row_in", [H * NCH, 5, P])
        zq, zk, zv = (sb(f"z_d{x}", [P, SEQ]) for x in "qkv")
        mq, mk, mv, mo = (sb(f"z_m{x}", [P, SEQ]) for x in "qkvo")
        k_tok = sb("k_tok", [P, NCH, P])
        v_tok = sb("v_tok", [P, NCH, P])
        E_ = sb("e_maps", [P, 2, SEQ])
        p_t = sb("p_t", [P, NCH, P])
        stat = sb("stat", [P, 2, 8])
        mix = sb("mix", [P, NCH, PV1])
        ssq = sb("ssq", [P, 4, NCH])
        sqj = sb("sqj", [P, NCH, P], mybir.dt.bfloat16)
        cols = sb("cols", [P, SEQ])
        neg_g = sb("neg_g", [P, NCH, P])
        v_1 = sb("v_1", [P, 2, PV1])
        k_w = sb("k_w", [P, 2, P])
        d_t = sb("d_t", [P, 2, P])
        w_t = sb("w_t", [P, 2, P])
        inter_v = sb("inter_v", [P, 2, PV1])
        c_st = sb("c_st", [P, 2, PV1])
        c_out = sb("c_out", [P, P])
        BS, BO, BT, BF = 0, 4, 5, 7

        with nc.Block() as block:
            def split_mix_hi(act, row, n):
                for hf in range(2):
                    act.wait_ge(o_cols, 2 * n + hf + 1)
                    act.activation(acts_hi[:, row, 512 * hf:512 * hf + 512], cols[:, 512 * hf:512 * hf + 512], ACT.Copy).then_inc(o_hi, 1)

            def out_rows(dve, h, i):
                dve.wait_ge(a_pv, NCH * h + i + 1)
                dve.tensor_scalar(mix[:, i, 0:DH], ps[:, BO, 0:DH], stat[:, i % 2, 2:3], None, ALU.mult).then_inc(a_out, 1)

            @block.sync
            def _(sp):
                sp.dma_start(row_in[:], ROWS.rearrange("q h (c t) -> (h c) q t", c=NCH)).then_inc(s_rowl, 16)
                sp.dma_start(decay_p[:], ENDS[3].unsqueeze(0).broadcast_to((P, H * NCH))).then_inc(s_rowl, 16)
                for h in range(H):
                    if h:
                        sp.wait_ge(a_pv, NCH * h)
                    for dst, z in ((zq, Z_DQ), (zk, Z_DK), (zv, Z_DV)):
                        sp.dma_start(dst[:], ZT[z + h, :, 0:SEQ]).then_inc(d_loaded, 16)
                    if h:
                        sp.wait_ge(m_num, NCH * h)
                        sp.wait_ge(o_cols, 2 * 2 * h)
                    for dst, z in ((mq, Z_MQ), (mk, Z_MK), (mv, Z_MV), (mo, Z_MO)):
                        sp.dma_start(dst[:], ZT[z + h, :, 0:SEQ]).then_inc(m_loaded, 16)
                    sp.dma_start(neg_g[:], ROWS[Q_G, h].rearrange("(c t) -> c t", c=NCH).unsqueeze(0)
                                 .broadcast_to((P, NCH, P))).then_inc(m_loaded, 16)
                    sp.wait_ge(tr_free, FILLS * h + FILLS_KV)
                    for dst, src in ((O["k_prompt"], k_tok), (O["v_prompt"], v_tok)):
                        sp.dma_start(dst[0, 0].rearrange("(c p) h d -> p c h d", p=P)[:, :, h, :], src[:]).then_inc(kv_stored, 16)
                    sp.wait_ge(tr_free, FILLS * (h + 1))
                    sp.wait_ge(m_c, NCH * (h + 1))
                    sp.dma_start(O["C_prompt"][0, 0, h], c_out[:]).then_inc(m_state, 16)
                    sp.dma_start(O["n_prompt"][0, 0, h].unsqueeze(1), c_st[:, NCH % 2, DH:PV1]).then_inc(m_state, 16)
                sp.wait_ge(kv_stored, 32 * H)
                sp.wait_ge(m_state, 32 * H)

            @block.gpsimd
            def _(pool):
                for n in range(2 * H):
                    h, br = n // 2, n % 2
                    if br:
                        pool.wait_ge(m_den, 5 * h + 5)
                    else:
                        pool.wait_ge(a_out, (NCH + 1) * (h + 1))
                    pool.tensor_tensor(ssq[:, 2 * br + 1, :], ssq[:, 2 * br, :], minus_half[:, 0:NCH], ALU.pow).then_inc(o_rstd, 1)

            @block.scalar
            def _(act):
                act.wait_ge(s_rowp, 1)
                act.activation(rows_t[:], ps[:, BF, 0:5 * H * NCH].rearrange("p (q r) -> p q r", q=5), ACT.Copy).then_inc(s_rowt, 1)

                def fill(n, dst, cnt):
                    act.wait_ge(tr_full, n + 1)
                    act.activation(dst, ps[:, BT + n % 2, 0:cnt * P].rearrange("p (c k) -> p c k", c=cnt), ACT.Copy).then_inc(tr_free, 1)

                def square(h, i):
                    act.wait_ge(a_out, (NCH + 1) * h + i + 1)
                    if h or i:
                        act.wait_ge(a_sq, NCH * h + i)
                    if h and i == 0:
                        act.wait_ge(m_sqs, NCH * h)
                    act.activation(sqj[:, 0, :], mix[:, i, 0:DH], ACT.Square, accum_out=ssq[:, 0, i:i + 1]).then_inc(a_sq, 1)

                for h in range(H):
                    f = FILLS * h
                    if h:
                        act.wait_ge(kv_stored, 32 * h)
                    for n in range(FILLS_KV):
                        dst = (v_tok, k_tok)[n // 2]
                        fill(f, dst[:, 4 * (n % 2):4 * (n % 2) + 4, :], 4)
                        f += 1
                    for i in range(NCH):
                        u = NCH * h + i
                        keys = (i + 1) * P
                        act.wait_ge(a_max_, 3 * u + 3)
                        for m in range(2):
                            act.activation(E_[:, m, 0:keys], ps[:, BS + 2 * m:BS + 2 * m + 2, :].rearrange("p b n -> p (b n)")[:, 0:keys],
                                           ACT.Exp, bias=stat[:, i % 2, 4 + m:5 + m], scale=SCALE_D,
                                           accum_out=stat[:, i % 2, m:m + 1]).then_inc(a_exp, 1)
                        if u:
                            act.wait_ge(a_pv, u)
                        for n in range((i + 4) // 4):
                            cnt = min(4, i + 1 - 4 * n)
                            fill(f, p_t[:, 4 * n:4 * n + cnt, :], cnt)
                            f += 1
                        if i:
                            square(h, i - 1)
                    square(h, NCH - 1)
                    split_mix_hi(act, 4 + h, 2 * h)

                    for c in range(NCH):
                        u = NCH * h + c
                        r = NCH * h + c
                        act.wait_ge(m_negg, h + 1)
                        if u > 1:
                            act.wait_ge(m_p, u - 1)
                        act.activation(d_t[:, c % 2, :], neg_g[:, c, :], ACT.Exp, bias=rows_t[:, Q_A, r:r + 1]).then_inc(m_d, 1)
                        act.wait_ge(tr_full, f + 1)
                        if u > 1:
                            act.wait_ge(m_cu, u - 1)
                        src = ps[:, BT + f % 2, 0:2 * P].rearrange("p (c k) -> p c k", c=2)
                        act.activation(k_w[:, c % 2, :], src[:, 0, :], ACT.Copy, scale=rows_t[:, Q_WEND, r:r + 1]).then_inc(m_prep, 1)
                        act.activation(v_1[:, c % 2, 0:DH], src[:, 1, :], ACT.Copy).then_inc(tr_free, 1)
                        f += 1
                        if c:
                            act.wait_ge(m_num, u + 1)
                            act.wait_ge(m_numv, u)
                            act.activation(inter_v[:, c % 2, :], ps[:, 2 + c % 2, 256:256 + PV1], ACT.Copy,
                                           scale=rows_t[:, Q_INTER, r:r + 1]).then_inc(m_tmp, 1)
                    if h:
                        act.wait_ge(m_state, 32 * h)
                    act.wait_ge(tr_full, f + 1)
                    act.activation(c_out[:], ps[:, BT + f % 2, 0:P], ACT.Copy).then_inc(tr_free, 1)
                    act.wait_ge(m_den, 5 * h + 4)
                    act.wait_ge(a_sq, NCH * (h + 1))
                    if h:
                        act.wait_ge(m_sqs, NCH * h)
                    for c in range(NCH):
                        act.activation(sqj[:, c, :], mix[:, c, 0:DH], ACT.Square, accum_out=ssq[:, 2, c:c + 1]).then_inc(m_sqs, 1)
                    split_mix_hi(act, h, 2 * h + 1)

            @block.vector
            def _(dve):
                dve.memset(v_1[:, :, DH:PV1], 1.0).then_inc(s_ones1, 1)
                dve.wait_ge(s_rowt, 1)
                dve.tensor_scalar(rows_t[:, Q_WEND, :], rows_t[:, Q_WEND, :], SCALE_M, None, ALU.mult).then_inc(s_rowt, 1)

                def normed_rows(row, n, gain, gate):
                    for hf in range(2):
                        m = 2 * n + hf
                        sl = slice(512 * hf, 512 * hf + 512)
                        dve.wait_ge(o_tr, m + 1)
                        if m >= 2:
                            dve.wait_ge(o_lo, m - 1)
                        if gate is None:
                            dve.tensor_scalar(cols[:, sl], ps[:, BF, :], gain, None, ALU.mult).then_inc(o_cols, 1)
                        else:
                            dve.scalar_tensor_tensor(out=cols[:, sl], in0=ps[:, BF, :], scalar=gain, in1=gate[:, sl],
                                                     op0=ALU.mult, op1=ALU.mult).then_inc(o_cols, 1)
                        dve.wait_ge(o_hi, m + 1)
                        dve.tensor_tensor(acts_lo[:, row, sl], cols[:, sl], acts_hi[:, row, sl].bitcast(F32),
                                          ALU.subtract).then_inc(o_lo, 1)

                for h in range(H):
                    for i in range(NCH):
                        u = NCH * h + i
                        keys = (i + 1) * P
                        sc = ps[:, BS:BS + 4, :].rearrange("p (m b) n -> p m (b n)", m=2)
                        diag = sc[:, :, i * P:keys]
                        dve.wait_ge(a_scores, u + 1)
                        dve.tensor_tensor(diag, diag, mask_q[:].unsqueeze(1).broadcast_to((P, 2, P)), ALU.add).then_inc(a_max_, 1)
                        dve.wait_ge(a_max_, 3 * u + 1)
                        dve.tensor_reduce(stat[:, i % 2, 4:6], sc[:, :, 0:keys], AX_X, ALU.max).then_inc(a_max_, 1)
                        dve.wait_ge(a_max_, 3 * u + 2)
                        dve.tensor_scalar(stat[:, i % 2, 4:6], stat[:, i % 2, 4:6], -SCALE_D, None, ALU.mult).then_inc(a_max_, 1)
                        dve.wait_ge(a_exp, 2 * u + 2)
                        dve.reciprocal(stat[:, i % 2, 2:4], stat[:, i % 2, 0:2]).then_inc(a_coef, 1)
                        dve.wait_ge(a_coef, 2 * u + 1)
                        dve.scalar_tensor_tensor(out=stat[:, i % 2, 6:7], in0=stat[:, i % 2, 3:4], scalar=neg_lam[:],
                                                 in1=stat[:, i % 2, 0:1], op0=ALU.mult, op1=ALU.mult).then_inc(a_coef, 1)
                        dve.wait_ge(a_coef, 2 * u + 2)
                        dve.scalar_tensor_tensor(out=E_[:, 0, 0:keys], in0=E_[:, 1, 0:keys], scalar=stat[:, i % 2, 6:7],
                                                 in1=E_[:, 0, 0:keys], op0=ALU.mult, op1=ALU.add).then_inc(a_diff, 1)
                        if i:
                            out_rows(dve, h, i - 1)
                    out_rows(dve, h, NCH - 1)
                    dve.wait_ge(a_sq, NCH * (h + 1))
                    dve.tensor_scalar(ssq[:, 0, :], ssq[:, 0, :], 1.0 / DH, EPS, ALU.mult, ALU.add).then_inc(a_out, 1)
                    dve.wait_ge(o_rstd, 2 * h + 1)
                    dve.tensor_tensor(mix[:, :, 0:DH], mix[:, :, 0:DH], ssq[:, 1, :].unsqueeze(2).broadcast_to((P, NCH, DH)),
                                      ALU.mult).then_inc(o_norm, 1)
                    normed_rows(4 + h, 2 * h, vec_t[:, 4 + h, 2:3], None)

                    dve.wait_ge(m_loaded, 80 * (h + 1))
                    dve.tensor_tensor(neg_g[:], mask_s[:].unsqueeze(1).broadcast_to((P, NCH, P)), neg_g[:],
                                      ALU.subtract).then_inc(m_negg, 1)

                    def weights(c):
                        u = NCH * h + c
                        dve.wait_ge(m_d, u + 1)
                        dve.wait_ge(m_s, u + 1)
                        if u > 1:
                            dve.wait_ge(m_num, u - 1)
                        dve.scalar_tensor_tensor(out=w_t[:, c % 2, :], in0=ps[:, c % 2, 0:P], scalar=SCALE_M,
                                                 in1=d_t[:, c % 2, :], op0=ALU.mult, op1=ALU.mult).then_inc(m_p, 1)

                    weights(0)
                    for c in range(NCH):
                        u = NCH * h + c
                        if c + 1 < NCH:
                            weights(c + 1)
                        dve.wait_ge(m_cu, u + 1)
                        if c == 0:
                            if h:
                                dve.wait_ge(m_state, 32 * h)
                            dve.tensor_copy(c_st[:, 1, :], ps[:, BO, 0:PV1]).then_inc(m_c, 1)
                            dve.tensor_copy(mix[:, c, :], ps[:, 2 + c % 2, 0:PV1]).then_inc(m_numv, 1)
                        else:
                            dve.wait_ge(m_c, u)
                            dve.scalar_tensor_tensor(out=c_st[:, (c + 1) % 2, :], in0=c_st[:, c % 2, :],
                                                     scalar=decay_p[:, u:u + 1], in1=ps[:, BO, 0:PV1],
                                                     op0=ALU.mult, op1=ALU.add).then_inc(m_c, 1)
                            dve.wait_ge(m_tmp, (NCH - 1) * h + c)
                            dve.tensor_tensor(mix[:, c, :], ps[:, 2 + c % 2, 0:PV1], inter_v[:, c % 2, :], ALU.add).then_inc(m_numv, 1)
                    dve.wait_ge(m_numv, NCH * (h + 1))
                    den = ssq[:, 3, :]
                    q = 5 * h
                    dve.scalar_tensor_tensor(out=den, in0=mix[:, :, DH], scalar=-1.0, in1=mix[:, :, DH],
                                             op0=ALU.mult, op1=ALU.max).then_inc(m_den, 1)
                    dve.wait_ge(m_den, q + 1)
                    dve.tensor_tensor(den, den, rows_t[:, Q_EMT, NCH * h:NCH * (h + 1)], ALU.max).then_inc(m_den, 1)
                    dve.wait_ge(m_den, q + 2)
                    dve.reciprocal(den, den).then_inc(m_den, 1)
                    dve.wait_ge(m_den, q + 3)
                    dve.tensor_tensor(mix[:, :, 0:DH], mix[:, :, 0:DH], den.unsqueeze(2).broadcast_to((P, NCH, DH)),
                                      ALU.mult).then_inc(m_den, 1)
                    dve.wait_ge(m_den, q + 4)
                    dve.wait_ge(m_sqs, NCH * (h + 1))
                    dve.tensor_scalar(ssq[:, 2, :], ssq[:, 2, :], 1.0 / DH, EPS, ALU.mult, ALU.add).then_inc(m_den, 1)
                    dve.wait_ge(o_rstd, 2 * h + 2)
                    dve.tensor_tensor(mix[:, :, 0:DH], mix[:, :, 0:DH], ssq[:, 3, :].unsqueeze(2).broadcast_to((P, NCH, DH)),
                                      ALU.mult).then_inc(o_norm, 1)
                    normed_rows(h, 2 * h + 1, vec_t[:, h, 2:3], mo)

            @block.tensor
            def _(pe):
                pe.wait_ge(s_rowl, 32)
                for q in range(5):
                    tr = pe.transpose(ps[:, BF, q * 32:(q + 1) * 32], row_in[:, q, :], ident[0:32, 0:32])
                tr.then_inc(s_rowp, 1)
                pe.wait_ge(s_rowt, 1)

                def fill(f, blocks):
                    if f >= 2:
                        pe.wait_ge(tr_free, f - 1)
                    for n, b in enumerate(blocks):
                        tr = pe.transpose(ps[:, BT + f % 2, n * P:(n + 1) * P], b, ident[:])
                    tr.then_inc(tr_full, 1)

                def out_tr(n):
                    pe.wait_ge(o_norm, n + 1)
                    for hf in range(2):
                        if 2 * n + hf:
                            pe.wait_ge(o_cols, 2 * n + hf)
                        for c in range(4):
                            tr = pe.transpose(ps[:, BF, c * P:(c + 1) * P], mix[:, 4 * hf + c, 0:DH], ident[:])
                        tr.then_inc(o_tr, 1)

                for h in range(H):
                    f = FILLS * h
                    pe.wait_ge(d_loaded, 48 * (h + 1))
                    for src in (zv, zk):
                        for n in range(2):
                            fill(f, [src[:, (4 * n + c) * P:(4 * n + c + 1) * P] for c in range(4)])
                            f += 1

                    def scores(i):
                        u = NCH * h + i
                        if i:
                            pe.wait_ge(a_exp, 2 * u)
                        elif h:
                            pe.wait_ge(m_p, NCH * h)
                            pe.wait_ge(m_numv, NCH * h)
                        keys = (i + 1) * P
                        for k0 in range(0, keys, 512):
                            k1 = min(keys, k0 + 512)
                            for m in range(2):
                                mm = pe.matmul(ps[:, BS + 2 * m + k0 // 512, 0:k1 - k0],
                                               zq[m * DQK:(m + 1) * DQK, i * P:(i + 1) * P],
                                               zk[m * DQK:(m + 1) * DQK, k0:k1], start=True, stop=True)
                        mm.then_inc(a_scores, 1)

                    scores(0)
                    for i in range(NCH):
                        u = NCH * h + i
                        if i + 1 < NCH:
                            scores(i + 1)
                        pe.wait_ge(a_diff, u + 1)
                        for n in range((i + 4) // 4):
                            fill(f, [E_[:, 0, c * P:(c + 1) * P] for c in range(4 * n, min(4 * n + 4, i + 1))])
                            f += 1
                        pe.wait_ge(tr_free, f)
                        if i:
                            pe.wait_ge(a_out, (NCH + 1) * h + i)
                        elif h:
                            pe.wait_ge(m_c, NCH * h)
                        for c in range(i + 1):
                            mm = pe.matmul(ps[:, BO, 0:DH], p_t[:, c, :], v_tok[:, c, :], start=(c == 0), stop=(c == i))
                        mm.then_inc(a_pv, 1)
                    out_tr(2 * h)

                    pe.wait_ge(m_loaded, 80 * (h + 1))

                    def prepare(c, f):
                        u = NCH * h + c
                        fill(f, [mk[:, c * P:(c + 1) * P], mv[:, c * P:(c + 1) * P]])
                        if c == 0:
                            pe.wait_ge(a_exp, 2 * NCH * (h + 1))
                        if u > 1:
                            pe.wait_ge(m_p, u - 1)
                        pe.matmul(ps[:, c % 2, 0:P], mk[:, c * P:(c + 1) * P], mq[:, c * P:(c + 1) * P],
                                  start=True, stop=True).then_inc(m_s, 1)

                    prepare(0, f)
                    for c in range(NCH):
                        u = NCH * h + c
                        if c + 1 < NCH:
                            prepare(c + 1, f + 1)
                        f += 1
                        pe.wait_ge(tr_free, f)
                        pe.wait_ge(m_p, u + 1)
                        if u == 0:
                            pe.wait_ge(s_ones1, 1)
                        if u >= 2:
                            pe.wait_ge(m_numv, u - 1)
                        if c == 0:
                            pe.wait_ge(a_out, (NCH + 1) * h + NCH)
                        num = pe.matmul(ps[:, 2 + c % 2, 0:PV1], w_t[:, c % 2, :], v_1[:, c % 2, :], start=True, stop=True)
                        if c:
                            pe.wait_ge(m_c, u)
                            num = pe.matmul(ps[:, 2 + c % 2, 256:256 + PV1], mq[:, c * P:(c + 1) * P], c_st[:, c % 2, :],
                                            start=True, stop=True)
                        num.then_inc(m_num, 1)
                        pe.matmul(ps[:, BO, 0:PV1], k_w[:, c % 2, :], v_1[:, c % 2, :], start=True, stop=True).then_inc(m_cu, 1)
                    pe.wait_ge(m_c, NCH * (h + 1))
                    fill(f, [c_st[:, NCH % 2, 0:DH]])
                    f += 1
                    out_tr(2 * h + 1)


    gate_loaded = [sem("gate_m_loaded"), sem("gate_d_loaded")]
    gated = [sem("gated_m"), sem("gated_d")]
    samples_hi, samples_lo = sem("samples_hi"), sem("samples_lo")
    merged_sum = sem("merged_sum")
    merged_hi = sem("merged_hi")
    merged_lo = sem("merged_lo")
    y_evac = [sem("y_evac_act"), sem("y_evac_dve")]
    OUT0, TILE5 = PROJ0 + 4, TILE4 + 2 * KT
    OUT_CHUNKS = D_MODEL // NC_
    FFN0, TILE6 = OUT0 + OUT_CHUNKS, TILE5 + KT
    WP = CW // 4

    def banks(b):
        return ps[:, b:b + NTB, 0:TB]

    def by_bank(ap):
        return ap.rearrange("p (b t) -> p b t", b=NTB)

    def up_chunk(i, half):
        return w_cols(I["w_up"][0], half * D_FF + NC_ * i)

    y_t = nc.alloc_sbuf_tensor_at("y_t", [P, KT, T], F32, offset=acts_lo_at)
    with ExitStack() as scope:
        cur[0] = scope
        mg_hi = sb("mg_hi", [P, KT, T], F32R)
        mg_lo = sb("mg_lo", [P, KT, T], F32R)
        gate = [sb("gate_m", [P, T]), sb("gate_d", [P, T])]

        with nc.Block() as block:
            @block.sync
            def _(sp):
                def gate_load(k):
                    if k:
                        sp.wait_ge(merged_lo, k)
                    sp.dma_start(gate[0][:], ZT[Z_GM + k]).then_inc(gate_loaded[0], 16)
                    if k:
                        sp.wait_ge(merged_sum, k)
                    sp.dma_start(gate[1][:], ZT[Z_GD + k]).then_inc(gate_loaded[1], 16)

                gate_load(0)
                for g in range(2):
                    src = (I["w_proj_m"][0], I["w_proj_d"][0])[g].rearrange("(k p) n -> p k n", p=P)
                    load_chunk(sp, g, src[:, :, WP:2 * WP], W_MIX // P, PROJ0 + g + 1)
                for k in range(1, KT):
                    gate_load(k)
                    if k == 4:
                        load_chunk(sp, 0, w_cols(I["w_out"][0], 0), KT, OUT0 - 1)
                    if k == 5:
                        load_chunk(sp, 1, w_cols(I["w_out"][0], NC_), KT, OUT0)
                for c in range(2, OUT_CHUNKS):
                    load_chunk(sp, c % 2, w_cols(I["w_out"][0], c * NC_), KT, OUT0 + c - 1)
                for half in range(2):
                    load_chunk(sp, half, up_chunk(0, half), KT, FFN0 - 1 + half)

            @block.scalar
            def _(act):
                act.activation(acts_hi[:, :, SEQ:T], branch_s[:], ACT.Copy).then_inc(samples_hi, 1)
                split_hi(act, 1, loads_of(PROJ0 + 1), TILE4)
                for k in range(KT):
                    if k in (3, 7):
                        n = PROJ0 + 2 if k == 3 else OUT0
                        split_hi(act, 0, loads_of(n), TILE4 + 2 * k + 1)
                        split_hi(act, 1, loads_of(n + 1), TILE4 + 2 * k + 2)
                    act.wait_ge(merged_sum, k + 1)
                    act.activation(mg_hi[:, k, :], gate[0][:], ACT.Copy).then_inc(merged_hi, 1)
                for c in range(OUT_CHUNKS):
                    if c:
                        split_hi(act, (c + 1) % 2, loads_of(OUT0 + c + 1), TILE5 + 2 * c)
                    act.wait_ge(tile_done, TILE5 + 2 * c + 1)
                    act.activation(by_bank(y_t[:, 2 * c, :]), banks(0), ACT.Copy).then_inc(y_evac[0], 1)

            @block.vector
            def _(dve):
                dve.wait_ge(samples_hi, 1)
                dve.tensor_tensor(acts_lo[:, :, SEQ:T], branch_s[:], acts_hi[:, :, SEQ:T].bitcast(F32), ALU.subtract)\
                    .then_inc(samples_lo, 1)
                split_lo(dve, 1, PROJ0 + 2)
                for k in range(KT):
                    for g in range(2):
                        dve.wait_ge(gate_loaded[g], 16 * (k + 1))
                        dve.wait_ge(tile_done, TILE4 + 2 * k + g + 1)
                        dve.tensor_tensor(by_bank(gate[g][:]), by_bank(gate[g][:]), banks(3 * g), ALU.mult)\
                            .then_inc(gated[g], 1)
                        if g == 0 and k in (3, 7):
                            split_lo(dve, 0, PROJ0 + (3 if k == 3 else 5))
                    dve.wait_ge(gated[0], k + 1)
                    dve.wait_ge(gated[1], k + 1)
                    dve.tensor_tensor(gate[0][:], gate[0][:], gate[1][:], ALU.add).then_inc(merged_sum, 1)
                    if k in (3, 7):
                        split_lo(dve, 1, PROJ0 + (4 if k == 3 else 6))
                    dve.wait_ge(merged_hi, k + 1)
                    dve.tensor_tensor(mg_lo[:, k, :], gate[0][:], mg_hi[:, k, :].bitcast(F32), ALU.subtract)\
                        .then_inc(merged_lo, 1)
                for c in range(OUT_CHUNKS):
                    if c:
                        split_lo(dve, (c + 1) % 2, OUT0 + c + 2)
                    dve.wait_ge(tile_done, TILE5 + 2 * c + 2)
                    dve.tensor_copy(by_bank(y_t[:, 2 * c + 1, :]), banks(3)).then_inc(y_evac[1], 1)

            @block.tensor
            def _(pe):
                pe.wait_ge(samples_lo, 1)
                for k in range(KT):
                    for g in range(2):
                        pe.wait_ge(w_lo_ready, PROJ0 + 2 * (k // 4) + g + 1)
                        if k:
                            pe.wait_ge(gated[g], k)
                        gemm_tile(pe, g, W_MIX // P, WP, k % 4, acts_hi[:, 4 * g:4 * g + 4, :],
                                  acts_lo[:, 4 * g:4 * g + 4, :], 3 * g)
                for c in range(OUT_CHUNKS):
                    pe.wait_ge(w_lo_ready, OUT0 + c + 1)
                    for j in range(2):
                        if c:
                            pe.wait_ge(y_evac[j], c)
                        else:
                            pe.wait_ge(gated[j], KT)
                        gemm_tile(pe, c % 2, KT, NC_, j, mg_hi, mg_lo, 3 * j, merged_lo if c == 0 and j == 0 else None)

    def post_norm(i, y_t, x_src, dst, last_vals=None):
        nm = ("mix", "ffn")[i]
        gain_loaded = sem(f"gain_loaded_{nm}")
        xr_loaded = [sem(f"xr_loaded_{nm}{s}") for s in range(2)]
        yr_tp = sem(f"yr_tp_{nm}")
        yr_ss = sem(f"yr_ss_{nm}")
        yr_v = sem(f"yr_v_{nm}")
        yr_rstd = sem(f"yr_rstd_{nm}")
        yr_g = sem(f"yr_g_{nm}")
        yr_x = sem(f"yr_x_{nm}")
        yr_stored = [sem(f"yr_stored_{nm}{s}") for s in range(2)]
        if i == 0:
            h_ss, h_v, h_rstd = sem("h_ss"), sem("h_v"), sem("h_rstd")
            h_s, h_tp, h_t = sem("h_scaled"), sem("h_tp"), sem("h_t")
            h_aff, h_hi, h_lo = sem("h_aff"), sem("h_hi"), sem("h_lo")
        else:
            lv_tp, lv_rows, lv_st = sem("lv_tp"), sem("lv_rows"), sem("lv_stored")
        with ExitStack() as scope:
            cur[0] = scope
            gain = sb(f"gain_{nm}", [P, 2, D_MODEL])
            xr = sb(f"xr_{nm}", [P, 2, D_MODEL])
            yr = sb(f"yr_{nm}", [P, 2, D_MODEL])
            sqr = sb(f"sqr_{nm}", [P, D_MODEL], mybir.dt.bfloat16)
            stats = sb(f"stats_{nm}", [P, NTT, 6])
            if i == 0:
                hs = sb("hs", [P, 2, D_MODEL])
                x_t = sb("x1_t", [P, KT, T])
            else:
                lv = sb("last_rows", [18, D_FF])

            def halves(b, r):
                return ps[0:r, b:b + 2, :]

            def rows2(ap, r):
                return ap[0:r].rearrange("p (b n) -> p b n", b=2)

            with nc.Block() as block:
                @block.sync
                def _(sp):
                    sp.dma_start(gain[:, 0, :], GATES[i, TS:TS + 1, :].broadcast_to((P, D_MODEL))).then_inc(gain_loaded, 16)
                    sp.dma_start(gain[0:TS, 1, :], GATES[i, 0:TS, :]).then_inc(gain_loaded, 16)
                    for t in range(NTT + 1):
                        if t < NTT:
                            if t >= 2:
                                sp.wait_ge(yr_x, t - 1)
                            sp.dma_start(xr[0:tile_rows(t), t % 2, :], x_src(t)).then_inc(xr_loaded[t % 2], 16)
                        if t >= 1:
                            u = t - 1
                            sp.wait_ge(yr_x, u + 1)
                            sp.dma_start(dst(u), yr[0:tile_rows(u), u % 2, :]).then_inc(yr_stored[u % 2], 16)
                    if i == 1:
                        sp.wait_ge(lv_rows, 2)
                        sp.dma_start(O["conv_prompt"][0, 0], lv[0:2, :]).then_inc(lv_st, 16)
                        sp.dma_start(O["conv_sample"][0].rearrange("b w f -> (b w) f"), lv[2:18, :]).then_inc(lv_st, 16)
                        sp.wait_ge(lv_st, 32)
                    for s in range(2):
                        sp.wait_ge(yr_stored[s], 16 * ((NTT + 1 - s) // 2))

                @block.tensor
                def _(pe):
                    def y_rows(t):
                        r, b = tile_rows(t), 2 * (t % 2)
                        if t >= 2:
                            pe.wait_ge(yr_g, t - 1)
                        for k in range(KT):
                            tr = pe.transpose(ps[0:r, b + k // 4, k % 4 * P:(k % 4 + 1) * P],
                                              y_t[:, k, t * P:t * P + r], ident[:])
                        tr.then_inc(yr_tp, 1)

                    def h_cols(t):
                        r, b = tile_rows(t), 4 + 2 * (t % 2)
                        pe.wait_ge(h_s, t + 1)
                        if t >= 2:
                            pe.wait_ge(h_t, t - 1)
                        for k in range(KT):
                            tr = pe.transpose(ps[:, b + k // 4, k % 4 * P:k % 4 * P + r],
                                              hs[0:r, t % 2, k * P:(k + 1) * P], ident[0:r, 0:r])
                        tr.then_inc(h_tp, 1)

                    if i == 1:
                        for g in range(2):
                            if g:
                                pe.wait_ge(lv_rows, 1)
                            for f in range(16 * g, min(16 * g + 16, FT)):
                                tr = pe.transpose(ps[0:18, 4 + f % 16 // 4, f % 4 * P:(f % 4 + 1) * P], last_vals[:, f, :], ident[:])
                            tr.then_inc(lv_tp, 1)
                            if g == 0:
                                y_rows(0)
                                y_rows(1)
                    for t in range(NTT + 2):
                        if t < NTT and not (i == 1 and t < 2):
                            y_rows(t)
                        if i == 0 and t >= 2:
                            h_cols(t - 2)

                @block.scalar
                def _(act):
                    def y_square(t):
                        r = tile_rows(t)
                        act.wait_ge(yr_tp, t + 1)
                        if t:
                            act.wait_ge(yr_ss, t)
                            if i == 0 and t >= 2:
                                act.wait_ge(h_ss, t - 1)
                        act.activation(rows2(sqr[:], r), halves(2 * (t % 2), r), ACT.Square,
                                       accum_out=stats[0:r, t, 0:1]).then_inc(yr_ss, 1)

                    def h_square(t):
                        r = tile_rows(t)
                        act.wait_ge(yr_x, t + 1)
                        act.wait_ge(yr_ss, min(t + 2, NTT))
                        act.activation(sqr[0:r], yr[0:r, t % 2, :], ACT.Square, accum_out=stats[0:r, t, 3:4]).then_inc(h_ss, 1)

                    def h_scale(t):
                        r = tile_rows(t)
                        act.wait_ge(h_rstd, t + 1)
                        if t >= 2:
                            act.wait_ge(h_tp, t - 1)
                        act.activation(hs[0:r, t % 2, :], yr[0:r, t % 2, :], ACT.Copy, scale=stats[0:r, t, 5:6]).then_inc(h_s, 1)

                    def h_evac(t):
                        r = tile_rows(t)
                        act.wait_ge(h_tp, t + 1)
                        act.activation(x_t[:, :, t * P:t * P + r].rearrange("p (b k) n -> p b k n", b=2),
                                       ps[:, 4 + 2 * (t % 2):6 + 2 * (t % 2), :].rearrange("p b (k n) -> p b k n", k=4)[:, :, :, 0:r],
                                       ACT.Copy).then_inc(h_t, 1)

                    for t in range(NTT + 2):
                        if t < NTT:
                            y_square(t)
                        if i == 0:
                            if 1 <= t <= NTT:
                                h_square(t - 1)
                                h_scale(t - 1)
                            if t >= 2:
                                h_evac(t - 2)
                    if i == 0:
                        split_rows_hi(act, x_t, h_aff, h_hi)

                @block.vector
                def _(dve):
                    if i == 1:
                        for g, (f0, f1) in enumerate(((0, 16), (16, FT))):
                            dve.wait_ge(lv_tp, g + 1)
                            n = f1 - f0
                            for b in range(0, n, 4):
                                m = min(4, n - b)
                                cp = dve.tensor_copy(lv[:, (f0 + b) * P:(f0 + b + m) * P], ps[0:18, 4 + b // 4, 0:m * P])
                            cp.then_inc(lv_rows, 1)
                    dve.wait_ge(gain_loaded, 32)

                    def y_out(t):
                        r, s = tile_rows(t), t % 2
                        dve.wait_ge(yr_ss, t + 1)
                        dve.tensor_scalar(stats[0:r, t, 1:2], stats[0:r, t, 0:1], 1.0 / D_MODEL, EPS, ALU.mult, ALU.add).then_inc(yr_v, 1)
                        dve.wait_ge(yr_rstd, t + 1)
                        if t >= 2:
                            dve.wait_ge(yr_stored[s], 16 * (t // 2))
                            if i == 0:
                                dve.wait_ge(h_s, t - 1)
                        dve.scalar_tensor_tensor(out=rows2(yr[:, s, :], r), in0=halves(2 * s, r), scalar=stats[0:r, t, 2:3],
                                                 in1=rows2(gain[:, t // NCH, :], r), op0=ALU.mult, op1=ALU.mult).then_inc(yr_g, 1)
                        dve.wait_ge(xr_loaded[s], 16 * (t // 2 + 1))
                        dve.wait_ge(yr_g, t + 1)
                        dve.tensor_tensor(yr[0:r, s, :], yr[0:r, s, :], xr[0:r, s, :], ALU.add).then_inc(yr_x, 1)

                    def h_stat(t):
                        r = tile_rows(t)
                        dve.wait_ge(h_ss, t + 1)
                        dve.tensor_scalar(stats[0:r, t, 4:5], stats[0:r, t, 3:4], 1.0 / D_MODEL, EPS, ALU.mult, ALU.add).then_inc(h_v, 1)

                    for t in range(NTT + 1):
                        if i == 0 and t >= 1:
                            h_stat(t - 1)
                        if t < NTT:
                            y_out(t)
                    if i == 0:
                        dve.wait_ge(h_t, NTT)
                        affine_rows(dve, x_t, 1, h_aff)
                        split_rows_lo(dve, x_t, h_hi, h_lo)

                @block.gpsimd
                def _(pool):
                    for t in range(NTT + 1):
                        if t < NTT:
                            r = tile_rows(t)
                            pool.wait_ge(yr_v, t + 1)
                            pool.tensor_tensor(stats[0:r, t, 2:3], stats[0:r, t, 1:2], minus_half[0:r, 0:1], ALU.pow).then_inc(yr_rstd, 1)
                        if i == 0 and t >= 1:
                            r = tile_rows(t - 1)
                            pool.wait_ge(h_v, t)
                            pool.tensor_tensor(stats[0:r, t - 1, 5:6], stats[0:r, t - 1, 4:5], minus_half[0:r, 0:1], ALU.pow).then_inc(h_rstd, 1)

    def x_rows(t):
        return I["x_prompt"][0, t * P:(t + 1) * P, :] if t < NCH else I["x_sample"].rearrange("b t d -> (b t) d")

    def x1_rows(t):
        return X1[t * P:t * P + tile_rows(t), :]

    def y_out_rows(t):
        return O["y_prompt"][0, t * P:(t + 1) * P, :] if t < NCH else O["y_sample"].rearrange("b t d -> (b t) d")

    post_norm(0, y_t, x_rows, x1_rows)

    NPAIR = FT // 2
    a_evac = sem("a_evac")
    a_state = sem("a_state")
    a_kept = sem("a_kept")
    f_conv = sem("f_conv")
    f_gelu = sem("f_gelu")
    f_mul = sem("f_mul")
    g_hi_s, g_lo_s = sem("g_hi"), sem("g_lo")
    f_add = sem("f_add")
    TAIL = CONV_W - 1
    AX = TAIL + SEQ + DEC_B * (TAIL + DEC_T)
    with ExitStack() as outer:
        cur[0] = outer
        f_t = sb("f_t", [P, KT, T])
        last_vals = sb("last_vals", [P, FT, TAIL * (1 + DEC_B)])
        with ExitStack() as scope:
            cur[0] = scope
            a_ext = [sb(f"a_ext{j}", [P, AX]) for j in range(2)]
            conv = [sb(f"conv{j}", [P, AX]) for j in range(2)]
            g_hi = sb("g_hi_t", [P, 2, T], F32R)
            g_lo = sb("g_lo_t", [P, 2, T], F32R)

            def seqs(ap):
                return ap[:, TAIL + SEQ:AX].rearrange("p (b w) -> p b w", b=DEC_B)

            EDGE = SEQ - 2 * TB

            def parts(buf, b):
                return [(buf[:, TAIL:TAIL + 2 * TB].rearrange("p (b t) -> p b t", b=2), ps[:, b:b + 2, 0:TB]),
                        (buf[:, TAIL + 2 * TB:TAIL + SEQ], ps[:, b + 2, 0:EDGE]),
                        (seqs(buf)[:, :, TAIL:], ps[:, b + 2, EDGE:TB].rearrange("p (b t) -> p b t", b=DEC_B))]

            def tiles_at(i):
                return TILE6 + 4 + 12 * (i - 1)

            with nc.Block() as block:
                @block.sync
                def _(sp):
                    def down(i):
                        return I["w_down"][0].rearrange("(k p) n -> p k n", p=P)[:, bass.ds(2 * i, 2), :]

                    with sp.Fori(0, 2 * (NPAIR // 2) - 1, 2) as m:
                        for q in range(2):
                            i = m + 1 + q
                            n = FFN0 + 3 * m + 3 * q + 2
                            load_chunk(sp, q % 2, up_chunk(i, 0), KT, n - 1)
                            load_chunk(sp, (q + 1) % 2, down(i - 1), 2, n)
                            load_chunk(sp, q % 2, up_chunk(i, 1), KT, n + 1)
                    load_chunk(sp, 0, down(NPAIR - 1), 2, FFN0 + 3 * NPAIR - 2)

                @block.gpsimd
                def _(pool):
                    for j in range(2):
                        pool.memset(a_ext[j][:, 0:TAIL], 0.0).then_inc(a_state, 1)
                    for k in range(KT):
                        pool.memset(f_t[:, k, :], 0.0).then_inc(f_add, 1)

                    def pair(i, first):
                        for j in range(2):
                            f = 2 * i + j
                            n = 2 * i + j
                            if not first:
                                pool.wait_ge(f_conv, 3 * (n - 1))
                            pool.tensor_copy(seqs(a_ext[j])[:, :, 0:TAIL],
                                             ff_t[:, bass.ds(f, 1), 0:16].rearrange("p f (b w) -> p (f b) w", b=DEC_B))\
                                .then_inc(a_state, 1)
                        for j in range(2):
                            n = 2 * i + j
                            pool.wait_ge(a_evac, 3 * n + 3)
                            keep = last_vals[:, bass.ds(2 * i + j, 1), :].rearrange("p f n -> p (f n)")
                            pool.tensor_copy(keep[:, 0:TAIL], a_ext[j][:, SEQ:SEQ + TAIL]).then_inc(a_kept, 1)
                            pool.tensor_copy(keep[:, TAIL:].rearrange("p (b w) -> p b w", b=DEC_B),
                                             seqs(a_ext[j])[:, :, DEC_T:DEC_T + TAIL]).then_inc(a_kept, 1)

                    pair(0, True)
                    with pool.Fori(0, 2 * (NPAIR // 2) - 1, 2) as m:
                        for q in range(2):
                            pair(m + 1 + q, False)

                def conv_weight(f, j):
                    return ff_t[:, bass.ds(f, 1), 16 + j:17 + j].rearrange("p f n -> p (f n)")

                @block.scalar
                def _(act):
                    def a_tile(i, j, tile, first):
                        act.wait_ge(tile_done, tile)
                        if not first:
                            act.wait_ge(f_conv, 3 * (2 * i + j) - 3)
                            act.wait_ge(a_kept, 2 * (2 * i + j) - 2)
                        for dst, src in parts(a_ext[j], 3 * j):
                            act.activation(dst, src, ACT.Copy).then_inc(a_evac, 1)

                    def gelu(i, j):
                        act.wait_ge(f_conv, 3 * (2 * i + j) + 3)
                        act.activation(conv[j][:, TAIL:AX], conv[j][:, TAIL:AX], ACT.Gelu_apprx_tanh).then_inc(f_gelu, 1)

                    def g_up(i, j, tiles):
                        act.wait_ge(f_mul, 3 * (2 * i + j) + 3)
                        if tiles is not None:
                            act.wait_ge(tile_done, tiles)
                        act.activation(g_hi[:, j, 0:SEQ], conv[j][:, TAIL:TAIL + SEQ], ACT.Copy).then_inc(g_hi_s, 1)
                        act.activation(g_hi[:, j, SEQ:T].rearrange("p (b t) -> p b t", b=DEC_B), seqs(conv[j])[:, :, TAIL:],
                                       ACT.Copy).then_inc(g_hi_s, 1)

                    a_tile(0, 0, TILE6 + 1, True)
                    split_hi(act, 1, loads_of(FFN0 + 1), TILE6)
                    gelu(0, 0)
                    a_tile(0, 1, TILE6 + 2, True)
                    split_hi(act, 0, loads_of(FFN0 + 2), TILE6 + 2)
                    gelu(0, 1)
                    g_up(0, 0, None)
                    g_up(0, 1, None)

                    def pair(i, q, loads, last):
                        t0 = tiles_at(i)
                        split_hi(act, (q + 1) % 2, loads[0], t0)
                        a_tile(i, 0, t0 + 1, False)
                        gelu(i, 0)
                        a_tile(i, 1, t0 + 2, False)
                        split_hi(act, q % 2, loads[1], t0 + 2)
                        gelu(i, 1)
                        split_hi(act, (q + 1) % 2, loads[2], t0 + 10)
                        g_up(i, 0, t0 + 10)
                        g_up(i, 1, None)

                    with act.Fori(0, 2 * (NPAIR // 2) - 1, 2) as m:
                        for q in range(2):
                            loads = [24 * m + 16 * ((FFN0 + 3 * q + d) // 2 + 1) for d in (3, 4, 5)]
                            pair(m + 1 + q, q, loads, False)

                @block.vector
                def _(dve):
                    def conv_op(i, j, w):
                        n = 2 * i + j
                        if w == 0:
                            dve.wait_ge(a_evac, 3 * n + 3)
                            dve.wait_ge(a_state, n + 3)
                            if not (isinstance(i, int) and i == 0):
                                dve.wait_ge(g_hi_s, 4 * i - 2 + 2 * j)
                                dve.wait_ge(g_lo_s, 4 * i - 2 + 2 * j)
                        out = conv[j][:, TAIL:AX]
                        src = a_ext[j][:, w:AX - TAIL + w]
                        f = 2 * i + j
                        if w == 0:
                            ins_ = dve.tensor_scalar(out, src, conv_weight(f, 0), conv_weight(f, CONV_W), ALU.mult, ALU.add)
                        else:
                            dve.wait_ge(f_conv, 3 * n + w)
                            ins_ = dve.scalar_tensor_tensor(out=out, in0=src, scalar=conv_weight(f, w), in1=out,
                                                            op0=ALU.mult, op1=ALU.add)
                        ins_.then_inc(f_conv, 1)

                    def mul_b(i, j, tile):
                        dve.wait_ge(tile_done, tile)
                        dve.wait_ge(f_gelu, 2 * i + j + 1)
                        for dst, src in parts(conv[j], 3 * j):
                            dve.tensor_tensor(dst, dst, src, ALU.mult).then_inc(f_mul, 1)

                    def g_low(i, j):
                        n = 2 * i + j
                        dve.wait_ge(g_hi_s, 2 * n + 1)
                        dve.tensor_tensor(g_lo[:, j, 0:SEQ], conv[j][:, TAIL:TAIL + SEQ], g_hi[:, j, 0:SEQ].bitcast(F32),
                                          ALU.subtract).then_inc(g_lo_s, 1)
                        dve.wait_ge(g_hi_s, 2 * n + 2)
                        dve.tensor_tensor(g_lo[:, j, SEQ:T].rearrange("p (b t) -> p b t", b=DEC_B), seqs(conv[j])[:, :, TAIL:],
                                          g_hi[:, j, SEQ:T].rearrange("p (b t) -> p b t", b=DEC_B).bitcast(F32),
                                          ALU.subtract).then_inc(g_lo_s, 1)

                    def add_down(k, tile, adds):
                        dve.wait_ge(tile_done, tile)
                        dve.wait_ge(f_add, adds)
                        dve.tensor_tensor(by_bank(f_t[:, k, :]), by_bank(f_t[:, k, :]), banks(3 * (k % 2)), ALU.add)\
                            .then_inc(f_add, 1)

                    split_lo(dve, 1, FFN0 + 2)
                    for w in range(CONV_W):
                        conv_op(0, 0, w)
                    for w in range(CONV_W):
                        conv_op(0, 1, w)
                    split_lo(dve, 0, FFN0 + 3)
                    for j in range(2):
                        mul_b(0, j, TILE6 + 3 + j)
                    for j in range(2):
                        g_low(0, j)
                    dve.wait_ge(f_add, KT)

                    def pair(i, q, n):
                        t0 = tiles_at(i)
                        split_lo(dve, (q + 1) % 2, n)
                        for w in range(CONV_W):
                            conv_op(i, 0, w)
                        for k in range(KT):
                            add_down(k, t0 + 3 + k, KT * (i - 1) + k + 1)
                            if k < CONV_W:
                                conv_op(i, 1, k)
                            if k == CONV_W:
                                split_lo(dve, q % 2, n + 1)
                        split_lo(dve, (q + 1) % 2, n + 2)
                        for j in range(2):
                            mul_b(i, j, t0 + 11 + j)
                            g_low(i, j)

                    with dve.Fori(0, 2 * (NPAIR // 2) - 1, 2) as m:
                        for q in range(2):
                            pair(m + 1 + q, q, FFN0 + 3 * m + 3 * q + 4)
                    for k in range(KT):
                        add_down(k, tiles_at(NPAIR) + k + 1, KT * (NPAIR - 1) + k + 1)

                @block.tensor
                def _(pe):
                    def down(i, slot, left, counts):
                        pe.wait_ge(g_lo_s, 4 * i + 4)
                        for k in range(KT):
                            if k < 2:
                                pe.wait_ge(left, counts[k])
                            else:
                                pe.wait_ge(f_add, KT * (i + 1) + k - 1)
                            gemm_tile(pe, slot, 2, D_MODEL, k, g_hi, g_lo, 3 * (k % 2))

                    def pair(i, q, n):
                        pe.wait_ge(w_lo_ready, n + 1)
                        for j in range(2):
                            pe.wait_ge(f_mul, 6 * i - 3 + 3 * j)
                            gemm_tile(pe, q % 2, KT, NC_, j, acts_hi, acts_lo, 3 * j)
                        pe.wait_ge(w_lo_ready, n + 2)
                        down(i - 1, (q + 1) % 2, a_evac, (6 * i + 3, 6 * i + 6))
                        pe.wait_ge(w_lo_ready, n + 3)
                        for j in range(2):
                            pe.wait_ge(f_add, KT * (i + 1) - 1 + j)
                            gemm_tile(pe, q % 2, KT, NC_, j, acts_hi, acts_lo, 3 * j)

                    for h in range(2):
                        pe.wait_ge(w_lo_ready, FFN0 + h + 1)
                        for j in range(2):
                            if h:
                                pe.wait_ge(a_evac, 3 * j + 3)
                            gemm_tile(pe, h, KT, NC_, j, acts_hi, acts_lo, 3 * j)
                    with pe.Fori(0, 2 * (NPAIR // 2) - 1, 2) as m:
                        for q in range(2):
                            pair(m + 1 + q, q, FFN0 + 3 * m + 3 * q + 2)
                    pe.wait_ge(w_lo_ready, FFN0 + 3 * NPAIR)
                    down(NPAIR - 1, 0, f_mul, (6 * NPAIR - 3, 6 * NPAIR))

        post_norm(1, f_t, x1_rows, y_out_rows, last_vals)
    base.close()


_OUTS = [
    ("y_prompt", (1, SEQ, D_MODEL)), ("y_sample", (DEC_B, DEC_T, D_MODEL)),
    ("k_prompt", (1, 1, SEQ, H, 2 * DQK)), ("v_prompt", (1, 1, SEQ, H, DH)),
    ("C_prompt", (1, 1, H, DH, DH)), ("n_prompt", (1, 1, H, DH)), ("m_prompt", (1, 1, H)),
    ("conv_prompt", (1, 1, CONV_W - 1, D_FF)),
    ("k_sample", (1, DEC_B, DEC_T, H, 2 * DQK)), ("v_sample", (1, DEC_B, DEC_T, H, DH)),
    ("C_sample", (1, DEC_B, H, DH, DH)), ("n_sample", (1, DEC_B, H, DH)), ("m_sample", (1, DEC_B, H)),
    ("conv_sample", (1, DEC_B, CONV_W - 1, D_FF)),
]


def kernel(**inputs):
    import numpy as _np
    import concourse.bacc as _bacc
    from concourse import mybir as _mybir
    from concourse.bass_utils import run_bass_kernel_spmd as _run

    nc = _bacc.Bacc("TRN2", target_bir_lowering=False, num_devices=1)
    arrays, ins, outs = {}, {}, {}
    for name, a in inputs.items():
        a = _np.ascontiguousarray(a)
        arrays[f"in_{name}"] = a
        ins[name] = nc.dram_tensor(f"in_{name}", a.shape, _mybir.dt.from_np(a.dtype), kind="ExternalInput").ap()
    for name, shape in _OUTS:
        outs[name] = nc.dram_tensor(f"out_{name}", shape, F32, kind="ExternalOutput").ap()
    build(nc, ins, outs)
    r = _run(nc, [arrays], core_ids=[0])
    return tuple(r.results[0][f"out_{name}"] for name, _ in _OUTS)
```

```python
import math
from contextlib import ExitStack

import concourse.bass as bass
from concourse import mybir
from concourse.alu_op_type import AluOpType as ALU

ACT = mybir.ActivationFunctionType
F32 = mybir.dt.float32
F32R = mybir.dt.float32r
I32 = mybir.dt.int32
AX_X = mybir.AxisListType.X

P = 128
D_MODEL, SEQ, DEC_B, DEC_T, PAST, PAGE = 1024, 1024, 8, 4, 256, 128
H, DH, DQK, D_FF, CONV_W = 4, 128, 64, 2816, 3
W_MIX = H * DH
D_IN = 4 * W_MIX + 2 * H + 3 * W_MIX + 2 * D_MODEL
EPS = 1e-6
LAM_INIT = 0.8 - 0.6 * math.exp(0.0)
NEG = -1e30
TS = DEC_B * DEC_T
T = SEQ + TS
NTB, TB = 3, T // 3
KT = D_MODEL // P
NCH = SEQ // P
NTT = NCH + 1
FT = D_FF // P
NPG = PAST // PAGE
CW = 2048
NC_ = 256
ADA_CHUNKS = 6 * D_MODEL // NC_
TOK_C = TS + 1
Z_MQ, Z_MK, Z_MV, Z_DQ, Z_DK, Z_DV, Z_MO, Z_GM, Z_GD = 0, 4, 8, 12, 16, 20, 24, 28, 36
Z_TILES = 44
D_COL = 4 * W_MIX + 2 * H
IF_COL = 4 * W_MIX
VECS = ("b_ada", "g_pre_mix", "g_pre_ffn", "g_post_mix", "g_post_ffn", "g_mlstm", "g_diff")
V_PRE, V_POST, V_BR = 6 * KT, 8 * KT, 10 * KT
NVEC = V_BR + 2 * H
M_CHUNKS = 4 * W_MIX // NC_
GATE_CHUNKS, GATE_COL = 8, 7 * W_MIX + 2 * H
Q_A, Q_G, Q_INTER, Q_EMT, Q_WEND = range(5)


def build(nc, ins, outs):
    I, O = ins, outs
    base = ExitStack()
    cur = [base]
    base.enter_context(nc.allow_non_contiguous_dma(reason="a few columns of 32 to 1024 elements"))

    def sb(name, shape, dt=F32):
        return cur[0].enter_context(nc.sbuf_tensor(name, shape, dt))

    def sem(name):
        return base.enter_context(nc.semaphore(name))

    def scratch(name, shape):
        return nc.dram_tensor(name, shape, F32).ap()

    ZT = scratch("z_scratch", (Z_TILES, P, T))
    GATES = scratch("gate_scratch", (2, TOK_C, D_MODEL))
    GIFP = scratch("if_scratch", (2, H, SEQ))
    GIFD = scratch("ifd_scratch", (2, H, TS))
    ROWS = scratch("rows_scratch", (5, H, SEQ))
    BRANCH = scratch("branch_scratch", (H, P, SEQ))
    ROWD = scratch("rowd_scratch", (5, H, TS))
    ENDS = scratch("ends_scratch", (4, H * NCH))
    DECD = scratch("decd_scratch", (1, H * DEC_B))
    X1 = scratch("x1_scratch", (T, D_MODEL))

    ps = base.enter_context(nc.psum_tensor("ps", [P, 8, 512], F32))
    w_raw = sb("w_raw", [P, 2, CW])
    w_hi = sb("w_hi", [P, 2, CW], F32R)
    w_lo = sb("w_lo", [P, 2, CW], F32R)
    ident = sb("ident", [P, P])
    mask_q = sb("mask_q", [P, P])
    mask_s = sb("mask_s", [P, P])
    mask_n = sb("mask_n", [TS, TS])
    ones = sb("ones", [P, P])
    ada_t = sb("ada_t", [P, 4, KT, TOK_C])
    gain_t = sb("gain_t", [P, 2 * H])
    ff_t = sb("ff_t", [P, FT, 20])
    neg_lam = sb("neg_lam", [P, 1])
    minus_half = sb("minus_half", [P, NTT])
    same_seq = sb("same_seq", [TS, DEC_B])
    rows_t = sb("rows_t", [P, 5, H * NCH])
    decay_p = sb("decay_p", [P, H * NCH])
    branch_s = sb("branch_s", [P, KT, TS])
    acts_hi = sb("acts_hi", [P, KT, T], F32R)
    acts_lo_at = nc.sbuf_base
    acts_lo = sb("acts_lo", [P, KT, T], F32R)

    w_loaded = [sem("w_loaded0"), sem("w_loaded1")]
    w_hi_ready = sem("w_hi_ready")
    w_lo_ready = sem("w_lo_ready")
    tile_done = sem("tile_done")

    class Steps:

        def __init__(self, name, names):
            self.sem, self.at = sem(name), {n: i + 1 for i, n in enumerate(names)}
            self.next = 1
            assert len(self.at) == len(names)

        def done(self, ins_, name):
            assert self.at[name] == self.next, name
            self.next += 1
            ins_.then_inc(self.sem, 1)

        def wait(self, engine, name):
            engine.wait_ge(self.sem, self.at[name])

    def load_chunk(sp, slot, src, kt, split_before=None):
        if split_before is not None:
            sp.wait_ge(w_lo_ready, split_before)
        sp.dma_start(w_raw[:, slot, :].rearrange("p (k n) -> p k n", k=kt), src).then_inc(w_loaded[slot], 16)

    def split_hi(act, slot, loads, tiles_before=None):
        act.wait_ge(w_loaded[slot], loads)
        if tiles_before is not None:
            act.wait_ge(tile_done, tiles_before)
        act.activation(w_hi[:, slot, :], w_raw[:, slot, :], ACT.Copy).then_inc(w_hi_ready, 1)

    def split_lo(dve, slot, chunks):
        dve.wait_ge(w_hi_ready, chunks)
        dve.tensor_tensor(w_lo[:, slot, :], w_raw[:, slot, :], w_hi[:, slot, :].bitcast(F32),
                          ALU.subtract).then_inc(w_lo_ready, 1)

    def products(kt):
        return [(k, w, a) for k in range(kt) for w, a in ((0, 0), (0, 1), (1, 0))]

    def gemm_tile(pe, slot, kt, cols, j, a_hi, a_lo, bank, rows_ready=None):
        w = [x[:, slot, :].rearrange("p (k n) -> p k n", k=kt) for x in (w_hi, w_lo)]
        order = products(kt)
        for n, (k, wi, ai) in enumerate(order):
            if rows_ready is not None and n % 3 == 0:
                pe.wait_ge(rows_ready, k + 1)
            for b in range(NTB):
                mm = pe.matmul(ps[:, bank + b, 0:TB], w[wi][:, k, j * P:(j + 1) * P],
                               (a_hi, a_lo)[ai][:, k, b * TB:(b + 1) * TB],
                               start=(n == 0), stop=(n == len(order) - 1))
        mm.then_inc(tile_done, 1)

    def loads_of(n):
        return 16 * (n // 2 + 1)

    def w_cols(w, col0):
        return w.rearrange("(k p) n -> p k n", p=P)[:, :, bass.ds(col0, NC_)]

    s_const = sem("s_const")
    s_small = sem("s_small")
    s_crow = sem("s_crow")
    s_wada = [sem(f"s_wada{i}") for i in range(4)]
    s_ct = sem("s_ct")
    s_vecp = sem("s_vecp")
    s_vect = sem("s_vect")
    s_lam = sem("s_lam")
    s_arow = sem("s_arow")
    s_atp = sem("s_atp")
    s_grow = sem("s_grow")
    s_gtp = sem("s_gtp")
    s_adat = sem("s_adat")
    s_gst = [sem("s_gst0"), sem("s_gst1")]
    s_xl = [sem(f"s_xl{i}") for i in range(4)]
    s_xss = sem("s_xss")
    s_xv = sem("s_xv")
    s_xr = sem("s_xr")
    s_xs = sem("s_xs")
    s_xtp = sem("s_xtp")
    s_xm = sem("s_xm")
    s_aff = sem("s_aff")
    s_ahi = sem("s_ahi")
    s_alo = sem("s_alo")

    def tile_rows(t):
        return P if t < NCH else TS

    def kt2(ap):
        return ap.rearrange("p (b k) n -> p b k n", b=2)

    def of_tokens(which, t):
        A = ada_t[:, which]
        return A[:, :, TS:TS + 1].broadcast_to((P, KT, P)) if t < NCH else A[:, :, 0:TS]

    def transposed_banks(b, r):
        return ps[:, b:b + 2, :].rearrange("p b (k n) -> p b k n", k=4)[:, :, :, 0:r]

    with ExitStack() as scope:
        cur[0] = scope
        XS = 4
        WS = 4
        w_ada = sb("w_ada_chunks", [P, WS, CW])
        c_rows = sb("c_rows", [TOK_C, D_MODEL])
        c_t = sb("c_t", [P, KT, TOK_C])
        vec_rows = sb("vec_rows", [NVEC, P])
        vec_t = sb("vec_t", [P, NVEC])
        ffrows = sb("ff_rows", [20, D_FF])
        lams = sb("lams", [1, 4, DQK])
        lam_e = sb("lam_e", [1, 4])
        lam_p = sb("lam_p", [1, DQK])
        gate_c = sb("gate_cols", [P, 2, 2, TOK_C])
        gate_row = sb("gate_row", [TOK_C, 2, NC_])
        x_in = sb("x_in", [P, XS, D_MODEL])
        x_a = sb("x_a", [P, 2, KT, P])
        sq = sb("sq", [P, D_MODEL], mybir.dt.bfloat16)
        st = sb("st", [P, NTT, 3])
        ada_row = sb("ada_row", [TOK_C, 2, NC_])
        BA, BT, BF, BX = 0, 2, 3, 4
        X0 = 9

        def is_gate(n):
            return n // 4 % 3 == 2

        def gates_to(n):
            return sum(1 for m in range(n + 1) if is_gate(m))

        with nc.Block() as block:
            @block.gpsimd
            def _(pool):
                pool.memset(ident[:], 0.0).then_inc(s_const, 1)
                pool.memset(mask_q[:], 0.0).then_inc(s_const, 1)
                pool.memset(mask_s[:], 0.0).then_inc(s_const, 1)
                pool.memset(mask_n[:], 0.0).then_inc(s_const, 1)
                pool.memset(ones[:], 1.0).then_inc(s_const, 1)
                pool.memset(minus_half[:], -0.5).then_inc(s_const, 1)
                pool.memset(same_seq[:], 1.0).then_inc(s_const, 1)
                pool.wait_ge(s_const, 7)
                pool.affine_select(out=ident[:], in_=ident[:], compare_op=ALU.not_equal, fill=1.0, base=0,
                                   pattern=[[-1, P]], channel_multiplier=1).then_inc(s_const, 1)
                pool.affine_select(out=mask_q[:], in_=mask_q[:], compare_op=ALU.is_ge, fill=NEG, base=0,
                                   pattern=[[-1, P]], channel_multiplier=1).then_inc(s_const, 1)
                pool.affine_select(out=mask_s[:], in_=mask_s[:], compare_op=ALU.is_ge, fill=NEG, base=0,
                                   pattern=[[1, P]], channel_multiplier=-1).then_inc(s_const, 1)
                m = mask_n[:].rearrange("p (b t) -> p b t", b=DEC_B)
                pool.affine_select(out=m, in_=m, compare_op=ALU.is_ge, fill=NEG, base=0,
                                   pattern=[[-DEC_T, DEC_B], [0, DEC_T]], channel_multiplier=1).then_inc(s_const, 1)
                pool.affine_select(out=same_seq[:], in_=same_seq[:], compare_op=ALU.is_ge, fill=0.0, base=0,
                                   pattern=[[-DEC_T, DEC_B]], channel_multiplier=1).then_inc(s_const, 1)
                pool.wait_ge(s_const, 12)
                pool.affine_select(out=same_seq[:], in_=same_seq[:], compare_op=ALU.is_ge, fill=0.0, base=DEC_T - 1,
                                   pattern=[[DEC_T, DEC_B]], channel_multiplier=-1).then_inc(s_const, 1)
                pool.affine_select(out=m, in_=m, compare_op=ALU.is_ge, fill=NEG, base=0,
                                   pattern=[[DEC_T, DEC_B], [1, DEC_T]], channel_multiplier=-1).then_inc(s_const, 1)

                def x_rstd(t):
                    r = tile_rows(t)
                    pool.wait_ge(s_xv, t + 1)
                    pool.tensor_tensor(st[0:r, t, 2:3], st[0:r, t, 1:2], minus_half[0:r, 0:1], ALU.pow).then_inc(s_xr, 1)

                def x_shift(t):
                    r = tile_rows(t)
                    pool.wait_ge(s_xm, t + 1)
                    pool.tensor_tensor(x_a[:, t % 2, :, 0:r], x_a[:, t % 2, :, 0:r], of_tokens(1, t), ALU.add).then_inc(s_aff, 1)

                def gate_store(n):
                    g = gates_to(n)
                    pool.wait_ge(s_grow, g)
                    pool.dma_start(GATES[n // 12, :, n % 4 * NC_:(n % 4 + 1) * NC_], gate_row[:, (g - 1) % 2, :])\
                        .then_inc(s_gst[(g - 1) % 2], 16)

                for n in range(ADA_CHUNKS):
                    if 0 <= n - X0 + 2 < NTT:
                        x_rstd(n - X0 + 2)
                    if 0 <= n - X0 < NTT:
                        x_shift(n - X0)
                    if n >= 2 and is_gate(n - 2):
                        gate_store(n - 2)
                gate_store(ADA_CHUNKS - 2)
                gate_store(ADA_CHUNKS - 1)
                for i in range(2):
                    pool.wait_ge(s_gst[i], 16 * 4)

            @block.sync
            def _(sp):
                sp.dma_start(c_rows[0:TS, :], I["c_sample"].unsqueeze(1).broadcast_to((DEC_B, DEC_T, D_MODEL)))\
                    .then_inc(s_crow, 16)
                sp.dma_start(c_rows[TS:TOK_C, :], I["c_prompt"]).then_inc(s_crow, 16)
                for n in range(ADA_CHUNKS):
                    if n >= WS:
                        sp.wait_ge(tile_done, n - WS + 1)
                    sp.dma_start(w_ada[:, n % WS, :].rearrange("p (k n) -> p k n", k=KT), w_cols(I["w_ada"][0], n * NC_))\
                        .then_inc(s_wada[n % WS], 16)
                for n in range(2):
                    load_chunk(sp, n, w_cols(I["w_in"][0], D_COL + n * NC_), KT)

            @block.scalar
            def _(act):
                r = 0
                for nm in VECS:
                    k = I[nm].shape[1] // P
                    act.dma_start(vec_rows[r:r + k, :], I[nm].rearrange("a (k n) -> (a k) n", k=k)).then_inc(s_small, 16)
                    r += k
                for i, nm in enumerate(("lambda_q1", "lambda_k1", "lambda_q2", "lambda_k2")):
                    act.dma_start(lams[:, i, :], I[nm]).then_inc(s_small, 16)
                act.dma_start(ffrows[0:16, :], I["state_conv"][0].rearrange("b w f -> (b w) f")).then_inc(s_small, 16)
                act.dma_start(ffrows[16:19, :], I["conv_w"][0]).then_inc(s_small, 16)
                act.dma_start(ffrows[19:20, :], I["conv_b"]).then_inc(s_small, 16)

                def load_x(t):
                    r = tile_rows(t)
                    src = I["x_prompt"][0, t * P:(t + 1) * P, :] if t < NCH else \
                        I["x_sample"].rearrange("b t d -> (b t) d")
                    act.dma_start(x_in[0:r, t % XS, :], src).then_inc(s_xl[t % XS], 16)

                for t in range(XS):
                    load_x(t)
                act.wait_ge(s_ct, 1)
                act.activation(c_t[:], ps[:, BX, 0:KT * TOK_C].rearrange("p (k n) -> p k n", k=KT), ACT.Copy).then_inc(s_ct, 1)
                act.wait_ge(s_lam, 4)
                act.activation(lam_e[:, 2:4], lam_e[:, 0:2], ACT.Exp).then_inc(s_lam, 1)

                def x_norm(t):
                    r, s = tile_rows(t), t % XS
                    act.wait_ge(s_xl[s], 16 * (t // XS + 1))
                    if t:
                        act.wait_ge(s_xss, t)
                    act.activation(sq[0:r, :], x_in[0:r, s, :], ACT.Square, accum_out=st[0:r, t, 0:1]).then_inc(s_xss, 1)
                    act.wait_ge(s_xr, t + 1)
                    act.activation(x_in[0:r, s, :], x_in[0:r, s, :], ACT.Copy, scale=st[0:r, t, 2:3]).then_inc(s_xs, 1)

                def x_hi(t):
                    r = tile_rows(t)
                    act.wait_ge(s_aff, t + 1)
                    act.activation(acts_hi[:, :, t * P:t * P + r], x_a[:, t % 2, :, 0:r], ACT.Copy).then_inc(s_ahi, 1)

                def gate_rows(n):
                    g = gates_to(n)
                    act.wait_ge(s_gtp, g)
                    if g > 2:
                        act.wait_ge(s_gst[(g - 1) % 2], 16 * ((g - 1) // 2))
                    act.activation(gate_row[:, (g - 1) % 2, :], ps[0:TOK_C, BF, 0:NC_], ACT.Copy).then_inc(s_grow, 1)

                for n in range(ADA_CHUNKS):
                    act.wait_ge(tile_done, n + 1)
                    if n >= 2:
                        act.wait_ge(s_atp, n - 1)
                    act.activation(ada_row[:, n % 2, :], ps[0:TOK_C, BA + n % 2, 0:NC_], ACT.Copy).then_inc(s_arow, 1)
                    if 0 <= n - X0 + 2 < NTT:
                        x_norm(n - X0 + 2)
                    if 0 <= n - X0 - 1 < NTT:
                        t = n - X0 - 1
                        x_hi(t)
                        if t + XS < NTT:
                            act.wait_ge(s_xtp, 2 * (t + 1))
                            load_x(t + XS)
                    if n >= 2 and is_gate(n - 2):
                        gate_rows(n - 2)
                split_hi(act, 0, 16)
                gate_rows(ADA_CHUNKS - 2)
                gate_rows(ADA_CHUNKS - 1)

            @block.vector
            def _(dve):
                dve.wait_ge(s_small, 16 * (len(VECS) + 7))
                for i in range(2):
                    dve.tensor_tensor(lam_p[:], lams[:, 2 * i, :], lams[:, 2 * i + 1, :], ALU.mult).then_inc(s_lam, 1)
                    dve.wait_ge(s_lam, 2 * i + 1)
                    dve.reduce_sum(lam_e[:, i:i + 1], lam_p[:], AX_X).then_inc(s_lam, 1)
                    dve.wait_ge(s_lam, 2 * i + 2)
                dve.wait_ge(s_vecp, 1)
                dve.tensor_copy(vec_t[:], ps[:, BX + 1, 0:NVEC]).then_inc(s_vect, 1)
                dve.wait_ge(s_vecp, 2)
                dve.tensor_copy(ff_t[:], ps[:, BF, 0:20 * FT].rearrange("p (k n) -> p k n", k=FT)).then_inc(s_vect, 1)
                dve.wait_ge(s_vect, 1)
                dve.tensor_copy(gain_t[:, 0:H], vec_t[:, V_BR:V_BR + H]).then_inc(s_vect, 1)
                dve.tensor_scalar(gain_t[:, H:2 * H], vec_t[:, V_BR + H:V_BR + 2 * H], 1.0 - LAM_INIT, None, ALU.mult).then_inc(s_vect, 1)
                for part in (1, 4):
                    b = vec_t[:, part * KT:(part + 1) * KT]
                    dve.tensor_scalar(b, b, 1.0, None, ALU.add).then_inc(s_vect, 1)
                dve.wait_ge(s_lam, 5)
                dve.tensor_tensor(lam_e[:, 0:1], lam_e[:, 3:4], lam_e[:, 2:3], ALU.subtract).then_inc(s_lam, 1)
                dve.wait_ge(s_lam, 6)
                dve.tensor_scalar(lam_e[:, 0:1], lam_e[:, 0:1], -LAM_INIT, None, ALU.add).then_inc(s_lam, 1)
                dve.wait_ge(s_vect, 6)

                def ada_evac(n):
                    part, q = n // 4, n % 4
                    which = part // 3
                    dve.wait_ge(s_atp, n + 1)
                    if is_gate(n) and gates_to(n) > 2:
                        dve.wait_ge(s_gtp, gates_to(n) - 2)
                    for kk in range(2):
                        k = 2 * q + kk
                        src = ps[:, BT, kk * TOK_C:(kk + 1) * TOK_C]
                        bias = vec_t[:, part * KT + k:part * KT + k + 1]
                        if part % 3 == 0:
                            ins_ = dve.tensor_scalar(ada_t[:, 2 * which + 1, k, :], src, bias, None, ALU.add)
                        elif part % 3 == 1:
                            g = V_PRE + which * KT + k
                            ins_ = dve.tensor_scalar(ada_t[:, 2 * which, k, :], src, bias, vec_t[:, g:g + 1], ALU.add, ALU.mult)
                        else:
                            g = V_POST + which * KT + k
                            ins_ = dve.tensor_scalar(gate_c[:, (gates_to(n) - 1) % 2, kk, :], src, bias, vec_t[:, g:g + 1],
                                                     ALU.add, ALU.mult)
                        ins_.then_inc(s_adat, 1)

                def x_stat(t):
                    r = tile_rows(t)
                    dve.wait_ge(s_xss, t + 1)
                    dve.tensor_scalar(st[0:r, t, 1:2], st[0:r, t, 0:1], 1.0 / D_MODEL, EPS, ALU.mult, ALU.add).then_inc(s_xv, 1)

                def x_mul(t):
                    r = tile_rows(t)
                    dve.wait_ge(s_xtp, 2 * t + 2)
                    if t >= 2:
                        dve.wait_ge(s_alo, t - 1)
                    dve.tensor_tensor(kt2(x_a[:, t % 2, :, 0:r]), transposed_banks(BX + 2 * (t % 2), r),
                                      kt2(of_tokens(0, t)), ALU.mult).then_inc(s_xm, 1)

                def x_lo(t):
                    r = tile_rows(t)
                    dve.wait_ge(s_ahi, t + 1)
                    dve.tensor_tensor(acts_lo[:, :, t * P:t * P + r], x_a[:, t % 2, :, 0:r],
                                      acts_hi[:, :, t * P:t * P + r].bitcast(F32), ALU.subtract).then_inc(s_alo, 1)

                for n in range(ADA_CHUNKS):
                    if n:
                        ada_evac(n - 1)
                    if 0 <= n - X0 + 2 < NTT:
                        x_stat(n - X0 + 2)
                    if 0 <= n - X0 < NTT:
                        if n == X0:
                            dve.wait_ge(s_adat, 2 * 8)
                        x_mul(n - X0)
                    if 0 <= n - X0 - 1 < NTT:
                        x_lo(n - X0 - 1)
                    if n == 4:
                        dve.wait_ge(s_vecp, 3)
                        dve.tensor_copy(neg_lam[:], ps[:, BF, 500:501]).then_inc(s_vect, 1)
                ada_evac(ADA_CHUNKS - 1)
                split_lo(dve, 0, 1)

            @block.tensor
            def _(pe):
                pe.wait_ge(s_const, 14)
                pe.wait_ge(s_crow, 32)
                for k in range(KT):
                    tr = pe.transpose(ps[:, BX, k * TOK_C:(k + 1) * TOK_C], c_rows[:, k * P:(k + 1) * P], ident[0:TOK_C, 0:TOK_C])
                tr.then_inc(s_ct, 1)
                pe.wait_ge(s_small, 16 * (len(VECS) + 7))
                pe.transpose(ps[:, BX + 1, 0:NVEC], vec_rows[:], ident[0:NVEC, 0:NVEC]).then_inc(s_vecp, 1)
                for k in range(FT):
                    tr = pe.transpose(ps[:, BF, 20 * k:20 * (k + 1)], ffrows[:, k * P:(k + 1) * P], ident[0:20, 0:20])
                tr.then_inc(s_vecp, 1)
                pe.wait_ge(s_ct, 2)

                def ada_chunk(n):
                    pe.wait_ge(s_wada[n % WS], 16 * (n // WS + 1))
                    if n >= 2:
                        pe.wait_ge(s_arow, n - 1)
                    w = w_ada[:, n % WS, :].rearrange("p (k n) -> p k n", k=KT)
                    for k in range(KT):
                        mm = pe.matmul(ps[0:TOK_C, BA + n % 2, 0:NC_], c_t[:, k, :], w[:, k, :], start=(k == 0), stop=(k == KT - 1))
                    mm.then_inc(tile_done, 1)

                def ada_tr(n):
                    pe.wait_ge(s_arow, n + 1)
                    if n:
                        pe.wait_ge(s_adat, 2 * n)
                    for kk in range(2):
                        tr = pe.transpose(ps[:, BT, kk * TOK_C:(kk + 1) * TOK_C], ada_row[:, n % 2, kk * P:(kk + 1) * P],
                                          ident[0:TOK_C, 0:TOK_C])
                    tr.then_inc(s_atp, 1)

                def gate_tr(n):
                    g = gates_to(n)
                    pe.wait_ge(s_adat, 2 * (n + 1))
                    if g > 1:
                        pe.wait_ge(s_grow, g - 1)
                    for kk in range(2):
                        tr = pe.transpose(ps[0:TOK_C, BF, kk * P:(kk + 1) * P], gate_c[:, (g - 1) % 2, kk, :], ident[:])
                    tr.then_inc(s_gtp, 1)

                def x_tr(t):
                    r = tile_rows(t)
                    pe.wait_ge(s_xs, t + 1)
                    if t >= 2:
                        pe.wait_ge(s_xm, t - 1)
                    for hf in range(2):
                        for k in range(4):
                            kk = 4 * hf + k
                            tr = pe.transpose(ps[:, BX + 2 * (t % 2) + hf, k * P:k * P + r],
                                              x_in[0:r, t % XS, kk * P:(kk + 1) * P], ident[0:r, 0:r])
                        tr.then_inc(s_xtp, 1)

                for n in range(ADA_CHUNKS):
                    ada_chunk(n)
                    if n:
                        ada_tr(n - 1)
                    if n >= 2 and is_gate(n - 2):
                        gate_tr(n - 2)
                    if 0 <= n - X0 < NTT:
                        x_tr(n - X0)
                    if n == 2:
                        pe.wait_ge(s_lam, 7)
                        pe.wait_ge(s_vect, 2)
                        pe.matmul(ps[:, BF, 500:501], ones[0:1, :], lam_e[:, 0:1], start=True, stop=True).then_inc(s_vecp, 1)
                ada_tr(ADA_CHUNKS - 1)
                gate_tr(ADA_CHUNKS - 2)
                gate_tr(ADA_CHUNKS - 1)

    s_if = sem("s_if")
    s_ifz = sem("s_ifz")
    s_ifhi = sem("s_ifhi")
    s_iflo = sem("s_iflo")
    s_ifmm = sem("s_ifmm")
    s_ifst = sem("s_ifst")
    z_evac = [sem("z_evac_act"), sem("z_evac_dve")]
    s_rl = sem("s_rows_loaded")
    s_rv = sem("s_rows_dve")
    s_ra = sem("s_rows_act")
    s_ends = sem("s_ends_moved")
    s_mrun = sem("s_m_moved")
    s_rst = sem("s_rows_stored")
    z_stored = [[sem(f"z_stored{j}{s}") for s in range(2)] for j in range(2)]
    IN_CHUNKS = 3 * W_MIX // NC_
    T0 = ADA_CHUNKS
    with ExitStack() as scope:
        cur[0] = scope
        if_raw = sb("if_raw", [P, KT, 2 * H])
        if_hi = sb("if_hi", [P, KT, P], F32R)
        if_lo = sb("if_lo", [P, KT, P], F32R)
        if_out = sb("if_out", [36, T])
        stage = sb("stage", [P, 2, 2, T])
        R = H * NCH
        assert NCH == DEC_B
        b_if = sb("b_if", [R, 2])
        WID = (P, DEC_T)
        raw_i = [sb(f"raw_i{g}", [R, w]) for g, w in enumerate(WID)]
        f_x = [sb(f"f_x{g}", [R, w]) for g, w in enumerate(WID)]
        f_abs = [sb(f"f_abs{g}", [R, w]) for g, w in enumerate(WID)]
        f_sum = [sb(f"f_sum{g}", [R, w]) for g, w in enumerate(WID)]
        a_max = [sb(f"a_max{g}", [R, w]) for g, w in enumerate(WID)]
        m_t = [sb(f"m_t{g}", [R, w]) for g, w in enumerate(WID)]
        rows = [sb(f"rows{g}", [R, 5, w]) for g, w in enumerate(WID)]
        m_in = [sb(f"m_in{g}", [R, 1]) for g in range(2)]
        neg_end = [sb(f"neg_end{g}", [R, 1]) for g in range(2)]
        ends = sb("ends", [H, 2, NCH])
        m_run = sb("m_run", [H, NCH + 1])

        def bank3(b):
            return ps[:, b:b + 3, 0:TB]

        A_END = 16

        with nc.Block() as block:
            @block.gpsimd
            def _(pool):
                pool.dma_start(b_if[:, 0:1], I["b_if"][0, 0:H].unsqueeze(1).broadcast_to((H, NCH)).unsqueeze(2))\
                    .then_inc(s_rl, 16)
                pool.dma_start(b_if[:, 1:2], I["b_if"][0, H:2 * H].unsqueeze(1).broadcast_to((H, NCH)).unsqueeze(2))\
                    .then_inc(s_rl, 16)
                pool.dma_start(m_in[1][:], I["state_m"][0].rearrange("b h -> h b").unsqueeze(2)).then_inc(s_rl, 16)
                for g in range(2):
                    pool.wait_ge(z_evac[g], 1)
                    pool.dma_start(GIFP[g], if_out[32 * g:32 * g + H, 0:SEQ]).then_inc(s_ifst, 16)
                    pool.dma_start(GIFD[g], if_out[32 * g:32 * g + H, SEQ:T]).then_inc(s_ifst, 16)
                pool.wait_ge(s_ifst, 64)
                for g, dst in enumerate((raw_i, f_x)):
                    pool.dma_start(dst[0][:], GIFP[g].rearrange("h (c t) -> (h c) t", c=NCH)).then_inc(s_rl, 16)
                    pool.dma_start(dst[1][:], GIFD[g].rearrange("h (b t) -> (h b) t", b=DEC_B)).then_inc(s_rl, 16)
                pool.wait_ge(s_rl, 16 * 7)
                pool.wait_ge(s_rv, A_END)
                pool.dma_start(ENDS[0].unsqueeze(1), f_sum[0][:, P - 1:P]).then_inc(s_ends, 16)
                pool.dma_start(ENDS[1].unsqueeze(1), a_max[0][:, P - 1:P]).then_inc(s_ends, 16)
                pool.wait_ge(s_ends, 32)
                for q in range(2):
                    pool.dma_start(ends[:, q, :], ENDS[q].rearrange("(h c) -> h c", c=NCH)).then_inc(s_ends, 16)
                pool.wait_ge(s_rv, A_END + 1)
                pool.dma_start(ENDS[2].rearrange("(h c) -> h c", c=NCH), m_run[:, 0:NCH]).then_inc(s_mrun, 16)
                pool.wait_ge(s_mrun, 16)
                pool.dma_start(m_in[0][:], ENDS[2].unsqueeze(1)).then_inc(s_mrun, 16)
                pool.dma_start(O["m_prompt"][0, 0].unsqueeze(1), m_run[:, NCH:NCH + 1]).then_inc(s_rst, 16)
                pool.wait_ge(s_ra, 10)
                pool.dma_start(ROWS.rearrange("q h (c t) -> (h c) q t", c=NCH), rows[0][:]).then_inc(s_rst, 16)
                pool.dma_start(ROWD.rearrange("q h (b t) -> (h b) q t", b=DEC_B), rows[1][:]).then_inc(s_rst, 16)
                pool.dma_start(ENDS[3].unsqueeze(1), rows[0][:, Q_INTER, P - 1:P]).then_inc(s_rst, 16)
                pool.dma_start(DECD[0].unsqueeze(1), rows[1][:, Q_INTER, DEC_T - 1:DEC_T]).then_inc(s_rst, 16)
                pool.dma_start(O["m_sample"][0].rearrange("b h -> h b").unsqueeze(2), m_t[1][:, DEC_T - 1:DEC_T]).then_inc(s_rst, 16)
                pool.wait_ge(s_rst, 96)

            @block.sync
            def _(sp):
                sp.dma_start(if_raw[:], I["w_in"][0].rearrange("(k p) n -> p k n", p=P)[:, :, IF_COL:IF_COL + 2 * H])\
                    .then_inc(s_if, 16)

                def store(c, s, zt):
                    for j in range(2):
                        sp.wait_ge(z_evac[j], c + 2)
                        sp.dma_start(ZT[bass.ds(zt + j, 1), :, :].rearrange("a p t -> p (a t)"), stage[:, j, s, :])\
                            .then_inc(z_stored[j][s], 16)

                for c in range(IN_CHUNKS):
                    m = c + 2
                    col = D_COL + m * NC_ if m < IN_CHUNKS else (m - IN_CHUNKS) * NC_
                    load_chunk(sp, c % 2, w_cols(I["w_in"][0], col), KT, m - 1)
                    store(c, c % 2, Z_DQ + 2 * c)
                for j in range(2):
                    for s in range(2):
                        sp.wait_ge(z_stored[j][s], 16 * IN_CHUNKS // 2)

            @block.scalar
            def _(act):
                act.wait_ge(s_if, 16)
                act.wait_ge(s_ifz, 2)
                for g in range(2):
                    act.activation(if_hi[:, :, 32 * g:32 * g + H], if_raw[:, :, g * H:(g + 1) * H], ACT.Copy).then_inc(s_ifhi, 1)

                act.wait_ge(s_ifmm, 1)
                act.activation(if_out[0:H, :].rearrange("p (b t) -> p b t", b=NTB), ps[0:H, 3:6, 0:TB], ACT.Copy)\
                    .then_inc(z_evac[0], 1)

                def chunk(c):
                    split_hi(act, (c + 1) % 2, loads_of(c + 1), T0 + 2 * c)
                    act.wait_ge(tile_done, T0 + 2 * c + 1)
                    if c >= 2:
                        act.wait_ge(z_stored[0][c % 2], 16 * (c // 2))
                    act.activation(stage[:, 0, c % 2, :].rearrange("p (b t) -> p b t", b=NTB), bank3(0), ACT.Copy)\
                        .then_inc(z_evac[0], 1)

                def log_sigmoid():
                    for g in range(2):
                        act.wait_ge(s_rv, 2 + 3 * g)
                        act.activation(f_abs[g][:], f_abs[g][:], ACT.Exp, scale=-1.0).then_inc(s_ra, 1)
                    for g in range(2):
                        act.wait_ge(s_rv, 7 + g)
                        act.activation(f_abs[g][:], f_abs[g][:], ACT.Ln).then_inc(s_ra, 1)

                def row_exps():
                    for g in range(2):
                        act.wait_ge(s_rv, A_END + 1 + 3 * (g + 1))
                        act.activation(rows[g][:, Q_INTER, :], rows[g][:, Q_G, :], ACT.Exp, bias=m_in[g][:], scale=-1.0)\
                            .then_inc(s_ra, 1)
                        act.activation(rows[g][:, Q_EMT, :], m_t[g][:], ACT.Exp, scale=-1.0).then_inc(s_ra, 1)
                        act.activation(rows[g][:, Q_WEND, :], rows[g][:, Q_A, :], ACT.Exp, bias=neg_end[g][:])\
                            .then_inc(s_ra, 1)

                for c in range(IN_CHUNKS):
                    chunk(c)
                    if c == 1:
                        log_sigmoid()
                row_exps()

            @block.vector
            def _(dve):
                dve.memset(if_hi[:].bitcast(F32), 0.0).then_inc(s_ifz, 1)
                dve.memset(if_lo[:].bitcast(F32), 0.0).then_inc(s_ifz, 1)
                dve.wait_ge(s_ifhi, 2)
                dve.wait_ge(s_ifz, 2)
                for g in range(2):
                    dve.tensor_tensor(if_lo[:, :, 32 * g:32 * g + H], if_raw[:, :, g * H:(g + 1) * H],
                                      if_hi[:, :, 32 * g:32 * g + H].bitcast(F32), ALU.subtract).then_inc(s_iflo, 1)
                dve.wait_ge(s_ifmm, 1)
                dve.tensor_copy(if_out[32:32 + H, :].rearrange("p (b t) -> p b t", b=NTB), ps[32:32 + H, 3:6, 0:TB])\
                    .then_inc(z_evac[1], 1)

                def chunk(c):
                    split_lo(dve, (c + 1) % 2, c + 2)
                    dve.wait_ge(tile_done, T0 + 2 * c + 2)
                    if c >= 2:
                        dve.wait_ge(z_stored[1][c % 2], 16 * (c // 2))
                    dve.tensor_copy(stage[:, 1, c % 2, :].rearrange("p (b t) -> p b t", b=NTB), bank3(3))\
                        .then_inc(z_evac[1], 1)

                def log_sigmoid():
                    dve.wait_ge(s_rl, 16 * 7)
                    for g in range(2):
                        n0 = 3 * g
                        dve.tensor_scalar(f_x[g][:], f_x[g][:], b_if[:, 1:2], None, ALU.add).then_inc(s_rv, 1)
                        dve.wait_ge(s_rv, n0 + 1)
                        dve.scalar_tensor_tensor(out=f_abs[g][:], in0=f_x[g][:], scalar=-1.0, in1=f_x[g][:],
                                                 op0=ALU.mult, op1=ALU.max).then_inc(s_rv, 1)
                        dve.tensor_scalar(f_x[g][:], f_x[g][:], 0.0, None, ALU.min).then_inc(s_rv, 1)
                    for g in range(2):
                        dve.wait_ge(s_ra, g + 1)
                        dve.tensor_scalar(f_abs[g][:], f_abs[g][:], 1.0, None, ALU.add).then_inc(s_rv, 1)
                    for g in range(2):
                        n0 = 8 + 4 * g
                        dve.wait_ge(s_ra, 3 + g)
                        dve.tensor_tensor(f_x[g][:], f_x[g][:], f_abs[g][:], ALU.subtract).then_inc(s_rv, 1)
                        dve.wait_ge(s_rv, n0 + 1)
                        dve.tensor_tensor_scan(f_sum[g][:], ones[0:R, 0:WID[g]], f_x[g][:], 0.0, ALU.mult, ALU.add)\
                            .then_inc(s_rv, 1)
                        dve.wait_ge(s_rv, n0 + 2)
                        dve.scalar_tensor_tensor(out=rows[g][:, Q_A, :], in0=raw_i[g][:], scalar=b_if[:, 0:1],
                                                 in1=f_sum[g][:], op0=ALU.add, op1=ALU.subtract).then_inc(s_rv, 1)
                        dve.wait_ge(s_rv, n0 + 3)
                        dve.tensor_tensor_scan(a_max[g][:], rows[g][:, Q_A, :], rows[g][:, Q_A, :], NEG * 100,
                                               ALU.max, ALU.max).then_inc(s_rv, 1)

                def chunk_m():
                    dve.memset(m_run[:, 0:1], 0.0)
                    dve.wait_ge(s_ends, 64)
                    dve.tensor_tensor_scan(m_run[:, 1:NCH + 1], ends[:, 1, :], ends[:, 0, :], 0.0, ALU.max, ALU.add)\
                        .then_inc(s_rv, 1)

                def row_gates():
                    dve.wait_ge(s_mrun, 32)
                    for g in range(2):
                        dve.tensor_scalar(rows[g][:, Q_G, :], a_max[g][:], m_in[g][:], None, ALU.max).then_inc(s_rv, 1)
                        dve.wait_ge(s_rv, A_END + 2 + 3 * g)
                        dve.tensor_scalar(neg_end[g][:], rows[g][:, Q_G, WID[g] - 1:WID[g]], -1.0, None, ALU.mult)\
                            .then_inc(s_rv, 1)
                        dve.tensor_tensor(m_t[g][:], f_sum[g][:], rows[g][:, Q_G, :], ALU.add).then_inc(s_rv, 1)

                for c in range(IN_CHUNKS):
                    chunk(c)
                    if c == 1:
                        log_sigmoid()
                    if c == 3:
                        chunk_m()
                    if c == 4:
                        row_gates()

            @block.tensor
            def _(pe):
                pe.wait_ge(s_iflo, 2)
                order = products(KT)
                for m, (k, wi, ai) in enumerate(order):
                    for b in range(NTB):
                        mm = pe.matmul(ps[:, 3 + b, 0:TB], (if_hi, if_lo)[wi][:, k, :],
                                       (acts_hi, acts_lo)[ai][:, k, b * TB:(b + 1) * TB],
                                       start=(m == 0), stop=(m == len(order) - 1))
                mm.then_inc(s_ifmm, 1)
                with pe.Fori(0, IN_CHUNKS - 1, 2) as i:
                    for s in range(2):
                        pe.wait_ge(w_lo_ready, i + s + 1)
                        for j in range(2):
                            pe.wait_ge(z_evac[j], i + s + 1)
                            gemm_tile(pe, s, KT, NC_, j, acts_hi, acts_lo, 3 * j)


    PER_CHUNK = 2 * NTB
    MZ0, TILEM = IN_CHUNKS, ADA_CHUNKS + 2 * IN_CHUNKS
    MZ_TILES = M_CHUNKS * PER_CHUNK
    GATE0 = MZ0 + M_CHUNKS
    UNITS = H * NCH
    HALVES = 2 * MZ_TILES // UNITS
    SPLIT_EVERY = UNITS // M_CHUNKS
    d_loaded = [sem("d_loaded0"), sem("d_loaded1")]
    tr_full = sem("tr_full")
    tr_free = sem("tr_free")
    kv_stored = sem("kv_stored")
    a_scores = sem("a_scores")
    a_max_ = sem("a_max")
    a_exp = sem("a_exp")
    a_coef = sem("a_coef")
    a_diff = sem("a_diff")
    a_pv = sem("a_pv")
    a_out = sem("a_out")
    a_sq = sem("a_sq")
    a_ms = sem("a_ms")
    o_rstd = sem("o_rstd")
    o_norm = sem("o_norm")
    o_tr = sem("o_tr")
    o_cols = sem("o_cols")
    o_stored = sem("o_stored")
    n_rows = sem("n_rows")
    n_rows_t = sem("n_rows_t")
    mz_evac = sem("mz_evac")
    mz_stored = [sem("mz_stored0"), sem("mz_stored1")]
    SCALE_D = DQK ** -0.5
    SCALE_M = DH ** -0.5
    PV1 = DH + 1
    FILLS_KV = 4

    def fills_before(u):
        return sum((v % NCH + 4) // 4 for v in range(u)) + FILLS_KV * min(u // NCH + 1, H)

    with ExitStack() as scope:
        cur[0] = scope
        zq, zk, zv = ([sb(f"z_d{x}{i}", [P, SEQ]) for i in range(2)] for x in "qkv")
        k_tok = sb("k_tok", [P, NCH, P])
        v_tok = sb("v_tok", [P, NCH, P])
        E_ = sb("e_maps", [P, 2, 2, SEQ])
        p_t = sb("p_t", [P, NCH, P])
        stat = sb("stat", [P, 2, 8])
        mix = sb("mix", [P, 2, NCH, DH])
        ssq = sb("ssq", [P, 2, 2, NCH])
        sqj = sb("sqj", [P, P], mybir.dt.bfloat16)
        cols = sb("cols", [P, SEQ])
        row_in = sb("row_in", [H * NCH, 5, P])
        out_z = sb("out_z", [P, 2, TB])
        BS, BO, BT, BZ = 0, 4, 5, 7

        def z_row(t):
            n = t // NTB
            return Z_MQ + n if n < 3 * H else Z_MO + n - 3 * H

        def tiles_before(u):
            return HALVES * u // 2

        with nc.Block() as block:
            @block.sync
            def _(sp):
                def load_head(h):
                    for dst, z in ((zq, Z_DQ), (zk, Z_DK), (zv, Z_DV)):
                        sp.dma_start(dst[h % 2][:], ZT[z + h, :, 0:SEQ]).then_inc(d_loaded[h % 2], 16)

                def z_store(t):
                    sp.wait_ge(mz_evac, t + 1)
                    sp.dma_start(ZT[z_row(t), :, t % NTB * TB:(t % NTB + 1) * TB], out_z[:, t % 2, :])\
                        .then_inc(mz_stored[t % 2], 16)

                load_head(0)
                load_head(1)
                sp.dma_start(row_in[:], ROWS.rearrange("q h (c t) -> (h c) q t", c=NCH)).then_inc(n_rows, 16)
                sp.dma_start(decay_p[:], ENDS[3].unsqueeze(0).broadcast_to((P, H * NCH))).then_inc(n_rows, 16)
                load_chunk(sp, 0, w_cols(I["w_in"][0], 2 * NC_), KT, MZ0 + 1)
                for u in range(UNITS):
                    h, i = u // NCH, u % NCH
                    if i == 1 and 1 <= h < H - 1:
                        sp.wait_ge(a_pv, NCH * h)
                        load_head(h + 1)
                    if i == 2:
                        sp.wait_ge(tr_free, fills_before(NCH * h + 1) - 1)
                        for dst, src in ((O["k_prompt"], k_tok), (O["v_prompt"], v_tok)):
                            sp.dma_start(dst[0, 0].rearrange("(c p) h d -> p c h d", p=P)[:, :, h, :], src[:]).then_inc(kv_stored, 16)
                    if i == 4 and h:
                        sp.wait_ge(o_cols, 2 * h)
                        sp.dma_start(BRANCH[h - 1], cols[:]).then_inc(o_stored, 16)
                    for t in range(tiles_before(u), tiles_before(u + 1)):
                        z_store(t)
                    if u % SPLIT_EVERY == 2:
                        n = MZ0 + u // SPLIT_EVERY + 3
                        col = (n - MZ0) * NC_ if n < GATE0 else GATE_COL + (n - GATE0) * NC_
                        if n < GATE0 + 2:
                            load_chunk(sp, n % 2, w_cols(I["w_in"][0], col), KT, n - 1)
                sp.wait_ge(o_cols, 2 * H)
                sp.dma_start(BRANCH[H - 1], cols[:]).then_inc(o_stored, 16)
                sp.wait_ge(kv_stored, 32 * H)
                sp.wait_ge(o_stored, 16 * H)
                for i in range(2):
                    sp.wait_ge(mz_stored[i], 8 * MZ_TILES)

            @block.gpsimd
            def _(pool):
                for h in range(H):
                    pool.wait_ge(a_ms, h + 1)
                    pool.tensor_tensor(ssq[:, h % 2, 1, :], ssq[:, h % 2, 0, :], minus_half[:, 0:NCH], ALU.pow).then_inc(o_rstd, 1)

            @block.scalar
            def _(act):
                def fill(n, dst, cnt):
                    act.wait_ge(tr_full, n + 1)
                    act.activation(dst, ps[:, BT + n % 2, 0:cnt * P].rearrange("p (c k) -> p c k", c=cnt), ACT.Copy).then_inc(tr_free, 1)

                def square(u):
                    h, i = u // NCH, u % NCH
                    act.wait_ge(a_out, u + 1)
                    if u:
                        act.wait_ge(a_sq, u)
                    act.activation(sqj[:], mix[:, h % 2, i, :], ACT.Square, accum_out=ssq[:, h % 2, 0, i:i + 1]).then_inc(a_sq, 1)

                def exps(u):
                    keys = (u % NCH + 1) * P
                    act.wait_ge(a_max_, 3 * u + 3)
                    if u >= 2:
                        act.wait_ge(tr_full, fills_before(u - 1) - (FILLS_KV if (u - 1) % NCH == 0 else 0))
                    for m in range(2):
                        act.activation(E_[:, u % 2, m, 0:keys], ps[:, BS + 2 * m:BS + 2 * m + 2, :].rearrange("p b n -> p (b n)")[:, 0:keys],
                                       ACT.Exp, bias=stat[:, u % 2, 4 + m:5 + m], scale=SCALE_D,
                                       accum_out=stat[:, u % 2, m:m + 1]).then_inc(a_exp, 1)

                def z_out(t):
                    act.wait_ge(tile_done, TILEM + t + 1)
                    if t >= 2:
                        act.wait_ge(mz_stored[t % 2], 16 * (t // 2))
                    act.activation(out_z[:, t % 2, :], ps[:, BZ, 0:TB], ACT.Copy).then_inc(mz_evac, 1)

                for u in range(UNITS):
                    h, i = u // NCH, u % NCH
                    f = fills_before(u)
                    exps(u)
                    if i == 0:
                        if h:
                            act.wait_ge(kv_stored, 32 * h)
                            act.wait_ge(a_pv, NCH * h)
                        for n in range(FILLS_KV):
                            dst = (v_tok, k_tok)[n // 2]
                            fill(f - FILLS_KV + n, dst[:, 4 * (n % 2):4 * (n % 2) + 4, :], 4)
                    t = tiles_before(u)
                    if u and u % 2 == 0:
                        z_out(t - 1)
                    if u % 2:
                        z_out(t)
                    if u:
                        act.wait_ge(a_pv, u)
                    for n in range((i + 4) // 4):
                        cnt = min(4, i + 1 - 4 * n)
                        fill(f + n, p_t[:, 4 * n:4 * n + cnt, :], cnt)
                    if u % 2 == 0:
                        z_out(t)
                    if u:
                        square(u - 1)
                    if u % SPLIT_EVERY == 1:
                        n = MZ0 + u // SPLIT_EVERY + 1
                        split_hi(act, n % 2, loads_of(n), TILEM + PER_CHUNK * (u // SPLIT_EVERY))
                z_out(MZ_TILES - 1)
                square(UNITS - 1)
                act.wait_ge(n_rows_t, 1)
                act.activation(rows_t[:], ps[:, BZ, 0:5 * H * NCH].rearrange("p (q r) -> p q r", q=5), ACT.Copy).then_inc(n_rows_t, 1)

            @block.vector
            def _(dve):
                def out_rows(u):
                    dve.wait_ge(a_pv, u + 1)
                    dve.tensor_scalar(mix[:, u // NCH % 2, u % NCH, :], ps[:, BO, 0:DH], stat[:, u % 2, 2:3], None, ALU.mult).then_inc(a_out, 1)

                def norm(h):
                    dve.wait_ge(a_sq, NCH * (h + 1))
                    q = ssq[:, h % 2]
                    dve.tensor_scalar(q[:, 0, :], q[:, 0, :], 1.0 / DH, EPS, ALU.mult, ALU.add).then_inc(a_ms, 1)
                    dve.wait_ge(o_rstd, h + 1)
                    dve.tensor_tensor(mix[:, h % 2], mix[:, h % 2], q[:, 1, :].unsqueeze(2).broadcast_to((P, NCH, DH)),
                                      ALU.mult).then_inc(o_norm, 1)

                def out_cols(h):
                    for hf in range(2):
                        dve.wait_ge(o_tr, 2 * h + hf + 1)
                        if h:
                            dve.wait_ge(o_stored, 16 * h)
                        dve.tensor_scalar(cols[:, 512 * hf:512 * hf + 512], ps[:, BT + hf, :], gain_t[:, H + h:H + h + 1], None, ALU.mult)\
                            .then_inc(o_cols, 1)

                for u in range(UNITS):
                    h, i = u // NCH, u % NCH
                    keys = (i + 1) * P
                    st_, E = stat[:, u % 2], E_[:, u % 2]
                    sc = ps[:, BS:BS + 4, :].rearrange("p (m b) n -> p m (b n)", m=2)
                    diag = sc[:, :, i * P:keys]
                    dve.wait_ge(a_scores, u + 1)
                    dve.tensor_tensor(diag, diag, mask_q[:].unsqueeze(1).broadcast_to((P, 2, P)), ALU.add).then_inc(a_max_, 1)
                    dve.wait_ge(a_max_, 3 * u + 1)
                    dve.tensor_reduce(st_[:, 4:6], sc[:, :, 0:keys], AX_X, ALU.max).then_inc(a_max_, 1)
                    dve.wait_ge(a_max_, 3 * u + 2)
                    dve.tensor_scalar(st_[:, 4:6], st_[:, 4:6], -SCALE_D, None, ALU.mult).then_inc(a_max_, 1)
                    if u:
                        out_rows(u - 1)
                    dve.wait_ge(a_exp, 2 * u + 2)
                    dve.reciprocal(st_[:, 2:4], st_[:, 0:2]).then_inc(a_coef, 1)
                    dve.wait_ge(a_coef, 2 * u + 1)
                    dve.scalar_tensor_tensor(out=st_[:, 6:7], in0=st_[:, 3:4], scalar=neg_lam[:],
                                             in1=st_[:, 0:1], op0=ALU.mult, op1=ALU.mult).then_inc(a_coef, 1)
                    dve.wait_ge(a_coef, 2 * u + 2)
                    dve.scalar_tensor_tensor(out=E[:, 0, 0:keys], in0=E[:, 1, 0:keys], scalar=st_[:, 6:7],
                                             in1=E[:, 0, 0:keys], op0=ALU.mult, op1=ALU.add).then_inc(a_diff, 1)
                    if u % SPLIT_EVERY == 2:
                        n = MZ0 + u // SPLIT_EVERY + 1
                        split_lo(dve, n % 2, n + 1)
                    if h and i == 1:
                        norm(h - 1)
                    if h and i == 2:
                        out_cols(h - 1)
                out_rows(UNITS - 1)
                norm(H - 1)
                dve.wait_ge(n_rows_t, 2)
                dve.tensor_scalar(rows_t[:, Q_WEND, :], rows_t[:, Q_WEND, :], SCALE_M, None, ALU.mult).then_inc(n_rows_t, 1)
                out_cols(H - 1)

            @block.tensor
            def _(pe):
                def fill(f, blocks):
                    if f >= 2:
                        pe.wait_ge(tr_free, f - 1)
                    for n, b in enumerate(blocks):
                        tr = pe.transpose(ps[:, BT + f % 2, n * P:(n + 1) * P], b, ident[:])
                    tr.then_inc(tr_full, 1)

                def out_tr(h, f):
                    pe.wait_ge(o_norm, h + 1)
                    pe.wait_ge(tr_free, f)
                    for hf in range(2):
                        for c in range(4):
                            tr = pe.transpose(ps[:, BT + hf, c * P:(c + 1) * P], mix[:, h % 2, 4 * hf + c, :], ident[:])
                        tr.then_inc(o_tr, 1)

                def scores(u):
                    h, i = u // NCH, u % NCH
                    if i == 0:
                        pe.wait_ge(d_loaded[h % 2], 48 * (h // 2 + 1))
                    if u:
                        pe.wait_ge(a_exp, 2 * u)
                    keys = (i + 1) * P
                    for k0 in range(0, keys, 512):
                        k1 = min(keys, k0 + 512)
                        for m in range(2):
                            mm = pe.matmul(ps[:, BS + 2 * m + k0 // 512, 0:k1 - k0],
                                           zq[h % 2][m * DQK:(m + 1) * DQK, i * P:(i + 1) * P],
                                           zk[h % 2][m * DQK:(m + 1) * DQK, k0:k1], start=True, stop=True)
                    mm.then_inc(a_scores, 1)

                def z_half(n):
                    t, hf = n // 2, n % 2
                    c, j, b = t // PER_CHUNK, t // NTB % 2, t % NTB
                    if n % (2 * PER_CHUNK) == 0:
                        pe.wait_ge(w_lo_ready, MZ0 + c + 1)
                    if hf == 0 and t:
                        pe.wait_ge(mz_evac, t)
                    w = [x[:, c % 2, :].rearrange("p (k n) -> p k n", k=KT) for x in (w_hi, w_lo)]
                    order = products(KT)
                    for m in range(len(order) // 2 * hf, len(order) // 2 * (hf + 1)):
                        k, wi, ai = order[m]
                        mm = pe.matmul(ps[:, BZ, 0:TB], w[wi][:, k, j * P:(j + 1) * P],
                                       (acts_hi, acts_lo)[ai][:, k, b * TB:(b + 1) * TB],
                                       start=(m == 0), stop=(m == len(order) - 1))
                    if hf:
                        mm.then_inc(tile_done, 1)

                z_half(0)
                z_half(1)
                scores(0)
                for u in range(UNITS):
                    h, i = u // NCH, u % NCH
                    f = fills_before(u)
                    if i == 0:
                        for n in range(FILLS_KV):
                            src = (zv, zk)[n // 2][h % 2]
                            fill(f - FILLS_KV + n, [src[:, (4 * (n % 2) + c) * P:(4 * (n % 2) + c + 1) * P] for c in range(4)])
                    if u + 1 < UNITS:
                        scores(u + 1)
                    if u:
                        z_half(HALVES * u)
                    if h and i == 2:
                        out_tr(h - 1, f)
                    pe.wait_ge(a_diff, u + 1)
                    if h and i == 2:
                        pe.wait_ge(o_cols, 2 * h)
                    for n in range((i + 4) // 4):
                        fill(f + n, [E_[:, u % 2, 0, c * P:(c + 1) * P] for c in range(4 * n, min(4 * n + 4, i + 1))])
                    if u:
                        z_half(HALVES * u + 1)
                    pe.wait_ge(tr_free, f + (i + 4) // 4)
                    if u:
                        pe.wait_ge(a_out, u)
                    for c in range(i + 1):
                        mm = pe.matmul(ps[:, BO, 0:DH], p_t[:, c, :], v_tok[:, c, :], start=(c == 0), stop=(c == i))
                    mm.then_inc(a_pv, 1)
                    z_half(HALVES * u + 2)
                pe.wait_ge(n_rows, 32)
                pe.wait_ge(mz_evac, MZ_TILES)
                for q in range(5):
                    tr = pe.transpose(ps[:, BZ, q * 32:(q + 1) * 32], row_in[:, q, :], ident[0:32, 0:32])
                tr.then_inc(n_rows_t, 1)
                out_tr(H - 1, fills_before(UNITS))

    B8 = range(DEC_B)
    PE_STEPS = (["tok_d", "tok_m", "new0", "new1"] + [("kt", 0)] + [x for b in B8[1:] for x in (("sc", b - 1), ("kt", b))] + [("sc", DEC_B - 1)]
                + ["rows0", "rows1", "pt0", "pt1", "pv", "o_rows", "o_cols"]
                + ["s_m", "num1"] + [("ct", 0)] + [x for b in B8[1:] for x in (("cq", b - 1), ("ct", b))] + [("cq", DEC_B - 1)]
                + ["num2", "n_new", "h_cols"] + [("cu", b) for b in B8])
    ACT_STEPS = (["tok_k", "tok_v", "tok_q", "tok_mk", "tok_mv", "o_gate"] + [("kt", b) for b in B8]
                 + ["sd0", "sd1", "exp0", "exp1", "pt0", "ptn0", "pt1", "ptn1", "o_t", "sq"]
                 + [("d", h) for h in range(H)] + [("ct", b) for b in B8] + ["num2_t"]
                 + [("sq", h) for h in range(H)])
    DVE_STEPS = (["one", "new0", "new1"]
                 + [x + str(g) for g in range(2) for x in ("max", "nmax", "rsum", "norm")]
                 + ["at0", "at1"] + [("atn", h) for h in range(H)] + ["o_rows", "o_ms", "o_nrm"]
                 + [("hd", h) for h in range(H)] + ["negg", "wm", "w", "num1a", "num1b", "nq", "nqs", "nqi"]
                 + [("num", h) for h in range(H)] + ["den", "abs", "max", "rec", "h", "ms", "hn"]
                 + [("hm", h) for h in range(H)]
                 + [x for b in B8 for x in (("kw", b), ("cd", b), ("ca", b))] + ["nd", "nn"])
    POOL_STEPS = ["pow_o", "pow_h"]

    d_small = sem("d_small")
    d_zs = sem("d_zs")
    d_tables = sem("d_tables")
    d_kl = [sem("d_kl0"), sem("d_kl1")]
    d_vl = sem("d_vl")
    d_c = sem("d_c")
    d_st = sem("d_stored")
    pes, acs, dvs, pos = (Steps("d_pe", PE_STEPS), Steps("d_act", ACT_STEPS), Steps("d_dve", DVE_STEPS),
                          Steps("d_pool", POOL_STEPS))
    TILEG = TILEM + MZ_TILES
    GATE_TILES = GATE_CHUNKS * PER_CHUNK
    AT_TOK, AT_K, AT_ROWS, AT_PT, AT_PV = 5, 7, 16, 17, 18
    AT_O = AT_PV + DEC_B
    AT_M, AT_C = AT_O + 1, AT_O + 2
    AT_N2, AT_CU = AT_C + DEC_B + 1, AT_C + DEC_B + 4
    PROJ0, TILE4 = GATE0 + GATE_CHUNKS, TILEG + GATE_TILES
    BG = 6
    gate_evac = sem("gate_evac")
    gate_stored = [sem("gate_stored0"), sem("gate_stored1")]
    NEWC = NPG * PAGE
    NK = NEWC + TS
    with ExitStack() as scope:
        cur[0] = scope
        zs = sb("zs", [P, 28, TS])
        table = sb("table", [1, DEC_B * NPG], I32)
        big = sb("big", [P, DEC_B, H, P])
        big_v = big[:].rearrange("p b h k -> p (b h k)")
        HB = NPG * H * P
        k_pg = big_v[:, 0:2 * HB].rearrange("p (s g n) -> p s g n", s=2, g=NPG)
        kt = big_v[:, 2 * HB:4 * HB].rearrange("p (s g h k) -> p s g h k", s=2, g=NPG, h=H)
        C = big
        v_pg = sb("v_pg", [P, DEC_B, NPG, H * P])
        ks_tok = sb("ks_tok", [TS, H, P])
        vs_tok = sb("vs_tok", [TS, H, P])
        q_tok = sb("q_tok", [TS, H, P])
        mk_tok = sb("mk_tok", [TS, H, P])
        mv_tok = sb("mv_tok", [TS, H, PV1])
        new_t = sb("new_t", [TS, DEC_B, H, 2, DEC_T])
        s_sb = sb("s_sb", [P, NPG, DEC_B, H, 2, DEC_T])
        e_s = sb("e_s", [P, 2, NK])
        sm = sb("sm", [P, 2, 4])
        pt = sb("pt", [P, 2, NPG, P])
        ptn = sb("ptn", [TS, 2, P])
        at = sb("at", [P, 2 * NPG * 4 * H, DEC_T])
        atn = sb("atn", [TS, H, TS])
        o_t = sb("o_t", [P, P])
        o_r = sb("o_r", [P, P])
        o_s = sb("o_s", [P, 3])
        squashed = sb("squashed", [P, 2, TB])
        junk = sb("junk", [P, P], mybir.dt.bfloat16)
        colq = sb("colq", [TS, 5, H])
        g_bc = sb("g_bc", [TS, H, TS])
        dec_bc = sb("dec_bc", [P, H, DEC_B])
        dec8 = sb("dec8", [DEC_B, H])
        d_s = sb("d_s", [TS, H, TS])
        w_s = sb("w_s", [TS, H, TS])
        wm = sb("wm", [TS, DEC_B, H])
        ct = v_pg[:, 0, :, :].rearrange("p s (h k) -> p s h k", h=H)
        kw = v_pg[0:TS, 1, :, :].rearrange("p s (h k) -> p s h k", h=H)
        n_tok = sb("n_tok", [TS, H, P])
        n8 = sb("n8", [DEC_B, H, P])
        num1 = sb("num1", [TS, H, PV1])
        num2 = sb("num2", [P, H, TS])
        nq = sb("nq", [TS, 4, H])

        with nc.Block() as block:
            def counted(part):
                at_ = [0]

                def until(n):
                    for t in range(at_[0], n):
                        part(t)
                    at_[0] = max(at_[0], n)
                return until

            def behind(t):
                return GATE0 + (t - 1) // PER_CHUNK + 1 if (t - 1) % PER_CHUNK == 0 else None

            @block.sync
            def _(sp):
                def gates(t):
                    if t >= 1:
                        c, j, b = (t - 1) // PER_CHUNK, (t - 1) // NTB % 2, (t - 1) % NTB
                        sp.wait_ge(gate_evac, t)
                        sp.dma_start(ZT[Z_GM + 2 * c + j, :, b * TB:(b + 1) * TB], squashed[:, (t - 1) % 2, :])\
                            .then_inc(gate_stored[(t - 1) % 2], 16)
                        n = behind(t)
                        if n is not None and n + 2 < PROJ0 + 2:
                            if n + 2 < PROJ0:
                                load_chunk(sp, n % 2, w_cols(I["w_in"][0], GATE_COL + (n + 2 - GATE0) * NC_), KT, n + 1)
                            else:
                                src = (I["w_proj_m"][0], I["w_proj_d"][0])[n % 2].rearrange("(k p) n -> p k n", p=P)
                                load_chunk(sp, n % 2, src[:, :, 0:CW // 4], W_MIX // P, n + 1)

                until = counted(gates)
                sp.dma_start(table[:], I["page_table"].rearrange("b g -> (b g)").unsqueeze(0)).then_inc(d_tables, 16)
                sp.dma_start(zs[:], ZT[0:28, :, SEQ:T].rearrange("a p t -> p a t")).then_inc(d_zs, 16)
                sp.wait_ge(d_tables, 16)
                load_chunk(sp, 0, w_cols(I["w_in"][0], GATE_COL + 2 * NC_), KT, GATE0 + 1)
                n_pool = I["cache_k"].shape[1]
                for b in range(DEC_B):
                    until(b + 2 if b < 2 else AT_K + b - 2)
                    if b >= 2:
                        pes.wait(sp, ("kt", b - 2))
                    for g in range(NPG):
                        page = sp.value_load(table[0:1, NPG * b + g:NPG * b + g + 1], min_val=0, max_val=n_pool - 1)
                        for dst, src, s in ((k_pg[:, b % 2, g, :], I["cache_k"], d_kl[b % 2]), (v_pg[:, b, g, :], I["cache_v"], d_vl)):
                            sp.dma_start(dst, src[0].rearrange("a p h d -> a p (h d)")[bass.ds(page, 1), :, :]
                                         .rearrange("a p n -> p (a n)")).then_inc(s, 16)
                until(AT_K + DEC_B)
                acs.wait(sp, "tok_v")
                sp.dma_start(O["k_sample"][0].rearrange("b t h d -> (b t) h d"), ks_tok[:]).then_inc(d_st, 16)
                sp.dma_start(O["v_sample"][0].rearrange("b t h d -> (b t) h d"), vs_tok[:]).then_inc(d_st, 16)
                for b in range(DEC_B):
                    until(AT_CU + b + 1)
                    dvs.wait(sp, ("ca", b))
                    sp.dma_start(O["C_sample"][0, b].rearrange("h v d -> v h d"), C[:, b, :, :]).then_inc(d_st, 16)
                dvs.wait(sp, "nn")
                sp.dma_start(O["n_sample"][0], n8[:]).then_inc(d_st, 16)
                until(GATE_TILES + 1)
                sp.wait_ge(d_st, 16 * 11)
                for i in range(2):
                    sp.wait_ge(gate_stored[i], 8 * GATE_TILES)

            @block.gpsimd
            def _(pool):
                dvs.wait(pool, "o_ms")
                pos.done(pool.tensor_tensor(o_s[:, 2:3], o_s[:, 1:2], minus_half[:, 0:1], ALU.pow), "pow_o")
                dvs.wait(pool, "ms")
                pos.done(pool.tensor_tensor(nq[:, 3, :], nq[:, 2, :], minus_half[0:TS, 0:H], ALU.pow), "pow_h")

            @block.scalar
            def _(act):
                act.dma_start(colq[:], ROWD.rearrange("q h t -> t q h").unsqueeze(3)).then_inc(d_small, 16)
                act.dma_start(g_bc[:], ROWD[Q_G].unsqueeze(0).broadcast_to((TS, H, TS))).then_inc(d_small, 16)
                act.dma_start(dec_bc[:], DECD[0].rearrange("(h b) -> h b", h=H).unsqueeze(0).broadcast_to((P, H, DEC_B))).then_inc(d_small, 16)
                act.dma_start(dec8[:], DECD[0].rearrange("(h b) -> b h", h=H).unsqueeze(2)).then_inc(d_small, 16)
                act.dma_start(n_tok[:], I["state_n"][0].unsqueeze(1).broadcast_to((DEC_B, DEC_T, H, P))).then_inc(d_small, 16)
                act.dma_start(n8[:], I["state_n"][0]).then_inc(d_small, 16)

                def gates(t):
                    if t >= 1:
                        act.wait_ge(tile_done, TILEG + t)
                        if t > 2:
                            act.wait_ge(gate_stored[(t - 1) % 2], 16 * ((t - 1) // 2))
                        act.activation(squashed[:, (t - 1) % 2, :], ps[:, BG + (t - 1) % 2, 0:TB], ACT.Sigmoid).then_inc(gate_evac, 1)
                        n = behind(t)
                        if n is not None:
                            split_hi(act, n % 2, loads_of(n), TILEG + t - 1)

                until = counted(gates)

                def load_states():
                    pes.wait(act, ("sc", DEC_B - 1))
                    for b in range(0, DEC_B, 2):
                        act.dma_start(C[:, b:b + 2, :, :], I["state_C"][0, b:b + 2].rearrange("b h v d -> v (b h) d")).then_inc(d_c, 16)

                def bank(n, rows, cols_):
                    return ps[0:rows, n, 0:cols_]

                until(AT_TOK)
                pes.wait(act, "tok_d")
                acs.done(act.activation(ks_tok[:], bank(0, TS, 512).rearrange("p (h d) -> p h d", h=H), ACT.Copy), "tok_k")
                acs.done(act.activation(vs_tok[:], bank(1, TS, 512).rearrange("p (h d) -> p h d", h=H), ACT.Copy), "tok_v")
                pes.wait(act, "tok_m")
                acs.done(act.activation(q_tok[:], bank(2, TS, 512).rearrange("p (h d) -> p h d", h=H), ACT.Copy), "tok_q")
                acs.done(act.activation(mk_tok[:], bank(3, TS, 512).rearrange("p (h d) -> p h d", h=H), ACT.Copy,
                                        scale=SCALE_M), "tok_mk")
                acs.done(act.activation(mv_tok[:, :, 0:DH], bank(4, TS, 512).rearrange("p (h d) -> p h d", h=H), ACT.Copy), "tok_mv")
                acs.done(act.activation(zs[:, Z_MO:Z_MO + H, :], zs[:, Z_MO:Z_MO + H, :], ACT.Sigmoid), "o_gate")
                for b in B8:
                    until(AT_K + b)
                    pes.wait(act, ("kt", b))
                    if b >= 2:
                        pes.wait(act, ("sc", b - 2))
                    k0 = 2 * (b % 2)
                    acs.done(act.activation(kt[:, b % 2, :, :, :], ps[:, k0:k0 + 2, :].rearrange("p g (h k) -> p g h k", h=H), ACT.Copy),
                             ("kt", b))
                until(AT_K + DEC_B)
                load_states()
                for m, bk in ((0, 4), (1, 5)):
                    acs.done(act.activation(s_sb[:, :, :, :, m, :].rearrange("p g b h t -> p (g b h) t"),
                                            ps[:, bk, 0:NPG * DEC_B * H * DEC_T].rearrange("p (a t) -> p a t", t=DEC_T), ACT.Copy), f"sd{m}")
                until(AT_ROWS)
                for g in range(2):
                    dvs.wait(act, f"nmax{g}")
                    acs.done(act.activation(e_s[:, g, :], ps[:, g, 0:NK], ACT.Exp, bias=sm[:, g, 1:2], scale=SCALE_D,
                                            accum_out=sm[:, g, 2:3]), f"exp{g}")
                until(AT_PT)
                for g in range(2):
                    pes.wait(act, f"pt{g}")
                    acs.done(act.activation(pt[:, g, :, :], ps[:, 2 + g, 0:NPG * P].rearrange("p (g k) -> p g k", g=NPG), ACT.Copy), f"pt{g}")
                    acs.done(act.activation(ptn[:, g, :], ps[0:TS, 2 + g, NPG * P:(NPG + 1) * P], ACT.Copy), f"ptn{g}")
                until(AT_O - 1)
                pes.wait(act, "pv")
                acs.done(act.activation(o_t[:], ps[:, 5, 0:P], ACT.Copy), "o_t")
                until(AT_O)
                dvs.wait(act, "o_rows")
                acs.done(act.activation(junk[:], o_r[:], ACT.Square, accum_out=o_s[:, 0:1]), "sq")
                until(AT_M)
                dvs.wait(act, "negg")
                for h in range(H):
                    acs.done(act.activation(d_s[:, h, :], g_bc[:, h, :], ACT.Exp, bias=colq[:, Q_A, h:h + 1]), ("d", h))
                for b in B8:
                    until(AT_C + b)
                    pes.wait(act, ("ct", b))
                    if b >= 2:
                        pes.wait(act, ("cq", b - 2))
                    acs.done(act.activation(ct[:, b % 2, :, :], ps[:, b % 2, :].rearrange("p (h k) -> p h k", h=H), ACT.Copy), ("ct", b))
                until(AT_C + DEC_B)
                pes.wait(act, ("cq", DEC_B - 1))
                acs.done(act.activation(num2[:], ps[:, 5, 0:H * TS].rearrange("p (h t) -> p h t", h=H), ACT.Copy), "num2_t")
                until(AT_N2)
                dvs.wait(act, "h")
                for h in range(H):
                    acs.wait(act, ("sq", h - 1) if h else "num2_t")
                    acs.done(act.activation(junk[0:TS, :], num1[:, h, 0:DH], ACT.Square, accum_out=nq[:, 1, h:h + 1]), ("sq", h))
                until(GATE_TILES + 1)

            @block.vector
            def _(dve):
                def gates(t):
                    if t >= 1 and behind(t) is not None:
                        split_lo(dve, behind(t) % 2, behind(t) + 1)

                until = counted(gates)
                dvs.done(dve.memset(mv_tok[:, :, DH:PV1], 1.0), "one")
                until(AT_TOK)
                for m in range(2):
                    until(AT_TOK + m)
                    pes.wait(dve, f"new{m}")
                    dvs.done(dve.tensor_tensor(new_t[:, :, :, m, :].rearrange("p b h t -> p h b t"),
                                               ps[0:TS, (5, 0)[m], 0:H * TS].rearrange("p (h b t) -> p h b t", h=H, b=DEC_B),
                                               mask_n[:].rearrange("p (b t) -> p b t", b=DEC_B).unsqueeze(1)
                                               .broadcast_to((TS, H, DEC_B, DEC_T)), ALU.add), f"new{m}")
                until(AT_ROWS)
                for g in range(2):
                    pes.wait(dve, f"rows{g}")
                    dvs.done(dve.tensor_reduce(sm[:, g, 0:1], ps[:, g, 0:NK], AX_X, ALU.max), f"max{g}")
                    dvs.wait(dve, f"max{g}")
                    dvs.done(dve.tensor_scalar(sm[:, g, 1:2], sm[:, g, 0:1], -SCALE_D, None, ALU.mult), f"nmax{g}")
                    acs.wait(dve, f"exp{g}")
                    dvs.done(dve.reciprocal(sm[:, g, 3:4], sm[:, g, 2:3]), f"rsum{g}")
                    dvs.wait(dve, f"rsum{g}")
                    dvs.done(dve.tensor_scalar(e_s[:, g, :], e_s[:, g, :], sm[:, g, 3:4], None, ALU.mult), f"norm{g}")
                until(AT_PT)
                for g in range(2):
                    acs.wait(dve, f"ptn{g}")
                    v = pt[:, g, :, :].rearrange("p g (a m t) -> p (g a) m t", m=2, t=DEC_T)
                    dvs.done(dve.scalar_tensor_tensor(out=at[:, 32 * g:32 * g + 32, :], in0=v[:, :, 1, :], scalar=neg_lam[:],
                                                      in1=v[:, :, 0, :], op0=ALU.mult, op1=ALU.add), f"at{g}")
                vn = ptn[:].rearrange("p g (b h m t) -> p (g b) h m t", b=4, h=H, m=2)
                for h in range(H):
                    dvs.done(dve.scalar_tensor_tensor(out=atn[:, h, :].rearrange("p (b t) -> p b t", t=DEC_T), in0=vn[:, :, h, 1, :],
                                                      scalar=neg_lam[0:TS], in1=vn[:, :, h, 0, :],
                                                      op0=ALU.mult, op1=ALU.add), ("atn", h))
                until(AT_O)
                pes.wait(dve, "o_rows")
                dvs.done(dve.tensor_copy(o_r[:], ps[:, 0, 0:P]), "o_rows")
                acs.wait(dve, "sq")
                dvs.done(dve.tensor_scalar(o_s[:, 1:2], o_s[:, 0:1], 1.0 / DH, EPS, ALU.mult, ALU.add), "o_ms")
                pos.wait(dve, "pow_o")
                dvs.done(dve.tensor_scalar(o_r[:], o_r[:], o_s[:, 2:3], None, ALU.mult), "o_nrm")
                until(AT_M)
                pes.wait(dve, "o_cols")
                for h in range(H):
                    dvs.done(dve.tensor_scalar(branch_s[:, H + h, :], ps[:, 1, h * TS:(h + 1) * TS], gain_t[:, H + h:H + h + 1], None, ALU.mult), ("hd", h))

                dve.wait_ge(d_small, 16 * 6)
                dvs.done(dve.tensor_tensor(g_bc[:], mask_n[:].unsqueeze(1).broadcast_to((TS, H, TS)), g_bc[:], ALU.subtract), "negg")
                dvs.done(dve.tensor_tensor(wm[:], same_seq[:].unsqueeze(2).broadcast_to((TS, DEC_B, H)),
                                           colq[:, Q_WEND, :].unsqueeze(1).broadcast_to((TS, DEC_B, H)), ALU.mult), "wm")
                pes.wait(dve, "s_m")
                acs.wait(dve, ("d", H - 1))
                dvs.done(dve.scalar_tensor_tensor(out=w_s[:].rearrange("p h t -> p (h t)"), in0=ps[0:TS, 4, 0:H * TS], scalar=SCALE_M,
                                                  in1=d_s[:].rearrange("p h t -> p (h t)"), op0=ALU.mult, op1=ALU.mult), "w")
                until(AT_C)
                pes.wait(dve, "num1")
                dvs.done(dve.tensor_copy(num1[:, 0:3, :], ps[0:TS, 2, 0:3 * PV1].rearrange("p (h v) -> p h v", h=3)), "num1a")
                dvs.done(dve.tensor_copy(num1[:, 3, :], ps[0:TS, 3, 0:PV1]), "num1b")
                acs.wait(dve, "tok_q")
                dvs.done(dve.tensor_tensor(q_tok[:], q_tok[:], n_tok[:], ALU.mult), "nq")
                dvs.wait(dve, "nq")
                dvs.done(dve.tensor_reduce(nq[:, 0, :], q_tok[:], AX_X, ALU.add), "nqs")
                dvs.wait(dve, "nqs")
                dvs.done(dve.tensor_tensor(nq[:, 0, :], nq[:, 0, :], colq[:, Q_INTER, :], ALU.mult), "nqi")
                until(AT_N2)
                pes.wait(dve, "num2")
                for h in range(H):
                    dvs.done(dve.scalar_tensor_tensor(out=num1[:, h, 0:DH], in0=ps[0:TS, 4, h * P:(h + 1) * P],
                                                      scalar=colq[:, Q_INTER, h:h + 1], in1=num1[:, h, 0:DH],
                                                      op0=ALU.mult, op1=ALU.add), ("num", h))
                dvs.wait(dve, ("num", H - 1))
                dvs.done(dve.tensor_tensor(nq[:, 0, :], nq[:, 0, :], num1[:, :, DH], ALU.add), "den")
                dvs.wait(dve, "den")
                dvs.done(dve.scalar_tensor_tensor(out=nq[:, 1, :], in0=nq[:, 0, :], scalar=-1.0, in1=nq[:, 0, :],
                                                  op0=ALU.mult, op1=ALU.max), "abs")
                dvs.wait(dve, "abs")
                dvs.done(dve.tensor_tensor(nq[:, 1, :], nq[:, 1, :], colq[:, Q_EMT, :], ALU.max), "max")
                dvs.wait(dve, "max")
                dvs.done(dve.reciprocal(nq[:, 2, :], nq[:, 1, :]), "rec")
                dvs.wait(dve, "rec")
                dvs.done(dve.tensor_tensor(num1[:, :, 0:DH], num1[:, :, 0:DH], nq[:, 2, :].unsqueeze(2).broadcast_to((TS, H, DH)),
                                           ALU.mult), "h")
                acs.wait(dve, ("sq", H - 1))
                dvs.done(dve.tensor_scalar(nq[:, 2, :], nq[:, 1, :], 1.0 / DH, EPS, ALU.mult, ALU.add), "ms")
                pos.wait(dve, "pow_h")
                dvs.done(dve.tensor_tensor(num1[:, :, 0:DH], num1[:, :, 0:DH], nq[:, 3, :].unsqueeze(2).broadcast_to((TS, H, DH)),
                                           ALU.mult), "hn")
                until(AT_N2 + 2)
                pes.wait(dve, "h_cols")
                for h in range(H):
                    dvs.done(dve.scalar_tensor_tensor(out=branch_s[:, h, :], in0=ps[:, 2, h * TS:(h + 1) * TS], scalar=gain_t[:, h:h + 1],
                                                      in1=zs[:, Z_MO + h, :], op0=ALU.mult, op1=ALU.mult), ("hm", h))
                dve.wait_ge(d_c, 64)
                for b in B8:
                    until(AT_CU + b - 1)
                    if b >= 2:
                        pes.wait(dve, ("cu", b - 2))
                    dvs.done(dve.tensor_tensor(kw[:, b % 2, :, :], mk_tok[:], wm[:, b, :].unsqueeze(2).broadcast_to((TS, H, P)), ALU.mult),
                             ("kw", b))
                    dvs.done(dve.tensor_tensor(C[:, b, :, :], C[:, b, :, :], dec_bc[:, :, b].unsqueeze(2).broadcast_to((P, H, P)), ALU.mult),
                             ("cd", b))
                    until(AT_CU + b)
                    pes.wait(dve, ("cu", b))
                    dvs.wait(dve, ("cd", b))
                    dvs.done(dve.tensor_tensor(C[:, b, :, :], C[:, b, :, :], ps[:, b % 2, :].rearrange("p (h k) -> p h k", h=H), ALU.add),
                             ("ca", b))
                dvs.done(dve.tensor_tensor(n8[:], n8[:], dec8[:].unsqueeze(2).broadcast_to((DEC_B, H, P)), ALU.mult), "nd")
                dvs.wait(dve, "nd")
                dvs.done(dve.tensor_tensor(n8[:], n8[:], ps[0:DEC_B, 3, :].rearrange("p (h k) -> p h k", h=H), ALU.add), "nn")
                until(GATE_TILES)

            @block.tensor
            def _(pe):
                def gates(t):
                    c, j, b = t // PER_CHUNK, t // NTB % 2, t % NTB
                    if t % PER_CHUNK == 0:
                        pe.wait_ge(w_lo_ready, GATE0 + c + 1)
                    if t >= 2:
                        pe.wait_ge(gate_evac, t - 1)
                    w = [x[:, c % 2, :].rearrange("p (k n) -> p k n", k=KT) for x in (w_hi, w_lo)]
                    order = products(KT)
                    for n, (k, wi, ai) in enumerate(order):
                        mm = pe.matmul(ps[:, BG + t % 2, 0:TB], w[wi][:, k, j * P:(j + 1) * P],
                                       (acts_hi, acts_lo)[ai][:, k, b * TB:(b + 1) * TB],
                                       start=(n == 0), stop=(n == len(order) - 1))
                    mm.then_inc(tile_done, 1)

                until = counted(gates)
                until(AT_TOK)
                pe.wait_ge(d_zs, 16)
                for bk, z in enumerate((Z_DK, Z_DV, Z_MQ, Z_MK, Z_MV)):
                    for h in range(H):
                        tr = pe.transpose(ps[0:TS, bk, h * P:(h + 1) * P], zs[:, z + h, :], ident[:])
                    if bk in (1, 4):
                        pes.done(tr, "tok_d" if bk == 1 else "tok_m")
                for m in range(2):
                    if m:
                        until(AT_TOK + 1)
                        acs.wait(pe, "tok_k")
                    for h in range(H):
                        mm = pe.matmul(ps[0:TS, (5, 0)[m], h * TS:(h + 1) * TS], zs[m * DQK:(m + 1) * DQK, Z_DK + h, :],
                                       zs[m * DQK:(m + 1) * DQK, Z_DQ + h, :], start=True, stop=True)
                    pes.done(mm, f"new{m}")
                acs.wait(pe, "tok_mv")
                dvs.wait(pe, "new1")

                def k_transposes(b):
                    pe.wait_ge(d_kl[b % 2], 16 * NPG * (b // 2 + 1))
                    if b >= 2:
                        acs.wait(pe, ("kt", b - 2))
                    for g in range(NPG):
                        for h in range(H):
                            tr = pe.transpose(ps[:, 2 * (b % 2) + g, h * P:(h + 1) * P], k_pg[:, b % 2, g, h * P:(h + 1) * P], ident[:])
                    pes.done(tr, ("kt", b))

                def scores(b):
                    acs.wait(pe, ("kt", b))
                    for m, bk in ((0, 4), (1, 5)):
                        for g in range(NPG):
                            for h in range(H):
                                c0 = ((g * DEC_B + b) * H + h) * DEC_T
                                mm = pe.matmul(ps[:, bk, c0:c0 + DEC_T], kt[m * DQK:(m + 1) * DQK, b % 2, g, h, :],
                                               zs[m * DQK:(m + 1) * DQK, Z_DQ + h, DEC_T * b:DEC_T * (b + 1)], start=True, stop=True)
                    pes.done(mm, ("sc", b))

                for b in B8:
                    until(AT_K + b)
                    if b:
                        scores(b - 1)
                    k_transposes(b)
                until(AT_K + DEC_B)
                scores(DEC_B - 1)
                until(AT_ROWS)
                acs.wait(pe, "sd1")
                for g in range(2):
                    for pg in range(NPG):
                        pe.transpose(ps[:, g, pg * P:(pg + 1) * P], s_sb[:, pg, 4 * g:4 * g + 4, :, :, :].rearrange("p b h m t -> p (b h m t)"),
                                     ident[:])
                    pes.done(pe.transpose(ps[:, g, NEWC:NK], new_t[:, 4 * g:4 * g + 4, :, :, :].rearrange("p b h m t -> p (b h m t)"),
                                          ident[0:TS, 0:TS]), f"rows{g}")
                until(AT_PT)
                for g in range(2):
                    dvs.wait(pe, f"norm{g}")
                    for pg in range(NPG):
                        pe.transpose(ps[:, 2 + g, pg * P:(pg + 1) * P], e_s[:, g, pg * P:(pg + 1) * P], ident[:])
                    pes.done(pe.transpose(ps[0:TS, 2 + g, NPG * P:(NPG + 1) * P], e_s[:, g, NEWC:NK], ident[:]), f"pt{g}")
                until(AT_PV)
                dvs.wait(pe, ("atn", H - 1))
                pe.wait_ge(d_vl, 16 * NPG * DEC_B)
                for h in range(H):
                    pe.matmul(ps[:, 5, h * TS:(h + 1) * TS], vs_tok[:, h, :], atn[:, h, :], start=(h == 0), stop=False, skip_group_check=True)
                for b in B8:
                    until(AT_PV + b)
                    for pg in range(NPG):
                        for h in range(H):
                            a = ((b // 4 * NPG + pg) * 4 + b % 4) * H + h
                            mm = pe.matmul(ps[:, 5, h * TS + DEC_T * b:h * TS + DEC_T * (b + 1)], v_pg[:, b, pg, h * P:(h + 1) * P],
                                           at[:, a, :], start=False, stop=(pg == NPG - 1), skip_group_check=True)
                pes.done(mm, "pv")
                until(AT_O)
                acs.wait(pe, "o_t")
                pes.done(pe.transpose(ps[:, 0, 0:P], o_t[:], ident[:]), "o_rows")
                until(AT_M)
                dvs.wait(pe, "o_nrm")
                pes.done(pe.transpose(ps[:, 1, 0:P], o_r[:], ident[:]), "o_cols")

                for h in range(H):
                    mm = pe.matmul(ps[0:TS, 4, h * TS:(h + 1) * TS], zs[:, Z_MK + h, :], zs[:, Z_MQ + h, :], start=True, stop=True)
                pes.done(mm, "s_m")
                until(AT_C)
                dvs.wait(pe, "w")
                for h in range(H):
                    mm = pe.matmul(ps[0:TS, 2 + h // 3, h % 3 * PV1:h % 3 * PV1 + PV1], w_s[:, h, :], mv_tok[:, h, :], start=True, stop=True)
                pes.done(mm, "num1")
                pe.wait_ge(d_c, 64)

                def state_q(b):
                    acs.wait(pe, ("ct", b))
                    for h in range(H):
                        mm = pe.matmul(ps[:, 5, h * TS + DEC_T * b:h * TS + DEC_T * (b + 1)], ct[:, b % 2, h, :],
                                       zs[:, Z_MQ + h, DEC_T * b:DEC_T * (b + 1)], start=True, stop=True)
                    pes.done(mm, ("cq", b))

                for b in B8:
                    until(AT_C + b)
                    if b:
                        state_q(b - 1)
                    if b == 1:
                        dvs.wait(pe, ("hd", H - 1))
                    if b >= 2:
                        acs.wait(pe, ("ct", b - 2))
                    for h in range(H):
                        tr = pe.transpose(ps[:, b % 2, h * P:(h + 1) * P], C[:, b, h, :], ident[:])
                    pes.done(tr, ("ct", b))
                until(AT_C + DEC_B)
                state_q(DEC_B - 1)
                until(AT_N2)
                acs.wait(pe, "num2_t")
                for h in range(H):
                    tr = pe.transpose(ps[0:TS, 4, h * P:(h + 1) * P], num2[:, h, :], ident[:])
                pes.done(tr, "num2")
                dvs.wait(pe, "num1b")
                for h in range(H):
                    mm = pe.matmul(ps[0:DEC_B, 3, h * P:(h + 1) * P], wm[:, :, h], mk_tok[:, h, :], start=True, stop=True)
                pes.done(mm, "n_new")
                until(AT_N2 + 2)
                dvs.wait(pe, "hn")
                for h in range(H):
                    tr = pe.transpose(ps[:, 2, h * TS:(h + 1) * TS], num1[:, h, 0:DH], ident[0:TS, 0:TS])
                pes.done(tr, "h_cols")
                for b in B8:
                    until(AT_CU + b)
                    dvs.wait(pe, ("kw", b))
                    if b >= 2:
                        dvs.wait(pe, ("ca", b - 2))
                    for h in range(H):
                        mm = pe.matmul(ps[:, b % 2, h * P:(h + 1) * P], mv_tok[:, h, 0:DH], kw[:, b % 2, h, :], start=True, stop=True)
                    pes.done(mm, ("cu", b))
                until(GATE_TILES)

    CH = range(NCH)

    NPE_STEPS = ([("kT", 0), ("vT", 0), ("s", 0)]
                 + [x for c in CH for x in (([("kT", c + 1), ("vT", c + 1), ("s", c + 1)] if c + 1 < NCH else [])
                                            + [("num", c), ("cu", c)] + ([("o_tr", c - 1)] if c else []))]
                 + [("o_tr", NCH - 1), "c_tr"])
    NACT_STEPS = ([("v", 0), ("d", 0), ("v", 1), ("d", 1)] + [x for h in range(H) for x in (("mo", h), ("mog", h))]
                  + [x for c in CH for x in (([("v", c + 1), ("d", c + 1)] if 1 <= c < NCH - 1 else [])
                                             + [("sq", c)] + ([("hi", c - 1)] if c else [])
                                             + ([("br", c)] if c < H else []))]
                  + [("hi", NCH - 1), "c_out"])
    NDVE_STEPS = (["ones", ("kw", 0), ("w", 0)]
                  + [x for c in CH for x in (([("kw", c + 1)] if c + 1 < NCH else [])
                                             + [("st", c), ("neg", c), ("abs", c), ("floor", c), ("rec", c), ("h", c)]
                                             + ([("w", c + 1)] if c + 1 < NCH else [])
                                             + ([("cols", c - 1)] if c else []) + [("ssum", c), ("ms", c)]
                                             + ([("lo", c - 1)] if c else []) + [("hn", c)]
                                             + ([("br", c)] if c < H else []))]
                  + [("cols", NCH - 1), ("lo", NCH - 1)])
    NPOOL_STEPS = ([("neg", 0), ("nega", 0), ("neg", 1), ("nega", 1), ("qi", 1)]
                   + [x for c in CH for x in (([("cd", c + 1)] if c + 1 < NCH else []) + [("pow", c)]
                                              + ([("neg", c + 2), ("nega", c + 2), ("qi", c + 2)] if c + 2 < NCH else []))])
    npe, nac, ndv, npo = (Steps("n_pe", NPE_STEPS), Steps("n_act", NACT_STEPS), Steps("n_dve", NDVE_STEPS),
                          Steps("n_pool", NPOOL_STEPS))
    n_mo = sem("n_mo")
    n_br = [sem("n_br0"), sem("n_br1")]
    n_l = [sem(f"n_l{i}") for i in range(3)]
    n_st = sem("n_st")
    with ExitStack() as scope:
        cur[0] = scope
        mo_g = sb("mo_g", [P, H, SEQ])
        br_d = sb("br_d", [P, 2, SEQ])
        LS = 3
        mq, mk, mv = (sb(f"z_m{x}", [P, LS, H, P]) for x in "qkv")
        g_bc = sb("g_chunk", [P, LS, H, P])
        i_bc = sb("i_chunk", [P, LS, H, P])
        k_w = sb("k_w", [P, 2, H, P])
        v_1 = sb("v_1", [P, 2, H, PV1])
        w_t = sb("w_t", [P, 2, H, P])
        c_st = sb("c_st", [P, 2, H, PV1])
        c_dec = sb("c_dec", [P, H, PV1])
        den = sb("den", [P, 2, 4, H])
        mix = sb("mix_m", [P, 2, H, DH])
        sqj = sb("sq_m", [P, H, DH])
        cols = sb("cols_m", [P, 2, H, P])
        c_out = sqj
        BK, BV, BS, BN, BC, BO = 0, 1, 2, 3, 5, 7

        def col(q, c):
            return rows_t[:, q, :].rearrange("p (h c) -> p h c", h=H)[:, :, c]

        def over(ap, n):
            return ap.unsqueeze(2).broadcast_to((P, H, n))

        def flat(ap):
            return ap.rearrange("p h k -> p (h k)")

        def bank4(b):
            return ps[:, b, :].rearrange("p (h k) -> p h k", h=H)

        def pair_banks(b, n):
            return ps[:, b:b + 2, 0:2 * PV1].rearrange("p g (h v) -> p g h v", h=2)[:, :, :, 0:n]

        def by_pair(ap):
            return ap.rearrange("p (g h) v -> p g h v", g=2)

        with nc.Block() as block:
            @block.sync
            def _(sp):
                def load(c):
                    s = c % LS
                    for dst, z in ((mk, Z_MK), (mv, Z_MV), (mq, Z_MQ)):
                        sp.dma_start(dst[:, s], ZT[z:z + H, :, c * P:(c + 1) * P].rearrange("h p t -> p h t")).then_inc(n_l[s], 16)
                    for dst, q in ((g_bc, Q_G), (i_bc, Q_INTER)):
                        sp.dma_start(dst[:, s], ROWS[q, :, c * P:(c + 1) * P].unsqueeze(0).broadcast_to((P, H, P))).then_inc(n_l[s], 16)

                for c in range(LS):
                    load(c)
                for c in range(2, H):
                    ndv.wait(sp, ("br", c - 2))
                    sp.dma_start(br_d[:, c % 2], BRANCH[c]).then_inc(n_br[c % 2], 16)
                    npe.wait(sp, ("num", c + 1 - LS))
                    load(c + 1)
                for c in range(H + 1, NCH):
                    npe.wait(sp, ("num", c - LS))
                    load(c)
                nac.wait(sp, "c_out")
                for h in range(H):
                    sp.dma_start(O["C_prompt"][0, 0, h], c_out[:, h]).then_inc(n_st, 16)
                sp.dma_start(O["n_prompt"][0, 0].rearrange("h d -> d h").unsqueeze(2), c_st[:, NCH % 2, :, DH:PV1]).then_inc(n_st, 16)
                sp.wait_ge(n_st, 16 * (H + 1))

            @block.gpsimd
            def _(pool):
                def exponents(c):
                    s = c % LS
                    pool.wait_ge(n_l[s], 80 * (c // LS + 1))
                    npo.done(pool.tensor_tensor(g_bc[:, s], mask_s[:].unsqueeze(1).broadcast_to((P, H, P)), g_bc[:, s], ALU.subtract), ("neg", c))
                    npo.wait(pool, ("neg", c))
                    npo.done(pool.tensor_tensor(g_bc[:, s], g_bc[:, s], over(col(Q_A, c), P), ALU.add), ("nega", c))

                def state_query(c):
                    npo.done(pool.tensor_tensor(i_bc[:, c % LS], i_bc[:, c % LS], mq[:, c % LS], ALU.mult), ("qi", c))

                exponents(0)
                exponents(1)
                state_query(1)
                for c in CH:
                    if c + 1 < NCH:
                        ndv.wait(pool, ("st", c))
                        npo.done(pool.tensor_tensor(c_dec[:], c_st[:, 1 - c % 2], decay_p[:].rearrange("p (h c) -> p h c", h=H)[:, :, c + 1]
                                                    .unsqueeze(2).broadcast_to((P, H, PV1)), ALU.mult), ("cd", c + 1))
                    ndv.wait(pool, ("ms", c))
                    npo.done(pool.tensor_tensor(den[:, c % 2, 3, :], den[:, c % 2, 2, :], minus_half[:, 0:H], ALU.pow), ("pow", c))
                    if c + 2 < NCH:
                        exponents(c + 2)
                        state_query(c + 2)

            @block.scalar
            def _(act):
                for h in range(H):
                    act.dma_start(mo_g[:, h], ZT[Z_MO + h, :, 0:SEQ]).then_inc(n_mo, 16)
                for h in range(2):
                    act.dma_start(br_d[:, h], BRANCH[h]).then_inc(n_br[h], 16)

                def out_gates(h):
                    act.wait_ge(n_mo, 16 * H)
                    nac.done(act.activation(mo_g[:, h], mo_g[:, h], ACT.Sigmoid), ("mo", h))
                    nac.wait(act, ("mo", h))
                    nac.done(act.activation(mo_g[:, h], mo_g[:, h], ACT.Copy, scale=gain_t[:, h:h + 1]), ("mog", h))

                def prepare(c):
                    s = c % 2
                    npe.wait(act, ("vT", c))
                    ndv.wait(act, "ones")
                    if c >= 2:
                        npe.wait(act, ("cu", c - 2))
                    nac.done(act.activation(v_1[:, s, :, 0:DH], bank4(BV), ACT.Copy), ("v", c))
                    npo.wait(act, ("nega", c))
                    nac.done(act.activation(flat(g_bc[:, c % LS]), flat(g_bc[:, c % LS]), ACT.Exp), ("d", c))

                prepare(0)
                prepare(1)
                for h in range(H):
                    out_gates(h)
                for c in CH:
                    s = c % 2
                    if 1 <= c < NCH - 1:
                        prepare(c + 1)
                    ndv.wait(act, ("h", c))
                    if c:
                        ndv.wait(act, ("ssum", c - 1))
                    nac.done(act.activation(flat(sqj[:]), flat(mix[:, s]), ACT.Square), ("sq", c))
                    if c:
                        ndv.wait(act, ("cols", c - 1))
                        nac.done(act.activation(acts_hi[:, 0:H, (c - 1) * P:c * P], cols[:, 1 - s], ACT.Copy), ("hi", c - 1))
                    if c < H:
                        act.wait_ge(n_br[c % 2], 16 * (c // 2 + 1))
                        nac.done(act.activation(acts_hi[:, H + c, 0:SEQ], br_d[:, c % 2], ACT.Copy), ("br", c))
                c = NCH - 1
                ndv.wait(act, ("cols", c))
                nac.done(act.activation(acts_hi[:, 0:H, c * P:(c + 1) * P], cols[:, c % 2], ACT.Copy), ("hi", c))
                npe.wait(act, "c_tr")
                nac.done(act.activation(c_out[:], bank4(BK), ACT.Copy), "c_out")

            @block.vector
            def _(dve):
                ndv.done(dve.memset(v_1[:, :, :, DH:PV1], 1.0), "ones")

                def k_weighted(c):
                    npe.wait(dve, ("kT", c))
                    if c >= 2:
                        npe.wait(dve, ("cu", c - 2))
                    ndv.done(dve.tensor_tensor(k_w[:, c % 2], bank4(BK), over(col(Q_WEND, c), P), ALU.mult), ("kw", c))

                def weights(c):
                    npe.wait(dve, ("s", c))
                    nac.wait(dve, ("d", c))
                    if c >= 2:
                        npe.wait(dve, ("num", c - 2))
                    ndv.done(dve.scalar_tensor_tensor(out=flat(w_t[:, c % 2]), in0=ps[:, BS, :], scalar=SCALE_M,
                                                      in1=flat(g_bc[:, c % LS]), op0=ALU.mult, op1=ALU.mult), ("w", c))

                def out_cols(c):
                    npe.wait(dve, ("o_tr", c))
                    nac.wait(dve, ("mog", H - 1))
                    if c >= 2:
                        ndv.wait(dve, ("lo", c - 2))
                    ndv.done(dve.tensor_tensor(cols[:, c % 2], bank4(BO), mo_g[:, :, c * P:(c + 1) * P], ALU.mult), ("cols", c))

                def out_low(c):
                    nac.wait(dve, ("hi", c))
                    ndv.done(dve.tensor_tensor(acts_lo[:, 0:H, c * P:(c + 1) * P], cols[:, c % 2],
                                               acts_hi[:, 0:H, c * P:(c + 1) * P].bitcast(F32), ALU.subtract), ("lo", c))

                k_weighted(0)
                weights(0)
                for c in CH:
                    s = c % 2
                    if c + 1 < NCH:
                        k_weighted(c + 1)
                    npe.wait(dve, ("cu", c))
                    if c:
                        npo.wait(dve, ("cd", c))
                        ndv.done(dve.tensor_tensor(by_pair(c_st[:, 1 - s]), by_pair(c_dec[:]), pair_banks(BC, PV1), ALU.add), ("st", c))
                    else:
                        ndv.done(dve.tensor_copy(by_pair(c_st[:, 1 - s]), pair_banks(BC, PV1)), ("st", c))
                    q = den[:, s]
                    dn = ps[:, BN:BN + 2, 0:2 * PV1].rearrange("p g (h v) -> p g h v", h=2)[:, :, :, DH]
                    if c >= 2:
                        ndv.wait(dve, ("hn", c - 2))
                        npe.wait(dve, ("o_tr", c - 2))
                    ndv.done(dve.tensor_scalar(q[:, 0, :].rearrange("p (g h) -> p g h", g=2), dn, -1.0, None, ALU.mult), ("neg", c))
                    ndv.wait(dve, ("neg", c))
                    ndv.done(dve.tensor_tensor(q[:, 0, :].rearrange("p (g h) -> p g h", g=2), dn,
                                               q[:, 0, :].rearrange("p (g h) -> p g h", g=2), ALU.max), ("abs", c))
                    ndv.wait(dve, ("abs", c))
                    ndv.done(dve.tensor_tensor(q[:, 0, :], q[:, 0, :], col(Q_EMT, c), ALU.max), ("floor", c))
                    ndv.wait(dve, ("floor", c))
                    ndv.done(dve.reciprocal(q[:, 1, :], q[:, 0, :]), ("rec", c))
                    ndv.wait(dve, ("rec", c))
                    ndv.done(dve.tensor_tensor(by_pair(mix[:, s]), pair_banks(BN, DH),
                                               by_pair(over(q[:, 1, :], DH)), ALU.mult), ("h", c))
                    if c + 1 < NCH:
                        weights(c + 1)
                    if c:
                        out_cols(c - 1)
                    nac.wait(dve, ("sq", c))
                    ndv.done(dve.reduce_sum(q[:, 2, :], sqj[:], AX_X), ("ssum", c))
                    ndv.wait(dve, ("ssum", c))
                    ndv.done(dve.tensor_scalar(q[:, 2, :], q[:, 2, :], 1.0 / DH, EPS, ALU.mult, ALU.add), ("ms", c))
                    if c:
                        out_low(c - 1)
                    npo.wait(dve, ("pow", c))
                    ndv.done(dve.tensor_tensor(mix[:, s], mix[:, s], over(q[:, 3, :], DH), ALU.mult), ("hn", c))
                    if c < H:
                        nac.wait(dve, ("br", c))
                        ndv.done(dve.tensor_tensor(acts_lo[:, H + c, 0:SEQ], br_d[:, c % 2], acts_hi[:, H + c, 0:SEQ].bitcast(F32),
                                                   ALU.subtract), ("br", c))
                out_cols(NCH - 1)
                out_low(NCH - 1)

            @block.tensor
            def _(pe):

                def prepare(c):
                    s = c % LS
                    pe.wait_ge(n_l[s], 80 * (c // LS + 1))
                    if c:
                        ndv.wait(pe, ("kw", c - 1))
                    for h in range(H):
                        tr = pe.transpose(ps[:, BK, h * P:(h + 1) * P], mk[:, s, h], ident[:])
                    npe.done(tr, ("kT", c))
                    if c:
                        nac.wait(pe, ("v", c - 1))
                    for h in range(H):
                        tr = pe.transpose(ps[:, BV, h * P:(h + 1) * P], mv[:, s, h], ident[:])
                    npe.done(tr, ("vT", c))
                    if c:
                        ndv.wait(pe, ("w", c - 1))
                    for h in range(H):
                        mm = pe.matmul(ps[:, BS, h * P:(h + 1) * P], mk[:, s, h], mq[:, s, h], start=True, stop=True)
                    npe.done(mm, ("s", c))

                def out_tr(c):
                    ndv.wait(pe, ("hn", c))
                    if c:
                        ndv.wait(pe, ("cols", c - 1))
                    for h in range(H):
                        tr = pe.transpose(ps[:, BO, h * P:(h + 1) * P], mix[:, c % 2, h], ident[:])
                    npe.done(tr, ("o_tr", c))

                def pair(b, h):
                    return ps[:, b + h // 2, h % 2 * PV1:h % 2 * PV1 + PV1]

                prepare(0)
                for c in CH:
                    s = c % 2
                    if c + 1 < NCH:
                        prepare(c + 1)
                    nac.wait(pe, ("v", c))
                    ndv.wait(pe, ("w", c))
                    if c:
                        ndv.wait(pe, ("h", c - 1))
                        npo.wait(pe, ("qi", c))
                    for h in range(H):
                        mm = pe.matmul(pair(BN, h), w_t[:, s, h], v_1[:, s, h], start=True, stop=(c == 0))
                        if c:
                            mm = pe.matmul(pair(BN, h), i_bc[:, c % LS, h], c_st[:, s, h], start=False, stop=True)
                    npe.done(mm, ("num", c))
                    ndv.wait(pe, ("kw", c))
                    if c:
                        ndv.wait(pe, ("st", c - 1))
                    for h in range(H):
                        mm = pe.matmul(pair(BC, h), k_w[:, s, h], v_1[:, s, h], start=True, stop=True)
                    npe.done(mm, ("cu", c))
                    if c:
                        out_tr(c - 1)
                out_tr(NCH - 1)
                for h in range(H):
                    tr = pe.transpose(ps[:, BK, h * P:(h + 1) * P], c_st[:, NCH % 2, h, 0:DH], ident[:])
                npe.done(tr, "c_tr")

    gate_loaded = [sem("gate_m_loaded"), sem("gate_d_loaded")]
    gated = [sem("gated_m"), sem("gated_d")]
    samples_hi, samples_lo = sem("samples_hi"), sem("samples_lo")
    merged_sum = sem("merged_sum")
    merged_hi = sem("merged_hi")
    merged_lo = sem("merged_lo")
    y_evac = [sem("y_evac_act"), sem("y_evac_dve")]
    OUT0, TILE5 = PROJ0 + 4, TILE4 + 2 * KT
    OUT_CHUNKS = D_MODEL // NC_
    FFN0, TILE6 = OUT0 + OUT_CHUNKS, TILE5 + KT
    WP = CW // 4

    def banks(b):
        return ps[:, b:b + NTB, 0:TB]

    def by_bank(ap):
        return ap.rearrange("p (b t) -> p b t", b=NTB)

    def up_chunk(i, half):
        return w_cols(I["w_up"][0], half * D_FF + NC_ * i)

    y_t = nc.alloc_sbuf_tensor_at("y_t", [P, KT, T], F32, offset=acts_lo_at)
    with ExitStack() as scope:
        cur[0] = scope
        mg_hi = sb("mg_hi", [P, KT, T], F32R)
        mg_lo = sb("mg_lo", [P, KT, T], F32R)
        gate = [sb("gate_m", [P, T]), sb("gate_d", [P, T])]

        with nc.Block() as block:
            @block.sync
            def _(sp):
                def gate_load(k):
                    if k:
                        sp.wait_ge(merged_lo, k)
                    sp.dma_start(gate[0][:], ZT[Z_GM + k]).then_inc(gate_loaded[0], 16)
                    if k:
                        sp.wait_ge(merged_sum, k)
                    sp.dma_start(gate[1][:], ZT[Z_GD + k]).then_inc(gate_loaded[1], 16)

                gate_load(0)
                for g in range(2):
                    src = (I["w_proj_m"][0], I["w_proj_d"][0])[g].rearrange("(k p) n -> p k n", p=P)
                    load_chunk(sp, g, src[:, :, WP:2 * WP], W_MIX // P, PROJ0 + g + 1)
                for k in range(1, KT):
                    gate_load(k)
                    if k == 4:
                        load_chunk(sp, 0, w_cols(I["w_out"][0], 0), KT, OUT0 - 1)
                    if k == 5:
                        load_chunk(sp, 1, w_cols(I["w_out"][0], NC_), KT, OUT0)
                for c in range(2, OUT_CHUNKS):
                    load_chunk(sp, c % 2, w_cols(I["w_out"][0], c * NC_), KT, OUT0 + c - 1)
                for half in range(2):
                    load_chunk(sp, half, up_chunk(0, half), KT, FFN0 - 1 + half)

            @block.scalar
            def _(act):
                act.activation(acts_hi[:, :, SEQ:T], branch_s[:], ACT.Copy).then_inc(samples_hi, 1)
                split_hi(act, 1, loads_of(PROJ0 + 1), TILE4)
                for k in range(KT):
                    if k in (3, 7):
                        n = PROJ0 + 2 if k == 3 else OUT0
                        split_hi(act, 0, loads_of(n), TILE4 + 2 * k + 1)
                        split_hi(act, 1, loads_of(n + 1), TILE4 + 2 * k + 2)
                    act.wait_ge(merged_sum, k + 1)
                    act.activation(mg_hi[:, k, :], gate[0][:], ACT.Copy).then_inc(merged_hi, 1)
                for c in range(OUT_CHUNKS):
                    if c:
                        split_hi(act, (c + 1) % 2, loads_of(OUT0 + c + 1), TILE5 + 2 * c)
                    act.wait_ge(tile_done, TILE5 + 2 * c + 1)
                    act.activation(by_bank(y_t[:, 2 * c, :]), banks(0), ACT.Copy).then_inc(y_evac[0], 1)

            @block.vector
            def _(dve):
                dve.wait_ge(samples_hi, 1)
                dve.tensor_tensor(acts_lo[:, :, SEQ:T], branch_s[:], acts_hi[:, :, SEQ:T].bitcast(F32), ALU.subtract)\
                    .then_inc(samples_lo, 1)
                split_lo(dve, 1, PROJ0 + 2)
                for k in range(KT):
                    for g in range(2):
                        dve.wait_ge(gate_loaded[g], 16 * (k + 1))
                        dve.wait_ge(tile_done, TILE4 + 2 * k + g + 1)
                        dve.tensor_tensor(by_bank(gate[g][:]), by_bank(gate[g][:]), banks(3 * g), ALU.mult)\
                            .then_inc(gated[g], 1)
                        if g == 0 and k in (3, 7):
                            split_lo(dve, 0, PROJ0 + (3 if k == 3 else 5))
                    dve.wait_ge(gated[0], k + 1)
                    dve.wait_ge(gated[1], k + 1)
                    dve.tensor_tensor(gate[0][:], gate[0][:], gate[1][:], ALU.add).then_inc(merged_sum, 1)
                    if k in (3, 7):
                        split_lo(dve, 1, PROJ0 + (4 if k == 3 else 6))
                    dve.wait_ge(merged_hi, k + 1)
                    dve.tensor_tensor(mg_lo[:, k, :], gate[0][:], mg_hi[:, k, :].bitcast(F32), ALU.subtract)\
                        .then_inc(merged_lo, 1)
                for c in range(OUT_CHUNKS):
                    if c:
                        split_lo(dve, (c + 1) % 2, OUT0 + c + 2)
                    dve.wait_ge(tile_done, TILE5 + 2 * c + 2)
                    dve.tensor_copy(by_bank(y_t[:, 2 * c + 1, :]), banks(3)).then_inc(y_evac[1], 1)

            @block.tensor
            def _(pe):
                pe.wait_ge(samples_lo, 1)
                for k in range(KT):
                    for g in range(2):
                        pe.wait_ge(w_lo_ready, PROJ0 + 2 * (k // 4) + g + 1)
                        if k:
                            pe.wait_ge(gated[g], k)
                        gemm_tile(pe, g, W_MIX // P, WP, k % 4, acts_hi[:, 4 * g:4 * g + 4, :],
                                  acts_lo[:, 4 * g:4 * g + 4, :], 3 * g)
                for c in range(OUT_CHUNKS):
                    pe.wait_ge(w_lo_ready, OUT0 + c + 1)
                    for j in range(2):
                        if c:
                            pe.wait_ge(y_evac[j], c)
                        else:
                            pe.wait_ge(gated[j], KT)
                        gemm_tile(pe, c % 2, KT, NC_, j, mg_hi, mg_lo, 3 * j, merged_lo if c == 0 and j == 0 else None)

    def post_norm(i, y_t, x_src, dst, last_vals=None):
        nm = ("mix", "ffn")[i]
        gain_loaded = sem(f"gain_loaded_{nm}")
        xr_loaded = [sem(f"xr_loaded_{nm}{s}") for s in range(2)]
        yr_tp = sem(f"yr_tp_{nm}")
        yr_ss = sem(f"yr_ss_{nm}")
        yr_v = sem(f"yr_v_{nm}")
        yr_rstd = sem(f"yr_rstd_{nm}")
        yr_g = sem(f"yr_g_{nm}")
        yr_x = sem(f"yr_x_{nm}")
        yr_stored = [sem(f"yr_stored_{nm}{s}") for s in range(2)]
        if i == 0:
            h_ss, h_v, h_rstd = sem("h_ss"), sem("h_v"), sem("h_rstd")
            h_s, h_tp, h_m = sem("h_scaled"), sem("h_tp"), sem("h_mul")
            h_aff, h_hi, h_lo = sem("h_shifted"), sem("h_hi"), sem("h_lo")
        else:
            lv_tp, lv_rows = sem("lv_tp"), sem("lv_rows")
        with ExitStack() as scope:
            cur[0] = scope
            gain = sb(f"gain_{nm}", [P, 2, D_MODEL])
            xr = sb(f"xr_{nm}", [P, 2, D_MODEL])
            YS = 4
            yr = sb(f"yr_{nm}", [P, YS, D_MODEL])
            sqr = sb(f"sqr_{nm}", [P, D_MODEL], mybir.dt.bfloat16)
            stats = sb(f"stats_{nm}", [P, NTT, 6])
            if i == 0:
                hs = sb("hs", [P, 2, D_MODEL])
                h_a = sb("h_a", [P, 2, KT, P])
            else:
                lv = sb("last_rows", [18, D_FF])

            NB = 2 if i == 0 else 4

            def halves(b, r):
                return ps[0:r, b:b + 2, :]

            def rows2(ap, r):
                return ap[0:r].rearrange("p (b n) -> p b n", b=2)

            with nc.Block() as block:
                @block.sync
                def _(sp):
                    sp.dma_start(gain[:, 0, :], GATES[i, TS:TS + 1, :].broadcast_to((P, D_MODEL))).then_inc(gain_loaded, 16)
                    sp.dma_start(gain[0:TS, 1, :], GATES[i, 0:TS, :]).then_inc(gain_loaded, 16)
                    for t in range(NTT + 1):
                        if t < NTT:
                            if t >= 2:
                                sp.wait_ge(yr_x, t - 1)
                            sp.dma_start(xr[0:tile_rows(t), t % 2, :], x_src(t)).then_inc(xr_loaded[t % 2], 16)
                        if t >= 1:
                            u = t - 1
                            sp.wait_ge(yr_x, u + 1)
                            sp.dma_start(dst(u), yr[0:tile_rows(u), u % YS, :]).then_inc(yr_stored[u % 2], 16)
                    if i == 1:
                        sp.wait_ge(lv_rows, 2)
                        sp.dma_start(O["conv_prompt"][0, 0], lv[0:2, :]).then_inc(yr_stored[0], 16)
                        sp.dma_start(O["conv_sample"][0].rearrange("b w f -> (b w) f"), lv[2:18, :]).then_inc(yr_stored[0], 16)
                    for s in range(2):
                        sp.wait_ge(yr_stored[s], 16 * ((NTT + 1 - s) // 2 + (2 if i == 1 and s == 0 else 0)))

                @block.tensor
                def _(pe):
                    def y_rows(t):
                        r, b = tile_rows(t), 2 * (t % NB)
                        if t >= NB:
                            pe.wait_ge(yr_g, t - NB + 1)
                        if i == 1 and t == 2:
                            pe.wait_ge(lv_rows, 2)
                        for k in range(KT):
                            tr = pe.transpose(ps[0:r, b + k // 4, k % 4 * P:(k % 4 + 1) * P],
                                              y_t[:, k, t * P:t * P + r], ident[:])
                        tr.then_inc(yr_tp, 1)

                    def h_cols(t):
                        r, b = tile_rows(t), 4 + 2 * (t % 2)
                        pe.wait_ge(h_s, t + 1)
                        if t >= 2:
                            pe.wait_ge(h_m, t - 1)
                        for k in range(KT):
                            tr = pe.transpose(ps[:, b + k // 4, k % 4 * P:k % 4 * P + r],
                                              hs[0:r, t % 2, k * P:(k + 1) * P], ident[0:r, 0:r])
                        tr.then_inc(h_tp, 1)

                    if i == 1:
                        for g in range(2):
                            if g:
                                pe.wait_ge(lv_rows, 1)
                            for f in range(16 * g, min(16 * g + 16, FT)):
                                tr = pe.transpose(ps[0:18, 4 + f % 16 // 4, f % 4 * P:(f % 4 + 1) * P], last_vals[:, f, :], ident[:])
                            tr.then_inc(lv_tp, 1)
                            if g == 0:
                                y_rows(0)
                                y_rows(1)
                    else:
                        y_rows(0)
                    for t in range(2 if i == 1 else 1, NTT + 4):
                        if t < NTT:
                            y_rows(t)
                        if i == 0 and t >= 4:
                            h_cols(t - 4)

                @block.scalar
                def _(act):
                    def y_square(t):
                        r = tile_rows(t)
                        act.wait_ge(yr_tp, t + 1)
                        if t:
                            act.wait_ge(yr_ss, t)
                        if i == 0 and t >= 3:
                            act.wait_ge(h_ss, t - 2)
                        act.activation(rows2(sqr[:], r), halves(2 * (t % NB), r), ACT.Square,
                                       accum_out=stats[0:r, t, 0:1]).then_inc(yr_ss, 1)

                    def h_square(t):
                        r = tile_rows(t)
                        act.wait_ge(yr_x, t + 1)
                        act.wait_ge(yr_ss, min(t + 3, NTT))
                        if t + 2 >= NTT:
                            act.wait_ge(h_ss, t)
                        act.activation(sqr[0:r], yr[0:r, t % YS, :], ACT.Square, accum_out=stats[0:r, t, 3:4]).then_inc(h_ss, 1)

                    def h_scale(t):
                        r = tile_rows(t)
                        act.wait_ge(h_rstd, t + 1)
                        if t >= 2:
                            act.wait_ge(h_tp, t - 1)
                        act.activation(hs[0:r, t % 2, :], yr[0:r, t % YS, :], ACT.Copy, scale=stats[0:r, t, 5:6]).then_inc(h_s, 1)

                    def h_up(t):
                        r = tile_rows(t)
                        act.wait_ge(h_aff, t + 1)
                        act.activation(acts_hi[:, :, t * P:t * P + r], h_a[:, t % 2, :, 0:r], ACT.Copy).then_inc(h_hi, 1)

                    def last_rows():
                        for g, (f0, f1) in enumerate(((0, 16), (16, FT))):
                            act.wait_ge(lv_tp, g + 1)
                            for b in range(0, f1 - f0, 4):
                                m = min(4, f1 - f0 - b)
                                cp = act.activation(lv[:, (f0 + b) * P:(f0 + b + m) * P], ps[0:18, 4 + b // 4, 0:m * P], ACT.Copy)
                            cp.then_inc(lv_rows, 1)

                    for t in range(NTT + 5 if i == 0 else NTT):
                        if i == 1 and t == 2:
                            last_rows()
                        if t < NTT:
                            y_square(t)
                        if i == 0 and 0 <= t - 2 < NTT:
                            h_square(t - 2)
                        if i == 0 and 0 <= t - 3 < NTT:
                            h_scale(t - 3)
                        if i == 0 and 0 <= t - 5 < NTT:
                            h_up(t - 5)

                @block.vector
                def _(dve):
                    dve.wait_ge(gain_loaded, 32)

                    def y_stat(t):
                        r = tile_rows(t)
                        dve.wait_ge(yr_ss, t + 1)
                        dve.tensor_scalar(stats[0:r, t, 1:2], stats[0:r, t, 0:1], 1.0 / D_MODEL, EPS, ALU.mult, ALU.add).then_inc(yr_v, 1)

                    def y_out(t):
                        r, s = tile_rows(t), t % 2
                        yt = yr[:, t % YS, :]
                        dve.wait_ge(yr_rstd, t + 1)
                        if t >= YS:
                            dve.wait_ge(yr_stored[s], 16 * (t // 2))
                            if i == 0:
                                dve.wait_ge(h_s, t - YS + 1)
                        dve.scalar_tensor_tensor(out=rows2(yt, r), in0=halves(2 * (t % NB), r), scalar=stats[0:r, t, 2:3],
                                                 in1=rows2(gain[:, t // NCH, :], r), op0=ALU.mult, op1=ALU.mult).then_inc(yr_g, 1)
                        dve.wait_ge(xr_loaded[s], 16 * (t // 2 + 1))
                        dve.wait_ge(yr_g, t + 1)
                        dve.tensor_tensor(yt[0:r], yt[0:r], xr[0:r, s, :], ALU.add).then_inc(yr_x, 1)

                    def h_stat(t):
                        r = tile_rows(t)
                        dve.wait_ge(h_ss, t + 1)
                        dve.tensor_scalar(stats[0:r, t, 4:5], stats[0:r, t, 3:4], 1.0 / D_MODEL, EPS, ALU.mult, ALU.add).then_inc(h_v, 1)

                    def h_mul(t):
                        r = tile_rows(t)
                        dve.wait_ge(h_tp, t + 1)
                        if t >= 2:
                            dve.wait_ge(h_lo, t - 1)
                        dve.tensor_tensor(kt2(h_a[:, t % 2, :, 0:r]), transposed_banks(4 + 2 * (t % 2), r),
                                          kt2(of_tokens(2, t)), ALU.mult).then_inc(h_m, 1)

                    def h_low(t):
                        r = tile_rows(t)
                        dve.wait_ge(h_hi, t + 1)
                        dve.tensor_tensor(acts_lo[:, :, t * P:t * P + r], h_a[:, t % 2, :, 0:r],
                                          acts_hi[:, :, t * P:t * P + r].bitcast(F32), ALU.subtract).then_inc(h_lo, 1)

                    for t in range(NTT + 5 if i == 0 else NTT + 1):
                        if t < NTT:
                            y_stat(t)
                        if i == 0 and 0 <= t - 2 < NTT:
                            h_stat(t - 2)
                        if 0 <= t - 1 < NTT:
                            y_out(t - 1)
                        if i == 0 and 0 <= t - 4 < NTT:
                            h_mul(t - 4)
                        if i == 0 and 0 <= t - 5 < NTT:
                            h_low(t - 5)

                @block.gpsimd
                def _(pool):
                    def h_shift(t):
                        r = tile_rows(t)
                        pool.wait_ge(h_m, t + 1)
                        pool.tensor_tensor(h_a[:, t % 2, :, 0:r], h_a[:, t % 2, :, 0:r], of_tokens(3, t), ALU.add).then_inc(h_aff, 1)

                    for t in range(NTT + 4 if i == 0 else NTT):
                        if t < NTT:
                            r = tile_rows(t)
                            pool.wait_ge(yr_v, t + 1)
                            pool.tensor_tensor(stats[0:r, t, 2:3], stats[0:r, t, 1:2], minus_half[0:r, 0:1], ALU.pow).then_inc(yr_rstd, 1)
                        if i == 0 and 0 <= t - 2 < NTT:
                            r = tile_rows(t - 2)
                            pool.wait_ge(h_v, t - 1)
                            pool.tensor_tensor(stats[0:r, t - 2, 5:6], stats[0:r, t - 2, 4:5], minus_half[0:r, 0:1], ALU.pow).then_inc(h_rstd, 1)
                        if i == 0 and 0 <= t - 4 < NTT:
                            h_shift(t - 4)

    def x_rows(t):
        return I["x_prompt"][0, t * P:(t + 1) * P, :] if t < NCH else I["x_sample"].rearrange("b t d -> (b t) d")

    def x1_rows(t):
        return X1[t * P:t * P + tile_rows(t), :]

    def y_out_rows(t):
        return O["y_prompt"][0, t * P:(t + 1) * P, :] if t < NCH else O["y_sample"].rearrange("b t d -> (b t) d")

    post_norm(0, y_t, x_rows, x1_rows)

    NPAIR = FT // 2
    a_evac = sem("a_evac")
    a_state = sem("a_state")
    a_kept = sem("a_kept")
    f_conv = sem("f_conv")
    f_gelu = sem("f_gelu")
    f_mul = sem("f_mul")
    g_hi_s, g_lo_s = sem("g_hi"), sem("g_lo")
    f_add = sem("f_add")
    TAIL = CONV_W - 1
    AX = TAIL + SEQ + DEC_B * (TAIL + DEC_T)
    with ExitStack() as outer:
        cur[0] = outer
        f_t = sb("f_t", [P, KT, T])
        last_vals = sb("last_vals", [P, FT, TAIL * (1 + DEC_B)])
        with ExitStack() as scope:
            cur[0] = scope
            a_ext = [sb(f"a_ext{j}", [P, AX]) for j in range(2)]
            conv = [sb(f"conv{j}", [P, AX]) for j in range(2)]
            g_hi = sb("g_hi_t", [P, 2, T], F32R)
            g_lo = sb("g_lo_t", [P, 2, T], F32R)

            def seqs(ap):
                return ap[:, TAIL + SEQ:AX].rearrange("p (b w) -> p b w", b=DEC_B)

            EDGE = SEQ - 2 * TB

            def parts(buf, b):
                return [(buf[:, TAIL:TAIL + 2 * TB].rearrange("p (b t) -> p b t", b=2), ps[:, b:b + 2, 0:TB]),
                        (buf[:, TAIL + 2 * TB:TAIL + SEQ], ps[:, b + 2, 0:EDGE]),
                        (seqs(buf)[:, :, TAIL:], ps[:, b + 2, EDGE:TB].rearrange("p (b t) -> p b t", b=DEC_B))]

            def tiles_at(i):
                return TILE6 + 4 + 12 * (i - 1)

            with nc.Block() as block:
                @block.sync
                def _(sp):
                    def down(i):
                        return I["w_down"][0].rearrange("(k p) n -> p k n", p=P)[:, bass.ds(2 * i, 2), :]

                    with sp.Fori(0, 2 * (NPAIR // 2) - 1, 2) as m:
                        for q in range(2):
                            i = m + 1 + q
                            n = FFN0 + 3 * m + 3 * q + 2
                            load_chunk(sp, q % 2, up_chunk(i, 0), KT, n - 1)
                            load_chunk(sp, (q + 1) % 2, down(i - 1), 2, n)
                            load_chunk(sp, q % 2, up_chunk(i, 1), KT, n + 1)
                    load_chunk(sp, 0, down(NPAIR - 1), 2, FFN0 + 3 * NPAIR - 2)

                @block.gpsimd
                def _(pool):
                    for j in range(2):
                        pool.memset(a_ext[j][:, 0:TAIL], 0.0).then_inc(a_state, 1)
                    for k in range(KT):
                        pool.memset(f_t[:, k, :], 0.0).then_inc(f_add, 1)

                    def pair(i, first):
                        for j in range(2):
                            f = 2 * i + j
                            n = 2 * i + j
                            if not first:
                                pool.wait_ge(f_conv, 3 * (n - 1))
                            pool.tensor_copy(seqs(a_ext[j])[:, :, 0:TAIL],
                                             ff_t[:, bass.ds(f, 1), 0:16].rearrange("p f (b w) -> p (f b) w", b=DEC_B))\
                                .then_inc(a_state, 1)
                        for j in range(2):
                            n = 2 * i + j
                            pool.wait_ge(a_evac, 3 * n + 3)
                            keep = last_vals[:, bass.ds(2 * i + j, 1), :].rearrange("p f n -> p (f n)")
                            pool.tensor_copy(keep[:, 0:TAIL], a_ext[j][:, SEQ:SEQ + TAIL]).then_inc(a_kept, 1)
                            pool.tensor_copy(keep[:, TAIL:].rearrange("p (b w) -> p b w", b=DEC_B),
                                             seqs(a_ext[j])[:, :, DEC_T:DEC_T + TAIL]).then_inc(a_kept, 1)

                    pair(0, True)
                    with pool.Fori(0, 2 * (NPAIR // 2) - 1, 2) as m:
                        for q in range(2):
                            pair(m + 1 + q, False)

                def conv_weight(f, j):
                    return ff_t[:, bass.ds(f, 1), 16 + j:17 + j].rearrange("p f n -> p (f n)")

                @block.scalar
                def _(act):
                    def a_tile(i, j, tile, first):
                        act.wait_ge(tile_done, tile)
                        if not first:
                            act.wait_ge(f_conv, 3 * (2 * i + j) - 3)
                            act.wait_ge(a_kept, 2 * (2 * i + j) - 2)
                        for dst, src in parts(a_ext[j], 3 * j):
                            act.activation(dst, src, ACT.Copy).then_inc(a_evac, 1)

                    def gelu(i, j):
                        act.wait_ge(f_conv, 3 * (2 * i + j) + 3)
                        act.activation(conv[j][:, TAIL:AX], conv[j][:, TAIL:AX], ACT.Gelu_apprx_tanh).then_inc(f_gelu, 1)

                    def g_up(i, j, tiles):
                        act.wait_ge(f_mul, 3 * (2 * i + j) + 3)
                        if tiles is not None:
                            act.wait_ge(tile_done, tiles)
                        act.activation(g_hi[:, j, 0:SEQ], conv[j][:, TAIL:TAIL + SEQ], ACT.Copy).then_inc(g_hi_s, 1)
                        act.activation(g_hi[:, j, SEQ:T].rearrange("p (b t) -> p b t", b=DEC_B), seqs(conv[j])[:, :, TAIL:],
                                       ACT.Copy).then_inc(g_hi_s, 1)

                    a_tile(0, 0, TILE6 + 1, True)
                    split_hi(act, 1, loads_of(FFN0 + 1), TILE6)
                    gelu(0, 0)
                    a_tile(0, 1, TILE6 + 2, True)
                    split_hi(act, 0, loads_of(FFN0 + 2), TILE6 + 2)
                    gelu(0, 1)
                    g_up(0, 0, None)
                    g_up(0, 1, None)

                    def pair(i, q, loads):
                        t0 = tiles_at(i)
                        split_hi(act, (q + 1) % 2, loads[0], t0)
                        a_tile(i, 0, t0 + 1, False)
                        gelu(i, 0)
                        a_tile(i, 1, t0 + 2, False)
                        split_hi(act, q % 2, loads[1], t0 + 2)
                        gelu(i, 1)
                        split_hi(act, (q + 1) % 2, loads[2], t0 + 10)
                        g_up(i, 0, t0 + 10)
                        g_up(i, 1, None)

                    with act.Fori(0, 2 * (NPAIR // 2) - 1, 2) as m:
                        for q in range(2):
                            loads = [24 * m + 16 * ((FFN0 + 3 * q + d) // 2 + 1) for d in (3, 4, 5)]
                            pair(m + 1 + q, q, loads)

                @block.vector
                def _(dve):
                    def conv_op(i, j, w, first=False):
                        n = 2 * i + j
                        if w == 0:
                            dve.wait_ge(a_evac, 3 * n + 3)
                            dve.wait_ge(a_state, n + 3)
                            if not first:
                                dve.wait_ge(g_hi_s, 4 * i - 2 + 2 * j)
                                dve.wait_ge(g_lo_s, 4 * i - 2 + 2 * j)
                        out = conv[j][:, TAIL:AX]
                        src = a_ext[j][:, w:AX - TAIL + w]
                        f = 2 * i + j
                        if w == 0:
                            ins_ = dve.tensor_scalar(out, src, conv_weight(f, 0), conv_weight(f, CONV_W), ALU.mult, ALU.add)
                        else:
                            dve.wait_ge(f_conv, 3 * n + w)
                            ins_ = dve.scalar_tensor_tensor(out=out, in0=src, scalar=conv_weight(f, w), in1=out,
                                                            op0=ALU.mult, op1=ALU.add)
                        ins_.then_inc(f_conv, 1)

                    def mul_b(i, j, tile):
                        dve.wait_ge(tile_done, tile)
                        dve.wait_ge(f_gelu, 2 * i + j + 1)
                        for dst, src in parts(conv[j], 3 * j):
                            dve.tensor_tensor(dst, dst, src, ALU.mult).then_inc(f_mul, 1)

                    def g_low(i, j):
                        n = 2 * i + j
                        dve.wait_ge(g_hi_s, 2 * n + 1)
                        dve.tensor_tensor(g_lo[:, j, 0:SEQ], conv[j][:, TAIL:TAIL + SEQ], g_hi[:, j, 0:SEQ].bitcast(F32),
                                          ALU.subtract).then_inc(g_lo_s, 1)
                        dve.wait_ge(g_hi_s, 2 * n + 2)
                        dve.tensor_tensor(g_lo[:, j, SEQ:T].rearrange("p (b t) -> p b t", b=DEC_B), seqs(conv[j])[:, :, TAIL:],
                                          g_hi[:, j, SEQ:T].rearrange("p (b t) -> p b t", b=DEC_B).bitcast(F32),
                                          ALU.subtract).then_inc(g_lo_s, 1)

                    def add_down(k, tile, adds):
                        dve.wait_ge(tile_done, tile)
                        dve.wait_ge(f_add, adds)
                        dve.tensor_tensor(by_bank(f_t[:, k, :]), by_bank(f_t[:, k, :]), banks(3 * (k % 2)), ALU.add)\
                            .then_inc(f_add, 1)

                    split_lo(dve, 1, FFN0 + 2)
                    for w in range(CONV_W):
                        conv_op(0, 0, w, True)
                    for w in range(CONV_W):
                        conv_op(0, 1, w, True)
                    split_lo(dve, 0, FFN0 + 3)
                    for j in range(2):
                        mul_b(0, j, TILE6 + 3 + j)
                    for j in range(2):
                        g_low(0, j)
                    dve.wait_ge(f_add, KT)

                    def pair(i, q, n):
                        t0 = tiles_at(i)
                        split_lo(dve, (q + 1) % 2, n)
                        for w in range(CONV_W):
                            conv_op(i, 0, w)
                        for k in range(KT):
                            add_down(k, t0 + 3 + k, KT * (i - 1) + k + 1)
                            if k < CONV_W:
                                conv_op(i, 1, k)
                            if k == CONV_W:
                                split_lo(dve, q % 2, n + 1)
                        split_lo(dve, (q + 1) % 2, n + 2)
                        for j in range(2):
                            mul_b(i, j, t0 + 11 + j)
                            g_low(i, j)

                    with dve.Fori(0, 2 * (NPAIR // 2) - 1, 2) as m:
                        for q in range(2):
                            pair(m + 1 + q, q, FFN0 + 3 * m + 3 * q + 4)
                    for k in range(KT):
                        add_down(k, tiles_at(NPAIR) + k + 1, KT * (NPAIR - 1) + k + 1)

                @block.tensor
                def _(pe):
                    def down(i, slot, left, counts):
                        pe.wait_ge(g_lo_s, 4 * i + 4)
                        for k in range(KT):
                            if k < 2:
                                pe.wait_ge(left, counts[k])
                            else:
                                pe.wait_ge(f_add, KT * (i + 1) + k - 1)
                            gemm_tile(pe, slot, 2, D_MODEL, k, g_hi, g_lo, 3 * (k % 2))

                    def pair(i, q, n):
                        pe.wait_ge(w_lo_ready, n + 1)
                        for j in range(2):
                            pe.wait_ge(f_mul, 6 * i - 3 + 3 * j)
                            gemm_tile(pe, q % 2, KT, NC_, j, acts_hi, acts_lo, 3 * j)
                        pe.wait_ge(w_lo_ready, n + 2)
                        down(i - 1, (q + 1) % 2, a_evac, (6 * i + 3, 6 * i + 6))
                        pe.wait_ge(w_lo_ready, n + 3)
                        for j in range(2):
                            pe.wait_ge(f_add, KT * (i + 1) - 1 + j)
                            gemm_tile(pe, q % 2, KT, NC_, j, acts_hi, acts_lo, 3 * j)

                    for h in range(2):
                        pe.wait_ge(w_lo_ready, FFN0 + h + 1)
                        for j in range(2):
                            if h:
                                pe.wait_ge(a_evac, 3 * j + 3)
                            gemm_tile(pe, h, KT, NC_, j, acts_hi, acts_lo, 3 * j)
                    with pe.Fori(0, 2 * (NPAIR // 2) - 1, 2) as m:
                        for q in range(2):
                            pair(m + 1 + q, q, FFN0 + 3 * m + 3 * q + 2)
                    pe.wait_ge(w_lo_ready, FFN0 + 3 * NPAIR)
                    down(NPAIR - 1, 0, f_mul, (6 * NPAIR - 3, 6 * NPAIR))

        post_norm(1, f_t, x1_rows, y_out_rows, last_vals)
    base.close()


_OUTS = [
    ("y_prompt", (1, SEQ, D_MODEL)), ("y_sample", (DEC_B, DEC_T, D_MODEL)),
    ("k_prompt", (1, 1, SEQ, H, 2 * DQK)), ("v_prompt", (1, 1, SEQ, H, DH)),
    ("C_prompt", (1, 1, H, DH, DH)), ("n_prompt", (1, 1, H, DH)), ("m_prompt", (1, 1, H)),
    ("conv_prompt", (1, 1, CONV_W - 1, D_FF)),
    ("k_sample", (1, DEC_B, DEC_T, H, 2 * DQK)), ("v_sample", (1, DEC_B, DEC_T, H, DH)),
    ("C_sample", (1, DEC_B, H, DH, DH)), ("n_sample", (1, DEC_B, H, DH)), ("m_sample", (1, DEC_B, H)),
    ("conv_sample", (1, DEC_B, CONV_W - 1, D_FF)),
]


def kernel(**inputs):
    import numpy as _np
    import concourse.bacc as _bacc
    from concourse import mybir as _mybir
    from concourse.bass_utils import run_bass_kernel_spmd as _run

    nc = _bacc.Bacc("TRN2", target_bir_lowering=False, num_devices=1)
    arrays, ins, outs = {}, {}, {}
    for name, a in inputs.items():
        a = _np.ascontiguousarray(a)
        arrays[f"in_{name}"] = a
        ins[name] = nc.dram_tensor(f"in_{name}", a.shape, _mybir.dt.from_np(a.dtype), kind="ExternalInput").ap()
    for name, shape in _OUTS:
        outs[name] = nc.dram_tensor(f"out_{name}", shape, F32, kind="ExternalOutput").ap()
    build(nc, ins, outs)
    r = _run(nc, [arrays], core_ids=[0])
    return tuple(r.results[0][f"out_{name}"] for name, _ in _OUTS)
```
